# Optimizing a Trainium2 kernel written in Bass

```python
import math
import jax, jax.numpy as jnp
from jax import lax
import numpy as np

D_MODEL = 1024
BATCH = 1
SEQ = 256
DEPTH = 2

D_MIX = D_MODEL
D_MLSTM = D_MIX // 2
D_S5 = D_MIX - D_MLSTM
MLSTM_HEADS = 4
MLSTM_HEAD_DIM = D_MLSTM // MLSTM_HEADS
MLSTM_CHUNK = 64
CONV_WIDTH = 4
S5_GROUP = 16
S5_GROUPS = D_S5 // S5_GROUP
S5_STATE = 64
D_FF_DENSE = 2816
N_EXPERTS = 8
TOP_K = 2
D_FF_EXPERT = 3584
N_DENSE = (DEPTH + 1) // 2
N_MOE = DEPTH // 2
RMS_EPS = 1e-6
PROJ_SPLITS = (D_MLSTM, 2 * D_MLSTM, 3 * D_MLSTM, 4 * D_MLSTM,
               4 * D_MLSTM + MLSTM_HEADS, 4 * D_MLSTM + 2 * MLSTM_HEADS)
PROJ_COLS = 4 * D_MLSTM + 2 * MLSTM_HEADS + D_S5

kernel_name = "hybrid_mlstm_s5_moe_trunk"

def rmsnorm(x, g):
    xf = x.astype(jnp.float32)
    y = xf * lax.rsqrt(jnp.mean(xf * xf, axis=-1, keepdims=True) + RMS_EPS)
    return (y * g.astype(jnp.float32)).astype(x.dtype)

def causal_dwconv(x, w):
    c = x.shape[-1]
    return lax.conv_general_dilated(
        x, w[:, None, :].astype(x.dtype), window_strides=(1,),
        padding=((w.shape[0] - 1, 0),),
        dimension_numbers=("NWC", "WIO", "NWC"), feature_group_count=c)

def _mlstm_chunk(carry, xs):
    c_state, n_state, m_state = carry
    q, k, v, lf, li = xs
    L = q.shape[2]
    b = jnp.cumsum(lf, axis=-1)
    causal = jnp.tril(jnp.ones((L, L), dtype=bool))
    log_d = jnp.where(causal, b[..., :, None] - b[..., None, :] + li[..., None, :], -jnp.inf)
    m_inter = b + m_state[..., None]
    m_t = jnp.maximum(m_inter, jnp.max(log_d, axis=-1))
    d = jnp.exp(log_d - m_t[..., None])
    inter = jnp.exp(m_inter - m_t)
    s = jnp.einsum('bhtd,bhsd->bhts', q, k) * d
    num = jnp.einsum('bhts,bhse->bhte', s, v) + inter[..., None] * jnp.einsum('bhtd,bhde->bhte', q, c_state)
    den = jnp.sum(s, axis=-1) + inter * jnp.einsum('bhtd,bhd->bht', q, n_state)
    h = num / jnp.maximum(jnp.abs(den), jnp.exp(-m_t))[..., None]
    b_end = b[..., -1]
    log_w = b_end[..., None] - b + li
    m_new = jnp.maximum(b_end + m_state, jnp.max(log_w, axis=-1))
    w = jnp.exp(log_w - m_new[..., None])
    decay = jnp.exp(b_end + m_state - m_new)
    c_new = decay[..., None, None] * c_state + jnp.einsum('bhs,bhsd,bhse->bhde', w, k, v)
    n_new = decay[..., None] * n_state + jnp.einsum('bhs,bhsd->bhd', w, k)
    return (c_new, n_new, m_new), h

def mlstm(q, k, v, li, lf):
    B, S, H, dh = q.shape
    nc = S // MLSTM_CHUNK
    to_chunks = lambda t: t.reshape(B, nc, MLSTM_CHUNK, H, dh).transpose(1, 0, 3, 2, 4)
    g_chunks = lambda t: t.reshape(B, nc, MLSTM_CHUNK, H).transpose(1, 0, 3, 2)
    init = (jnp.zeros((B, H, dh, dh), jnp.float32), jnp.zeros((B, H, dh), jnp.float32),
            jnp.zeros((B, H), jnp.float32))
    _, h = lax.scan(_mlstm_chunk, init,
                    (to_chunks(q), to_chunks(k), to_chunks(v), g_chunks(lf), g_chunks(li)))
    return h.transpose(1, 0, 3, 2, 4).reshape(B, S, H, dh)

def s5_ssm(u, a_re, a_im, log_dt, b_re, b_im, c_re, c_im, d_skip):
    S = u.shape[1]
    dt = jnp.exp(log_dt)[:, None]
    mag = jnp.exp(a_re * dt)
    ab_re = mag * jnp.cos(a_im * dt)
    ab_im = mag * jnp.sin(a_im * dt)
    lam2 = a_re * a_re + a_im * a_im
    z_re = ab_re - 1.0
    f_re = (z_re * a_re + ab_im * a_im) / lam2
    f_im = (ab_im * a_re - z_re * a_im) / lam2
    bb_re = f_re[..., None] * b_re - f_im[..., None] * b_im
    bb_im = f_re[..., None] * b_im + f_im[..., None] * b_re
    bu_re = jnp.einsum('gph,bsgh->bsgp', bb_re, u)
    bu_im = jnp.einsum('gph,bsgh->bsgp', bb_im, u)
    shape_a = (1, S) + ab_re.shape
    a_seq_re = jnp.broadcast_to(ab_re[None, None], shape_a)
    a_seq_im = jnp.broadcast_to(ab_im[None, None], shape_a)

    def combine(e1, e2):
        a1r, a1i, b1r, b1i = e1
        a2r, a2i, b2r, b2i = e2
        return (a2r * a1r - a2i * a1i, a2r * a1i + a2i * a1r,
                a2r * b1r - a2i * b1i + b2r, a2r * b1i + a2i * b1r + b2i)

    _, _, x_re, x_im = lax.associative_scan(combine, (a_seq_re, a_seq_im, bu_re, bu_im), axis=1)
    y = (jnp.einsum('ghp,bsgp->bsgh', c_re, x_re) - jnp.einsum('ghp,bsgp->bsgh', c_im, x_im)
         + d_skip * u)
    return y

def hybrid_mixer(h, w_in, conv_qk, b_igate, b_fgate, norm_mlstm, a_re, a_im, log_dt,
                 b_re, b_im, c_re, c_im, d_skip, w_glu, norm_s5, w_out):
    B, S, _ = h.shape
    f32 = jnp.float32
    proj = h @ w_in
    q_pre, k_pre, v, o_pre, i_pre, f_pre, u = jnp.split(proj, PROJ_SPLITS, axis=-1)
    qk = jax.nn.silu(causal_dwconv(jnp.concatenate([q_pre, k_pre], axis=-1), conv_qk)).astype(f32)
    hd = (B, S, MLSTM_HEADS, MLSTM_HEAD_DIM)
    q = qk[..., :D_MLSTM].reshape(hd)
    k = qk[..., D_MLSTM:].reshape(hd) * (MLSTM_HEAD_DIM ** -0.5)
    vv = v.astype(f32).reshape(hd)
    li = i_pre.astype(f32) + b_igate.astype(f32)
    lf = jax.nn.log_sigmoid(f_pre.astype(f32) + b_fgate.astype(f32))
    hm = mlstm(q, k, vv, li, lf)
    hm = hm * lax.rsqrt(jnp.mean(hm * hm, axis=-1, keepdims=True) + RMS_EPS)
    hm = hm.reshape(B, S, D_MLSTM) * norm_mlstm.astype(f32)
    hm = jax.nn.sigmoid(o_pre.astype(f32)) * hm
    ug = u.astype(f32).reshape(B, S, S5_GROUPS, S5_GROUP)
    ys = s5_ssm(ug, a_re.astype(f32), a_im.astype(f32), log_dt.astype(f32),
                b_re.astype(f32), b_im.astype(f32), c_re.astype(f32), c_im.astype(f32),
                d_skip.astype(f32).reshape(S5_GROUPS, S5_GROUP)).reshape(B, S, D_S5)
    g = jax.nn.gelu(ys)
    ys = g * jax.nn.sigmoid(g @ w_glu.astype(f32))
    ys = ys * lax.rsqrt(jnp.mean(ys * ys, axis=-1, keepdims=True) + RMS_EPS) * norm_s5.astype(f32)
    mixed = jnp.concatenate([hm, ys], axis=-1).astype(h.dtype)
    return mixed @ w_out

def swiglu(x, w_gate, w_up, w_down):
    return (jax.nn.silu(x @ w_gate) * (x @ w_up)) @ w_down

def moe_swiglu(x, w_router, b_router, w_gate, w_up, w_down):
    B, S, D = x.shape
    xt = x.reshape(B * S, D)
    logits = (xt @ w_router).astype(jnp.float32) + b_router.astype(jnp.float32)
    top_v, top_i = lax.top_k(logits, TOP_K)
    gates = jax.nn.softmax(top_v, axis=-1)
    combine = jnp.einsum('tk,tke->te', gates, jax.nn.one_hot(top_i, N_EXPERTS, dtype=jnp.float32))
    out = jnp.zeros_like(xt)
    for e in range(N_EXPERTS):
        out = out + combine[:, e:e + 1].astype(xt.dtype) * swiglu(xt, w_gate[e], w_up[e], w_down[e])
    return out.reshape(B, S, D)

def setup_inputs(seed: int = 0) -> dict:
    key = jax.random.key(seed)
    ks = jax.random.split(key, 32)
    f32 = jnp.float32
    nrm = lambda k, shape, scale: jax.random.normal(k, shape, f32) * scale
    n_idx = jnp.arange(S5_STATE, dtype=f32)
    return {
        "x": nrm(ks[0], (BATCH, SEQ, D_MODEL), 1.0),
        "norm_mix": 1.0 + nrm(ks[1], (DEPTH, D_MODEL), 0.02),
        "w_in": nrm(ks[2], (DEPTH, D_MODEL, PROJ_COLS), D_MODEL ** -0.5),
        "conv_qk": nrm(ks[3], (DEPTH, CONV_WIDTH, 2 * D_MLSTM), CONV_WIDTH ** -0.5),
        "b_igate": nrm(ks[4], (DEPTH, MLSTM_HEADS), 0.1),
        "b_fgate": jnp.linspace(3.0, 6.0, MLSTM_HEADS, dtype=f32)[None, :] + nrm(ks[5], (DEPTH, MLSTM_HEADS), 0.1),
        "norm_mlstm": 1.0 + nrm(ks[6], (DEPTH, D_MLSTM), 0.02),
        "s5_a_re": -0.5 + nrm(ks[7], (DEPTH, S5_GROUPS, S5_STATE), 1e-3),
        "s5_a_im": jnp.pi * n_idx + nrm(ks[8], (DEPTH, S5_GROUPS, S5_STATE), 1e-3),
        "s5_log_dt": jax.random.uniform(ks[9], (DEPTH, S5_GROUPS), f32, math.log(1e-3), math.log(1e-1)),
        "s5_b_re": nrm(ks[10], (DEPTH, S5_GROUPS, S5_STATE, S5_GROUP), (2 * S5_GROUP) ** -0.5),
        "s5_b_im": nrm(ks[11], (DEPTH, S5_GROUPS, S5_STATE, S5_GROUP), (2 * S5_GROUP) ** -0.5),
        "s5_c_re": nrm(ks[12], (DEPTH, S5_GROUPS, S5_GROUP, S5_STATE), (2 * S5_STATE) ** -0.5),
        "s5_c_im": nrm(ks[13], (DEPTH, S5_GROUPS, S5_GROUP, S5_STATE), (2 * S5_STATE) ** -0.5),
        "s5_d": nrm(ks[14], (DEPTH, D_S5), 1.0),
        "w_glu": nrm(ks[15], (DEPTH, D_S5, D_S5), D_S5 ** -0.5),
        "norm_s5": 1.0 + nrm(ks[16], (DEPTH, D_S5), 0.02),
        "w_out": nrm(ks[17], (DEPTH, D_MIX, D_MODEL), D_MIX ** -0.5),
        "norm_ffn": 1.0 + nrm(ks[18], (DEPTH, D_MODEL), 0.02),
        "ffn_w_gate": nrm(ks[19], (N_DENSE, D_MODEL, D_FF_DENSE), D_MODEL ** -0.5),
        "ffn_w_up": nrm(ks[20], (N_DENSE, D_MODEL, D_FF_DENSE), D_MODEL ** -0.5),
        "ffn_w_down": nrm(ks[21], (N_DENSE, D_FF_DENSE, D_MODEL), D_FF_DENSE ** -0.5),
        "moe_w_router": nrm(ks[22], (N_MOE, D_MODEL, N_EXPERTS), D_MODEL ** -0.5),
        "moe_b_router": nrm(ks[23], (N_MOE, N_EXPERTS), 0.01),
        "moe_w_gate": nrm(ks[24], (N_MOE, N_EXPERTS, D_MODEL, D_FF_EXPERT), D_MODEL ** -0.5),
        "moe_w_up": nrm(ks[25], (N_MOE, N_EXPERTS, D_MODEL, D_FF_EXPERT), D_MODEL ** -0.5),
        "moe_w_down": nrm(ks[26], (N_MOE, N_EXPERTS, D_FF_EXPERT, D_MODEL), D_FF_EXPERT ** -0.5),
        "norm_final": 1.0 + nrm(ks[27], (D_MODEL,), 0.02),
    }

def reference(x, norm_mix, w_in, conv_qk, b_igate, b_fgate, norm_mlstm, s5_a_re, s5_a_im,
              s5_log_dt, s5_b_re, s5_b_im, s5_c_re, s5_c_im, s5_d, w_glu, norm_s5, w_out,
              norm_ffn, ffn_w_gate, ffn_w_up, ffn_w_down, moe_w_router, moe_b_router,
              moe_w_gate, moe_w_up, moe_w_down, norm_final):
    for l in range(DEPTH):
        hn = rmsnorm(x, norm_mix[l])
        x = x + hybrid_mixer(hn, w_in[l], conv_qk[l], b_igate[l], b_fgate[l], norm_mlstm[l],
                             s5_a_re[l], s5_a_im[l], s5_log_dt[l], s5_b_re[l], s5_b_im[l],
                             s5_c_re[l], s5_c_im[l], s5_d[l], w_glu[l], norm_s5[l], w_out[l])
        hn = rmsnorm(x, norm_ffn[l])
        j = l // 2
        if l % 2 == 0:
            x = x + swiglu(hn, ffn_w_gate[j], ffn_w_up[j], ffn_w_down[j])
        else:
            x = x + moe_swiglu(hn, moe_w_router[j], moe_b_router[j], moe_w_gate[j],
                               moe_w_up[j], moe_w_down[j])
    return rmsnorm(x, norm_final)


_drawn_inputs = setup_inputs


def setup_inputs(seed=0):
    import zlib

    import numpy as np

    out = dict(_drawn_inputs(seed))
    spreads = {}
    factors = {'b_igate': 64.0,
     'norm_mlstm': 11.494,
     's5_a_re': 64.0,
     'norm_s5': 2.74,
     'moe_b_router': 18.227,
     'norm_final': 9.656,
     's5_b_re': 3.091,
     's5_b_im': 2.904,
     's5_c_re': 2.935,
     's5_c_im': 2.73,
     'norm_ffn': 4.871}
    for name, (base, spread) in spreads.items():
        noise = np.random.default_rng([zlib.crc32(name.encode()), seed]).standard_normal(out[name].shape)
        drawn = base * np.exp(spread * noise) if base else spread * noise
        out[name] = __import__('jax').numpy.asarray(drawn.astype(out[name].dtype))
    for name, factor in factors.items():
        out[name] = (out[name] * factor).astype(out[name].dtype)
    return out
```

```python
from contextlib import ExitStack
import math

import numpy as np
import concourse.bass as bass
from concourse import mybir

F32 = mybir.dt.float32
I32 = mybir.dt.int32
ALU = mybir.AluOpType
ACT = mybir.ActivationFunctionType
AX = mybir.AxisListType.X

P = 128
SEQ, DM = 256, 1024
NT = SEQ // P
KT = DM // P
DEPTH = 2
DH = 128
NH = 4
DML = NH * DH
DS5 = DM - DML
CW = 4
GP = 16
NS = 64
NG = DS5 // GP
CT = DS5 // P
PAIRS = NG // 2
PPC = PAIRS // CT
FD = 2816
FT = FD // P
NE = 8
FE = 3584
GW = 512
NJ = FE // GW
EPS = 1e-6
IF0 = 4 * DML
U0 = IF0 + 2 * NH
QK = 2 * DML // P

CHUNK = 8 * 512
RING = 5
MRING = 7
PER_ITEM = 3 * NJ
TAIL = NE - 1

TWO_PI = 2.0 * math.pi
PI_A = 6.28125
PI_B = float(np.float32(np.round((TWO_PI - PI_A) * 2.0**21) / 2.0**21))
PI_C = TWO_PI - PI_A - PI_B
ROUND_INT = 1.5 * 2.0**23
ROUND_12 = 1.5 * 2.0**11
SIN_SCALE = 6.283185
NEG = -1.0e30
PICK = 3.0e38
GELU_A = 0.044715
GELU_B = math.sqrt(2.0 / math.pi)

VEC_ROWS = [("norm_mix", KT), ("conv", CW * QK), ("norm_mlstm", NH), ("s5_d", CT), ("norm_s5", CT), ("norm_ffn", KT)]
VEC_PER = sum(n for _, n in VEC_ROWS)


def vec_col(l, name, i=0):
    at = l * VEC_PER
    for n, rows in VEC_ROWS:
        if n == name:
            return at + i
        at += rows
    raise KeyError(name)


def mixer_steps(l):
    proj = {0: [("if", l)], 2: [("qk", l, 0)], 4: [("qk", l, 1)], 6: [("qk", l, 2)], 8: [("qk", l, 3)],
            10: [("v", l, 0)], 12: [("v", l, 1)], 14: [("o", l, 0)], 15: [("o", l, 1)]}
    return proj


def products():
    out = [(("vec",), "V", 0), (("s5p",), "V", 1)]
    turn = {"lo": 0, "hi": 0}

    def lo(name, who):
        out.append((name, who, turn["lo"] % 4))
        turn["lo"] += 1

    def hi(name, who):
        out.append((name, who, 4 + turn["hi"] % 4))
        turn["hi"] += 1

    def norm(l, what):
        for j in range(4):
            lo(("xT", l, what, j), "VA"[j % 2])

    def prep(l):
        for n in ("b_re", "b_im"):
            hi((n, l), "A")
        for n in ("c_re", "c_im"):
            hi((n, l), "V")

    for l in range(DEPTH):
        if l == 0:
            prep(0)
        norm(l, 0)
        for i in range(2):
            hi(("u", l, i), "A")
        for i in range(4):
            lo(("bu", l, i), "V")
        y = 0
        for i in range(PAIRS):
            for n in mixer_steps(l).get(i, []):
                out.append((n, "V" if n[0] == "if" else "A", 4 + turn["hi"] % 2))
                turn["hi"] += 1
            if i + 4 < PAIRS:
                lo(("bu", l, i + 4), "V")
            if i % PPC == PPC - 1:
                out.append((("y", l, i // PPC), "V", 6 + y % 2))
                y += 1
        hi(("tr", l), "A")
        for i in range(2):
            lo(("z", l, i), "A")
        for h in range(NH):
            hi(("mu", l, h), "V")
            hi(("sc", l, h), "V")
            if h:
                lo(("num", l, h - 1), "V")
        lo(("num", l, NH - 1), "V")
        hi(("ss", l), "V")
        for t in range(NT):
            for c in range(2):
                hi(("os", l, t, c), "V")
        for i in range(2):
            lo(("hmT", l, i), "A")
        for t in range(NT):
            for c in range(2):
                lo(("oh", l, t, c), "V")
        if l == 0:
            prep(1)
        norm(l, 1)
        if l == 0:
            for f in range(FT):
                lo(("gu", f), "V")
            for t in range(NT):
                for c in range(2):
                    out.append((("ffn", t, c), "V", 4 + 2 * t + c))
        else:
            out.append((("router",), "V", 4))
            out.append((("pos",), "V", 5))
    return out


class Banks:

    def __init__(self):
        self.at, self.before = {}, {}
        last, count = {}, {"V": 0, "A": 0}
        n = 0
        for name, who, bank in products():
            count[who] += 1
            n += name[0] != "y"
            self.at[name] = (n, who, count[who], bank)
            self.before[name] = last.get(bank)
            last[bank] = name
        self.last = last


def chunk_plan():
    plan = []
    for l in range(DEPTH):
        plan += [("u", l), ("q", l), ("k", l), ("v", l), ("o", l), ("glu", l), ("out", l, 0), ("out", l, 1)]
        if l == 0:
            for j in range((FD + GW - 1) // GW):
                plan += [("fg", j), ("fu", j), ("fd", j)]
    return plan


def trunk_kernel(nc, x, norm_mix, w_in, conv_qk, b_igate, b_fgate, norm_mlstm, s5_a_re, s5_a_im, s5_log_dt,
                 s5_b_re, s5_b_im, s5_c_re, s5_c_im, s5_d, w_glu, norm_s5, w_out, norm_ffn, ffn_w_gate,
                 ffn_w_up, ffn_w_down, moe_w_router, moe_b_router, moe_w_gate, moe_w_up, moe_w_down,
                 norm_final, out):
    banks = Banks()
    plan = chunk_plan()
    chunk_no = {name: n for n, name in enumerate(plan)}

    ctx = ExitStack()
    with ctx:
        def sb(name, shape, dt=F32):
            return ctx.enter_context(nc.sbuf_tensor(name, shape, dt))

        def sem(name):
            return ctx.enter_context(nc.semaphore(name))

        ring = sb("ring", [P, RING, CHUNK])
        arena = sb("arena", [P, 20000])
        x_res = sb("x_res", [P, NT, DM])
        hn = sb("hn", [P, NT, DM])
        hnT = sb("hnT", [P, KT, SEQ])
        ident = sb("ident", [P, P])
        ones = sb("ones", [P, P])
        lower = sb("lower", [P, P])
        cmask = sb("cmask", [P, SEQ])
        times = sb("times", [P, SEQ])
        head_pick = sb("head_pick", [NH, NH, P])
        neg_half = sb("neg_half", [P, NT * NH])
        half_pi = sb("half_pi", [P, 1])
        vec = sb("vec", [P, DEPTH * VEC_PER])
        s5p = sb("s5p", [P, 3, DEPTH, PAIRS])
        bT = sb("bT", [P, 2, CT, P])
        cT = sb("cT", [P, 3, CT, P])
        fac = sb("fac", [P, 24, PAIRS])
        w_if = sb("w_if", [P, KT, 2 * NH])
        w_rt = sb("w_rt", [P, KT, NE])
        b_rt = sb("b_rt", [P, NE])
        b_if = sb("b_if", [NH, DEPTH, 2])
        small = sb("small", [P, 64])

        at = [0]

        def carve(shape, base=None):
            n = int(np.prod(shape))
            a = at[0] if base is None else base
            if base is None:
                at[0] += n
            assert a + n <= 20000, (a, n)
            v = arena[:, a:a + n]
            letters = "abcd"[:len(shape)]
            if len(shape) > 1:
                v = v.rearrange(f"p ({' '.join(letters)}) -> p {' '.join(letters)}",
                                **{k: s for k, s in zip(letters[1:], shape[1:])})
            return v

        qk_pre = carve([QK, SEQ + CW - 1])
        qk = carve([QK, SEQ])
        v_aug = carve([NT, NH, DH + 1])
        o_gate = carve([NT, DML])
        uT = carve([CT, SEQ])
        gT = carve([CT, SEQ])
        ysT = carve([CT, SEQ])
        hm = carve([NT, NH, DH])
        trig_at = at[0]
        trig = carve([2, 2, 3, SEQ])
        turn = carve([3, 2, SEQ])
        phase = carve([2, 2, SEQ])
        rot = carve([2, 2, SEQ])
        drive = carve([2, SEQ])
        state = carve([2, SEQ])
        back = carve([2, 2, 2, SEQ])
        mix_end = at[0]
        mixT = hn[:, :, :].rearrange("p t d -> p (t d)").rearrange("p (k t) -> p k t", t=SEQ)
        sbase = mix_end - 2 * 2 * 2 * SEQ
        dec = carve([2, SEQ + P], sbase)
        scr = carve([2, SEQ + P], sbase + 2 * (SEQ + P))
        gates = carve([10, SEQ], trig_at)
        pbase = mix_end - 8 * SEQ - 2 * SEQ - 2 * SEQ - 4 * SEQ
        b_raw = sb("b_raw", [P, 2, PAIRS, GP])
        c_raw = sb("c_raw", [P, 2, CT, NS])
        b_blk = carve([2, PAIRS, 2, GP], pbase)
        b_tmp = carve([4, PAIRS, GP], pbase + 4 * PAIRS * GP)
        c_dup = carve([2, CT, 2, NS], pbase + 8 * PAIRS * GP)
        vec_rows = carve([P], 0)
        s5_rows = carve([P], P)
        dt_rows = carve([2], 2 * P)
        assert pbase + 8 * PAIRS * GP + 4 * CT * NS <= mix_end
        fbase = QK * (SEQ + CW - 1)
        f_silu = carve([2, SEQ], fbase)
        f_hid = carve([3, SEQ], fbase + 2 * SEQ)
        sq = hn[:, :, :]
        m_ring = [ring[:, s, :] for s in range(RING)] + [carve([CHUNK], s * CHUNK) for s in range(MRING - RING)]
        ebase = (MRING - RING) * CHUNK
        xe = carve([KT, P], ebase)
        e_silu = carve([2, GW], ebase + 1024)
        e_hid = carve([3, GW], ebase + 2048)
        e_hidT = carve([GW // P, P], ebase + 3584)
        ye = carve([DM], ebase + 4096)
        pick = carve([NT, P], ebase + 5120)
        pickg = carve([NT, P], ebase + 5376)
        pickT = carve([NT, P], ebase + 5632)
        rt = carve([24, NT, NE], ebase + 5888)
        items = 12
        posI = carve([NT, items], ebase + 6272)
        gateI = carve([NT, items], ebase + 6296)
        over = carve([8, NE], ebase + 6320)
        desc = carve([NE], ebase + 6456)
        gfin = carve([DM], ebase + 6464)
        assert ebase + 6464 + 1024 <= 20000
        n_list = sb("n_list", [P, 4], I32)

        ps = [ctx.enter_context(nc.psum_tensor(f"ps{i}", [P, 512], F32)) for i in range(8)]

        s_x = sem("s_x")
        s_par = sem("s_par")
        s_bc = sem("s_bc")
        s_wif = sem("s_wif")
        s_rt_in = sem("s_rt_in")
        s_gfin = sem("s_gfin")
        ring_full = [sem(f"ring_full{i}") for i in range(MRING)]
        ffn_down = sem("ffn_down")
        e_down = sem("e_down")
        product_ready = sem("product_ready")
        drained = {"V": sem("drained_v"), "A": sem("drained_a")}
        consts = sem("consts")
        dve_chain = sem("dve_chain")
        act_chain = sem("act_chain")
        pool_chain = sem("pool_chain")
        ms_ready = sem("ms_ready")
        rs_ready = sem("rs_ready")
        hn_ready = sem("hn_ready")
        dt_wide = sem("dt_wide")
        prep_in = sem("prep_in")
        fac_act = sem("fac_act")
        blk_ready = sem("blk_ready")
        fac_ready = sem("fac_ready")
        phase_ready = sem("phase_ready")
        trig_ready = sem("trig_ready")
        tile_done = sem("tile_done")
        back_used = sem("back_used")
        conv_ready = sem("conv_ready")
        qk_ready = sem("qk_ready")
        g_in = sem("g_in")
        g_out = sem("g_out")
        gate_rows = sem("gate_rows")
        y_in = sem("y_in")
        y_tanh = sem("y_tanh")
        y_ready = sem("y_ready")
        glu_ready = sem("glu_ready")
        dec_ready = sem("dec_ready")
        score_ready = sem("score_ready")
        hm_ready = sem("hm_ready")
        mixed_s5 = sem("mixed_s5")
        ffn_silu = sem("ffn_silu")
        route_in = sem("route_in")
        route_exp = sem("route_exp")
        route_mask = sem("route_mask")
        items_ready = sem("items_ready")
        e_gate = sem("e_gate")
        e_up = sem("e_up")
        e_tr = sem("e_tr")
        e_sc = sem("e_sc")
        e_gather = sem("e_gather")
        e_pt = sem("e_pt")
        a_silu = sem("a_silu")
        a_hT = sem("a_hT")
        a_ye = sem("a_ye")
        a_pt = sem("a_pt")
        v_hid = sem("v_hid")
        v_xe = sem("v_xe")
        v_add = sem("v_add")
        v_pick = sem("v_pick")
        fin_ready = sem("fin_ready")
        s_out = sem("s_out")

        def bank(name):
            return ps[banks.at[name][3]]

        def arrived(eng, name):
            if name[0] == "y":
                eng.wait_ge(back_used, PAIRS * name[1] + PPC * (name[2] + 1))
            else:
                eng.wait_ge(product_ready, banks.at[name][0])

        def wait_drained(eng, name):
            _, who, n, _ = banks.at[name]
            eng.wait_ge(drained[who], n)

        def open_bank(eng, name):
            if banks.before[name]:
                wait_drained(eng, banks.before[name])

        def chunk(name):
            return ring[:, chunk_no[name] % RING, :]

        def chunk_wait(eng, name):
            n = chunk_no[name]
            eng.wait_ge(ring_full[n % RING], 16 * (n // RING + 1))

        def wait_unused(eng, c):
            kind, i = c[0], c[1]
            if kind == "fd" and i < FD // GW:
                eng.wait_ge(ffn_down, i + 1)
                return
            last = {"u": ("u", i, 1), "q": ("qk", i, 1), "k": ("qk", i, 3), "v": ("v", i, 1), "o": ("o", i, 1),
                    "glu": ("z", i, 1), "out": ("oh", i, NT - 1, c[-1]), "fd": ("ffn", NT - 1, 1),
                    "fg": ("gu", min(4 * i + 3, FT - 1)), "fu": ("gu", min(4 * i + 3, FT - 1))}[kind]
            arrived(eng, last)

        uses = [sum(1 for n in range(len(plan)) if n % RING == s) for s in range(RING)] + [0] * (MRING - RING)

        def v3(ap, k):
            return ap.rearrange("p (k n) -> p k n", k=k)

        block = ctx.enter_context(nc.Block())

        @block.sync
        def _(sp):
            sp.dma_start(x_res[:, :, :], x.rearrange("b (t p) d -> p (b t) d", p=P)).then_inc(s_x, 16)
            rows = {"norm_mix": norm_mix, "norm_mlstm": norm_mlstm, "s5_d": s5_d, "norm_s5": norm_s5,
                    "norm_ffn": norm_ffn}
            for l in range(DEPTH):
                for name, n in VEC_ROWS:
                    a = vec_col(l, name)
                    if name == "conv":
                        src = conv_qk[l].rearrange("w (k p) -> (w k) p", p=P)
                    else:
                        src = rows[name][l].rearrange("(k p) -> k p", p=P)
                    sp.dma_start(vec_rows[a:a + n, :], src).then_inc(s_par, 16)
            for i, a in enumerate((s5_a_re, s5_a_im)):
                sp.dma_start(s5_rows[32 * i:32 * i + 32, :],
                             a.rearrange("l (g h) s -> (l g) (h s)", h=2)).then_inc(s_par, 16)
            sp.dma_start(dt_rows[64:96, :], s5_log_dt.rearrange("l (g h) -> (l g) h", h=2)).then_inc(s_par, 16)
            for i, b in enumerate((b_igate, b_fgate)):
                sp.dma_start(b_if[:, :, i], b.rearrange("l h -> h l"),
                             allow_slow_non_contiguous=True).then_inc(s_par, 16)

            def layer_params(l):
                for i, b in enumerate((s5_b_re, s5_b_im)):
                    sp.dma_start(b_raw[:, i, :, :],
                                 b[l].rearrange("(g h) s c -> (h s) g c", h=2)).then_inc(s_bc, 16)
                for i, c in enumerate((s5_c_re, s5_c_im)):
                    sp.dma_start(c_raw[:, i, :, :],
                                 c[l].rearrange("(k g) c s -> (g c) k s", k=CT)).then_inc(s_bc, 16)
                if l:
                    wait_drained(sp, ("if", l - 1))
                sp.dma_start(w_if[:, :, :],
                             w_in[l, :, IF0:U0].rearrange("(k p) n -> p k n", p=P)).then_inc(s_wif, 16)

            layer_params(0)
            sp.dma_start(w_rt[:, :, :], moe_w_router[0].rearrange("(k p) n -> p k n", p=P)).then_inc(s_rt_in, 16)
            sp.dma_start(b_rt[:, :], moe_b_router[0:1, :].to_broadcast([P, NE])).then_inc(s_rt_in, 16)
            wcol = {"q": 0, "k": DML, "v": 2 * DML, "o": 3 * DML, "u": U0}
            for n, c in enumerate(plan):
                if n >= RING:
                    wait_unused(sp, plan[n - RING])
                if c == ("out", 0, 0):
                    sp.wait_ge(blk_ready, 2)
                    layer_params(1)
                slot = ring[:, n % RING, :]
                kind = c[0]
                if kind in wcol:
                    a = wcol[kind]
                    dst, src = v3(slot, KT), w_in[c[1], :, a:a + 512]
                elif kind == "glu":
                    dst, src = v3(slot[:, 0:DS5 * CT], CT), w_glu[c[1]]
                elif kind == "out":
                    dst, src = v3(slot, KT), w_out[c[1], :, 512 * c[2]:512 * c[2] + 512]
                else:
                    a, b = c[1] * GW, min(c[1] * GW + GW, FD)
                    if kind == "fd":
                        dst = v3(slot[:, 0:(b - a) // P * DM], (b - a) // P)
                        src = ffn_w_down[0, a:b, :]
                    else:
                        dst = v3(slot[:, 0:KT * (b - a)], KT)
                        src = (ffn_w_gate if kind == "fg" else ffn_w_up)[0, :, a:b]
                sp.dma_start(dst, src.rearrange("(k p) n -> p k n", p=P)).then_inc(ring_full[n % RING], 16)

            order = []
            for j in range(NJ):
                order += [("g", j), ("u", j)] + ([("d", j - 1)] if j else [])
            order.append(("d", NJ - 1))

            def load_item(e, it, first=False):
                for m, (kind, j) in enumerate(order):
                    s = m % MRING
                    if m >= MRING or not first:
                        bk, bj = order[m - MRING]
                        sp.wait_ge({"g": e_gate, "u": e_up, "d": e_down}[bk],
                                   it * NJ + (bj + 1 - (NJ if m < MRING else 0)))
                    elif m < RING:
                        wait_unused(sp, plan[max(n for n in range(len(plan)) if n % RING == s)])
                    elif m == RING:
                        wait_drained(sp, ("oh", 1, NT - 1, 1))
                        sp.dma_start(gfin, norm_final.rearrange("(a n) -> a n", a=1)
                                     .to_broadcast([P, DM])).then_inc(s_gfin, 16)
                    a = j * GW
                    if kind == "d":
                        src = moe_w_down[0, bass.ds(e, 1), a:a + GW, :]
                        dst = v3(m_ring[s], GW // P)
                    else:
                        src = (moe_w_gate if kind == "g" else moe_w_up)[0, bass.ds(e, 1), :, a:a + GW]
                        dst = v3(m_ring[s], KT)
                    sp.dma_start(dst, src.rearrange("e (k p) n -> p (e k) n", p=P)).then_inc(ring_full[s], 16)

            load_item(0, 0, first=True)
            with sp.Fori(1, NE) as e:
                load_item(e, e)
            sp.wait_ge(items_ready, 1)
            n_over = sp.value_load(n_list[0:1, 0:1], min_val=0, max_val=3)
            with sp.If(n_over > 0):
                with sp.Fori(0, n_over) as k:
                    e = sp.value_load(n_list[0:1, bass.ds(k + 1, 1)], min_val=0, max_val=NE - 1)
                    load_item(e, k + NE)
            for t in range(NT):
                sp.wait_ge(fin_ready, t + 1)
                sp.dma_start(out[0, t * P:(t + 1) * P, :], hn[:, t, :]).then_inc(s_out, 16)
            sp.wait_ge(s_out, 16 * NT)

        @block.gpsimd
        def _(pool):
            chain = [0]

            def link(ins):
                chain[0] += 1
                ins.then_inc(pool_chain, 1)
                pool.wait_ge(pool_chain, chain[0])

            nc.gpsimd.memset(neg_half[:, :], -0.5)
            nc.gpsimd.memset(half_pi[:, :], math.pi / 2)
            nc.gpsimd.memset(ident[:, :], 0.0)
            nc.gpsimd.memset(lower[:, :], 1.0)
            nc.gpsimd.memset(cmask[:, :], 0.0)
            nc.gpsimd.memset(head_pick[:, :, :], 0.0)
            link(nc.gpsimd.memset(ones[:, :], 1.0))
            nc.gpsimd.affine_select(out=ident[:, :], in_=ident[:, :], compare_op=ALU.not_equal, fill=1.0, base=0,
                                    pattern=[[-1, P]], channel_multiplier=1)
            nc.gpsimd.affine_select(out=lower[:, :], in_=lower[:, :], compare_op=ALU.is_gt, fill=0.0, base=0,
                                    pattern=[[1, P]], channel_multiplier=-1)
            nc.gpsimd.affine_select(out=cmask[:, :], in_=cmask[:, :], compare_op=ALU.is_ge, fill=NEG, base=0,
                                    pattern=[[1, SEQ]], channel_multiplier=-1)
            nc.gpsimd.affine_select(out=head_pick[:, :, :], in_=head_pick[:, :, :], compare_op=ALU.not_equal,
                                    fill=-1.0, base=0, pattern=[[-1, NH], [0, P]], channel_multiplier=1)
            nc.gpsimd.iota(times[:, :], pattern=[[1, SEQ]], base=0, channel_multiplier=0,
                           allow_small_or_imprecise_dtypes=True).then_inc(consts, 1)
            pool.wait_ge(consts, 1)

            def rsqrt(cols):
                nc.gpsimd.tensor_tensor(small[:, cols], small[:, cols], neg_half[:, 0:cols.stop - cols.start],
                                        ALU.pow).then_inc(rs_ready, 1)

            def phases(l, i2):
                n = l * PAIRS // 2 + i2
                if n:
                    pool.wait_ge(phase_ready, n)
                for k in range(2):
                    i = 2 * i2 + k
                    nc.gpsimd.tensor_scalar(turn[:, 0, k, :], times[:, :], fac[:, 20, i:i + 1], None, ALU.mult)
                    ins = nc.gpsimd.tensor_scalar(turn[:, 2, k, :], times[:, :], fac[:, 21, i:i + 1], None, ALU.mult)
                link(ins)
                link(nc.gpsimd.tensor_scalar(turn[:, 1, :, :], turn[:, 0, :, :], ROUND_INT, ROUND_INT,
                                             ALU.add, ALU.subtract))
                link(nc.gpsimd.tensor_tensor(turn[:, 0, :, :], turn[:, 0, :, :], turn[:, 1, :, :], ALU.subtract))
                link(nc.gpsimd.tensor_tensor(turn[:, 0, :, :], turn[:, 0, :, :], turn[:, 2, :, :], ALU.add))
                link(nc.gpsimd.tensor_scalar(turn[:, 1, :, :], turn[:, 0, :, :], ROUND_INT, ROUND_INT,
                                             ALU.add, ALU.subtract))
                if n:
                    pool.wait_ge(trig_ready, n)
                nc.gpsimd.tensor_tensor(phase[:, 0, :, :], turn[:, 0, :, :], turn[:, 1, :, :],
                                        ALU.subtract).then_inc(phase_ready, 1)

            for l in range(DEPTH):
                pool.wait_ge(ms_ready, 3 * l + 1)
                rsqrt(slice(0, NT))
                pool.wait_ge(fac_ready, l + 1)
                for i2 in range(PAIRS // 2):
                    phases(l, i2)
                wait_drained(pool, ("ss", l))
                rsqrt(slice(8, 8 + NT))
                pool.wait_ge(ms_ready, 3 * l + 2)
                rsqrt(slice(16, 16 + NT * NH))
                pool.wait_ge(ms_ready, 3 * l + 3)
                rsqrt(slice(0, NT))
            pool.wait_ge(ms_ready, 3 * DEPTH + 1)
            rsqrt(slice(0, NT))

        @block.scalar
        def _(act):
            chain = [0]

            def link(ins):
                chain[0] += 1
                ins.then_inc(act_chain, 1)
                act.wait_ge(act_chain, chain[0])

            def prep(l):
                act.wait_ge(prep_in, 3 * l + 1)
                nc.scalar.activation(fac[:, 0, :], s5p[:, 2, l, :], ACT.Exp).then_inc(fac_act, 1)
                act.wait_ge(prep_in, 3 * l + 2)
                nc.scalar.activation(fac[:, 1, :], fac[:, 4, :], ACT.Exp).then_inc(fac_act, 1)
                act.wait_ge(prep_in, 3 * l + 3)
                nc.scalar.activation(fac[:, 2, :], fac[:, 5, :], ACT.Sin).then_inc(fac_act, 1)
                nc.scalar.activation(fac[:, 3, :], fac[:, 6, :], ACT.Sin, scale=-1.0,
                                     bias=half_pi[:, 0:1]).then_inc(fac_act, 1)
                for i, n in enumerate(("b_re", "b_im")):
                    arrived(act, (n, l))
                    nc.scalar.activation(bT[:, i, :, :], v3(bank((n, l))[:, :], CT),
                                         ACT.Copy).then_inc(drained["A"], 1)

            def xT(l, what):
                for j in (1, 3):
                    arrived(act, ("xT", l, what, j))
                    for k in range(2):
                        c = vec_col(l, ("norm_mix", "norm_ffn")[what], 2 * j + k)
                        ins = nc.scalar.activation(hnT[:, 2 * j + k, :], bank(("xT", l, what, j))[:, k * SEQ:(k + 1) * SEQ],
                                                   ACT.Copy, scale=vec[:, c:c + 1])
                    ins.then_inc(drained["A"], 1)

            def trig_pair(l, i2):
                n = l * PAIRS // 2 + i2
                act.wait_ge(phase_ready, n + 1)
                if n >= 2:
                    act.wait_ge(tile_done, 2 * (n - 1))
                b = i2 % 2
                link(nc.scalar.activation(phase[:, 1, :, :], phase[:, 0, :, :], ACT.Abs))
                nc.scalar.activation(trig[:, b, :, 1, :], phase[:, 0, :, :], ACT.Sin, scale=SIN_SCALE)
                nc.scalar.activation(trig[:, b, :, 0, :], phase[:, 1, :, :], ACT.Sin, scale=-SIN_SCALE,
                                     bias=half_pi[:, 0:1])
                ins = nc.scalar.activation(trig[:, b, :, 2, :], phase[:, 1, :, :], ACT.Sin, scale=-SIN_SCALE,
                                           bias=half_pi[:, 0:1])
                ins.then_inc(trig_ready, 1)

            def mixer(l):
                for i in range(2):
                    arrived(act, ("u", l, i))
                    nc.scalar.activation(uT[:, 2 * i:2 * i + 2, :], v3(bank(("u", l, i))[:, :], 2),
                                         ACT.Copy).then_inc(drained["A"], 1)
                trig_pair(l, 0)
                trig_pair(l, 1)
                for i in range(PAIRS):
                    for n in mixer_steps(l).get(i, []):
                        if n[0] == "if":
                            continue
                        arrived(act, n)
                        src = bank(n)[:, :]
                        if n[0] == "qk":
                            dst = qk_pre[:, 2 * n[2]:2 * n[2] + 2, CW - 1:]
                            nc.scalar.activation(dst, v3(src, 2), ACT.Copy).then_inc(drained["A"], 1)
                        elif n[0] == "v":
                            nc.scalar.activation(v_aug[:, n[2], :, 0:DH], v3(src, NH),
                                                 ACT.Copy).then_inc(drained["A"], 1)
                        else:
                            nc.scalar.activation(o_gate[:, n[2], :], src, ACT.Tanh,
                                                 scale=0.5).then_inc(drained["A"], 1)
                    if i % 2 == 1 and i // 2 + 2 < PAIRS // 2:
                        trig_pair(l, i // 2 + 2)
                    if i in (5, 7, 9, 11):
                        m = (i - 5) // 2
                        act.wait_ge(conv_ready, 4 * l + m + 1)
                        nc.scalar.activation(qk[:, 2 * m:2 * m + 2, :], qk[:, 2 * m:2 * m + 2, :],
                                             ACT.Silu).then_inc(qk_ready, 1)
                for c in range(CT):
                    wait_drained(act, ("y", l, c))
                    nc.scalar.activation(gT[:, c, :], ysT[:, c, :], ACT.Square).then_inc(y_in, 1)
                    act.wait_ge(y_tanh, CT * l + c + 1)
                    nc.scalar.activation(gT[:, c, :], gT[:, c, :], ACT.Tanh, scale=GELU_B).then_inc(y_ready, 1)
                act.wait_ge(g_in, 2 * l + 1)
                link(nc.scalar.activation(gates[0:NH, 2, :], gates[0:NH, 1, :], ACT.Exp))
                nc.scalar.activation(gates[0:NH, 3, :], gates[0:NH, 2, :], ACT.Ln, bias=1.0).then_inc(g_out, 1)
                act.wait_ge(g_in, 2 * l + 2)
                nc.scalar.activation(gates[0:NH, 8, :], gates[0:NH, 7, :], ACT.Exp).then_inc(gate_rows, 1)
                arrived(act, ("tr", l))
                nc.scalar.activation(small[:, 32:32 + 4 * NH], bank(("tr", l))[:, 0:4 * NH],
                                     ACT.Copy).then_inc(drained["A"], 1)
                for i in range(2):
                    arrived(act, ("z", l, i))
                    nc.scalar.activation(ysT[:, 2 * i:2 * i + 2, :], v3(bank(("z", l, i))[:, :], 2), ACT.Tanh,
                                         scale=0.25).then_inc(drained["A"], 1)
                for h in range(NH):
                    wait_drained(act, ("mu", l, h))
                    nc.scalar.activation(dec[:, h % 2, :], dec[:, h % 2, :], ACT.Exp).then_inc(dec_ready, 1)
                for i in range(2):
                    arrived(act, ("hmT", l, i))
                    for k in range(2):
                        c = vec_col(l, "norm_mlstm", 2 * i + k)
                        ins = nc.scalar.activation(mixT[:, 2 * i + k, :], bank(("hmT", l, i))[:, k * SEQ:(k + 1) * SEQ],
                                                   ACT.Copy, scale=vec[:, c:c + 1])
                    ins.then_inc(drained["A"], 1)

            prep(0)
            for l in range(DEPTH):
                xT(l, 0)
                mixer(l)
                if l == 0:
                    prep(1)
                xT(l, 1)
                if l == 0:
                    for f in range(FT):
                        arrived(act, ("gu", f))
                        if f >= 2:
                            wait_drained(act, ("gu", f - 2))
                        nc.scalar.activation(f_silu[:, f % 2, :], bank(("gu", f))[:, 0:SEQ],
                                             ACT.Silu).then_inc(ffn_silu, 1)
            act.wait_ge(route_in, 1)
            nc.scalar.activation(rt[:, 8, :, 0:1], rt[:, 7, :, 0:1], ACT.Exp).then_inc(route_exp, 1)

            def finish_y(it):
                act.wait_ge(e_tr, NJ * it)
                nc.scalar.activation(e_hidT, v3(ps[4][:, :], 4), ACT.Copy).then_inc(a_hT, 1)
                act.wait_ge(e_down, it * NJ)
                nc.scalar.activation(ye[:, 0:512], ps[6][:, :], ACT.Copy)
                nc.scalar.activation(ye[:, 512:1024], ps[7][:, :], ACT.Copy).then_inc(a_ye, 1)

            def item(it, first=False):
                for j in range(NJ):
                    act.wait_ge(e_gate, it * NJ + (j + 1))
                    if j == 0 and not first:
                        act.wait_ge(v_hid, it * NJ)
                    elif j >= 2 or (j and not first):
                        act.wait_ge(v_hid, it * NJ + (j - 1))
                    nc.scalar.activation(e_silu[:, j % 2, :], ps[2 * (j % 2)][:, :], ACT.Silu).then_inc(a_silu, 1)
                    if j == 0:
                        if not first:
                            finish_y(it)
                        continue
                    act.wait_ge(e_tr, it * NJ + j)
                    nc.scalar.activation(e_hidT, v3(ps[4][:, :], 4), ACT.Copy).then_inc(a_hT, 1)
                    if j == 1:
                        act.wait_ge(e_pt, it + 1)
                        nc.scalar.activation(pickT, v3(ps[5][:, 0:SEQ], NT), ACT.Copy).then_inc(a_pt, 1)

            item(0, first=True)
            with act.Fori(1, NE) as e:
                item(e)
            act.wait_ge(items_ready, 1)
            n_over = act.value_load(n_list[0:1, 0:1], min_val=0, max_val=3)
            with act.If(n_over > 0):
                with act.Fori(0, n_over) as k:
                    item(k + NE)
            finish_y(n_over + NE)

        @block.vector
        def _(dve):
            V = nc.vector
            chain = [0]

            def link(ins):
                chain[0] += 1
                ins.then_inc(dve_chain, 1)
                dve.wait_ge(dve_chain, chain[0])

            def norm(n):
                for t in range(NT):
                    ins = V.tensor_tensor_reduce(out=hn[:, t, :], in0=x_res[:, t, :], in1=x_res[:, t, :], scale=1.0,
                                                 scalar=0.0, op0=ALU.mult, op1=ALU.add, accum_out=small[:, t:t + 1])
                link(ins)
                V.tensor_scalar(small[:, 0:NT], small[:, 0:NT], 1.0 / DM, EPS, ALU.mult, ALU.add).then_inc(ms_ready, 1)
                dve.wait_ge(rs_ready, n)
                for t in range(NT):
                    if n == 4 * DEPTH + 1:
                        continue
                    V.tensor_scalar(hn[:, t, :], x_res[:, t, :], small[:, t:t + 1], None,
                                    ALU.mult).then_inc(hn_ready, 1)

            def xT(l, what):
                for j in (0, 2):
                    arrived(dve, ("xT", l, what, j))
                    for k in range(2):
                        c = vec_col(l, ("norm_mix", "norm_ffn")[what], 2 * j + k)
                        ins = V.tensor_scalar(hnT[:, 2 * j + k, :], bank(("xT", l, what, j))[:, k * SEQ:(k + 1) * SEQ],
                                              vec[:, c:c + 1], None, ALU.mult)
                    ins.then_inc(drained["V"], 1)

            def prep(l):
                a_re, a_im = s5p[:, 0, l, :], s5p[:, 1, l, :]
                F = lambda i: fac[:, i, :]
                V.tensor_copy(F(7), a_re).then_inc(prep_in, 1)
                dve.wait_ge(fac_act, 4 * l + 1)
                V.tensor_tensor(F(4), a_re, F(0), ALU.mult).then_inc(prep_in, 1)
                link(V.tensor_tensor(F(8), a_im, F(0), ALU.mult))
                link(V.tensor_scalar(F(9), F(8), 1.0 / TWO_PI, ROUND_INT, ALU.mult, ALU.add))
                link(V.tensor_scalar(F(9), F(9), ROUND_INT, None, ALU.subtract))
                link(V.scalar_tensor_tensor(out=F(8), in0=F(9), scalar=-PI_A, in1=F(8), op0=ALU.mult, op1=ALU.add))
                link(V.scalar_tensor_tensor(out=F(8), in0=F(9), scalar=-PI_B, in1=F(8), op0=ALU.mult, op1=ALU.add))
                link(V.scalar_tensor_tensor(out=F(8), in0=F(9), scalar=-PI_C, in1=F(8), op0=ALU.mult, op1=ALU.add))
                link(V.tensor_scalar(F(5), F(8), 3.1415925, -3.1415925, ALU.min, ALU.max))
                V.scalar_tensor_tensor(out=F(6), in0=F(5), scalar=-1.0, in1=F(5), op0=ALU.mult,
                                       op1=ALU.max).then_inc(prep_in, 1)
                link(V.tensor_scalar(F(9), F(8), 1.0 / TWO_PI, None, ALU.mult))
                link(V.tensor_scalar(F(20), F(9), ROUND_12, ROUND_12, ALU.add, ALU.subtract))
                V.tensor_tensor(F(21), F(9), F(20), ALU.subtract)
                link(V.tensor_tensor(F(10), a_re, a_re, ALU.mult))
                link(V.tensor_tensor(F(11), a_im, a_im, ALU.mult))
                link(V.tensor_tensor(F(10), F(10), F(11), ALU.add))
                link(V.reciprocal(F(10), F(10)))
                dve.wait_ge(fac_act, 4 * l + 4)
                link(V.tensor_tensor(F(12), F(1), F(3), ALU.mult))
                link(V.tensor_scalar(F(12), F(12), 1.0, None, ALU.subtract))
                link(V.tensor_tensor(F(13), F(1), F(2), ALU.mult))
                V.tensor_tensor(F(14), F(12), a_re, ALU.mult)
                link(V.tensor_tensor(F(15), F(13), a_im, ALU.mult))
                link(V.tensor_tensor(F(14), F(14), F(15), ALU.add))
                V.tensor_tensor(F(15), F(13), a_re, ALU.mult)
                link(V.tensor_tensor(F(16), F(12), a_im, ALU.mult))
                link(V.tensor_tensor(F(15), F(15), F(16), ALU.subtract))
                V.tensor_tensor(F(17), F(14), F(10), ALU.mult)
                link(V.tensor_tensor(F(18), F(15), F(10), ALU.mult))
                V.tensor_copy(F(19), F(1)).then_inc(fac_ready, 1)
                f_re = F(17).unsqueeze(2).to_broadcast([P, PAIRS, GP])
                f_im = F(18).unsqueeze(2).to_broadcast([P, PAIRS, GP])
                dve.wait_ge(s_bc, 64 * (l + 1))
                V.memset(b_blk, 0.0)
                V.tensor_tensor(b_tmp[:, 0], b_raw[:, 0], f_re, ALU.mult)
                V.tensor_tensor(b_tmp[:, 1], b_raw[:, 1], f_im, ALU.mult)
                V.tensor_tensor(b_tmp[:, 2], b_raw[:, 1], f_re, ALU.mult)
                link(V.tensor_tensor(b_tmp[:, 3], b_raw[:, 0], f_im, ALU.mult))
                for g in range(2):
                    r = slice(NS * g, NS * g + NS)
                    V.tensor_tensor(b_blk[r, 0, :, g, :], b_tmp[r, 0], b_tmp[r, 1], ALU.subtract)
                    ins = V.tensor_tensor(b_blk[r, 1, :, g, :], b_tmp[r, 2], b_tmp[r, 3], ALU.add)
                ins.then_inc(blk_ready, 1)
                for g in range(2):
                    ins = V.tensor_copy(c_dup[:, :, :, g, :].rearrange("p a b c -> p (a b) c"),
                                        c_raw[:, :, :, :].rearrange("p a b c -> p (a b) c"))
                ins.then_inc(blk_ready, 1)
                link(V.memset(cT[:, :, :, :], 0.0))
                for i, n in enumerate(("c_re", "c_im")):
                    arrived(dve, (n, l))
                    src = bank((n, l))[:, :].rearrange("p (k g c) -> p k g c", g=2, c=GP)
                    for g in range(2):
                        r = slice(NS * g, NS * g + NS)
                        for m, sign in ((0, 1.0), (1, -1.0)) if i == 0 else ((2, -1.0),):
                            dst = cT[r, m, :, :].rearrange("p a b -> p (a b)") \
                                .rearrange("p (k g c) -> p k g c", g=2, c=GP)[:, :, g, :]
                            ins = V.tensor_scalar(dst, src[r, :, g, :], sign, None, ALU.mult)
                    ins.then_inc(drained["V"], 1)

            def s5_tile(l, i):
                n = l * PAIRS + i
                b, k = (i // 2) % 2, i % 2
                dve.wait_ge(trig_ready, n // 2 + 1)
                arrived(dve, ("bu", l, i))
                bu = v3(bank(("bu", l, i))[:, :], 2)
                V.tensor_tensor(rot[:, 0, :, :], bu, trig[:, b, k, 0:2, :], ALU.mult)
                ins = V.tensor_tensor(rot[:, 1, :, :], bu, trig[:, b, k, 1:3, :], ALU.mult)
                ins.then_inc(drained["V"], 1)
                wait_drained(dve, ("bu", l, i))
                V.tensor_tensor(drive[:, 0, :], rot[:, 0, 0, :], rot[:, 0, 1, :], ALU.add)
                link(V.tensor_tensor(drive[:, 1, :], rot[:, 1, 1, :], rot[:, 1, 0, :], ALU.subtract))
                decay = fac[:, 19, i:i + 1].to_broadcast([P, SEQ])
                V.tensor_tensor_scan(state[:, 0, :], decay, drive[:, 0, :], 0.0, ALU.mult, ALU.add)
                link(V.tensor_tensor_scan(state[:, 1, :], decay, drive[:, 1, :], 0.0, ALU.mult, ALU.add))
                if n >= 2:
                    dve.wait_ge(back_used, n - 1)
                V.tensor_tensor(back[:, n % 2, 0, :, :], state[:, :, :], trig[:, b, k, 0:2, :], ALU.mult)
                V.tensor_tensor(back[:, n % 2, 1, :, :], state[:, :, :], trig[:, b, k, 1:3, :],
                                ALU.mult).then_inc(tile_done, 1)

            def y_tile(l, c):
                arrived(dve, ("y", l, c))
                col = vec_col(l, "s5_d", c)
                V.scalar_tensor_tensor(out=ysT[:, c, :], in0=uT[:, c, :], scalar=vec[:, col:col + 1],
                                       in1=bank(("y", l, c))[:, 0:SEQ], op0=ALU.mult,
                                       op1=ALU.add).then_inc(drained["V"], 1)

            def conv(l, m):
                wait_drained(dve, ("qk", l, m))
                for w in range(CW):
                    for k in (2 * m, 2 * m + 1):
                        col = vec_col(l, "conv", w * QK + k)
                        src = qk_pre[:, k, w:w + SEQ]
                        if w == 0:
                            ins = V.tensor_scalar(qk[:, k, :], src, vec[:, col:col + 1], None, ALU.mult)
                        else:
                            ins = V.scalar_tensor_tensor(out=qk[:, k, :], in0=src, scalar=vec[:, col:col + 1],
                                                         in1=qk[:, k, :], op0=ALU.mult, op1=ALU.add)
                    if w < CW - 1:
                        link(ins)
                ins.then_inc(conv_ready, 1)

            def gate_sums(l):
                G = lambda i: gates[0:NH, i, :]
                link(V.tensor_scalar(G(0), G(0), b_if[:, l, 1:2], None, ALU.add))
                V.scalar_tensor_tensor(out=G(1), in0=G(0), scalar=-1.0, in1=G(0), op0=ALU.mult,
                                       op1=ALU.min).then_inc(g_in, 1)
                dve.wait_ge(g_out, l + 1)
                link(V.scalar_tensor_tensor(out=G(4), in0=G(0), scalar=0.0, in1=G(3), op0=ALU.min,
                                            op1=ALU.subtract))
                link(V.tensor_tensor_scan(G(5), ones[0:NH, 0:1].to_broadcast([NH, SEQ]), G(4), 0.0,
                                          ALU.mult, ALU.add))
                link(V.scalar_tensor_tensor(out=G(6), in0=G(9), scalar=b_if[:, l, 0:1], in1=G(5), op0=ALU.add,
                                            op1=ALU.subtract))
                link(V.tensor_tensor_scan(G(2), G(6), G(6), 0.0, ALU.max, ALU.max))
                V.scalar_tensor_tensor(out=G(7), in0=G(5), scalar=-1.0, in1=G(2), op0=ALU.mult,
                                       op1=ALU.subtract).then_inc(g_in, 1)

            def head(l, h):
                arrived(dve, ("mu", l, h))
                mu = bank(("mu", l, h))
                if h >= 2:
                    arrived(dve, ("num", l, h - 2))
                a0, a1 = small[:, 32 + h:33 + h], small[:, 32 + NH + h:33 + NH + h]
                if h == 0:
                    wait_drained(dve, ("tr", l))
                V.scalar_tensor_tensor(out=dec[:, h % 2, 0:SEQ], in0=mu[:, 0:SEQ], scalar=a0, in1=cmask[:, :],
                                       op0=ALU.add, op1=ALU.min)
                V.scalar_tensor_tensor(out=dec[:, h % 2, SEQ:], in0=mu[:, P:SEQ], scalar=a1, in1=cmask[:, 0:P],
                                       op0=ALU.add, op1=ALU.min).then_inc(drained["V"], 1)
                arrived(dve, ("sc", l, h))
                dve.wait_ge(dec_ready, NH * l + h + 1)
                V.scalar_tensor_tensor(out=scr[:, h % 2, :], in0=bank(("sc", l, h))[:, 0:SEQ + P], scalar=DH ** -0.5,
                                       in1=dec[:, h % 2, :], op0=ALU.mult, op1=ALU.mult).then_inc(drained["V"], 1)

            def head_out(l, h):
                arrived(dve, ("num", l, h))
                num = v3(bank(("num", l, h))[:, :], 2)
                e = small[:, 32 + 2 * NH:32 + 4 * NH].rearrange("p (t h) -> p t h", t=NT)[:, :, h:h + 1]
                d = small[:, 48 + 2 * h:50 + 2 * h].unsqueeze(2)
                link(V.scalar_tensor_tensor(out=d, in0=num[:, :, DH:DH + 1], scalar=-1.0, in1=e, op0=ALU.mult,
                                            op1=ALU.max))
                link(V.scalar_tensor_tensor(out=d, in0=num[:, :, DH:DH + 1], scalar=1.0, in1=d, op0=ALU.mult,
                                            op1=ALU.max))
                link(V.reciprocal(d, d))
                for t in range(NT):
                    ins = V.tensor_scalar(hm[:, t, h, :], num[:, t, 0:DH], small[:, 48 + 2 * h + t:49 + 2 * h + t],
                                          None, ALU.mult)
                ins.then_inc(drained["V"], 1)
                wait_drained(dve, ("num", l, h))
                for t in range(NT):
                    ins = V.tensor_tensor_reduce(out=rot[:, 0, 0, t * P:(t + 1) * P], in0=hm[:, t, h, :],
                                                 in1=hm[:, t, h, :], scale=1.0, scalar=0.0, op0=ALU.mult,
                                                 op1=ALU.add, accum_out=small[:, 16 + t * NH + h:17 + t * NH + h])
                return ins

            dve.wait_ge(s_par, 16 * (2 * len(VEC_ROWS) + 5))
            V.tensor_copy(s5_rows[64:96, :].rearrange("p (h s) -> p h s", h=2),
                          dt_rows[64:96, :].unsqueeze(2).to_broadcast([32, 2, NS])).then_inc(dt_wide, 1)
            arrived(dve, ("vec",))
            V.tensor_copy(vec[:, :], bank(("vec",))[:, 0:DEPTH * VEC_PER]).then_inc(drained["V"], 1)
            arrived(dve, ("s5p",))
            V.tensor_copy(s5p[:, :, :, :].rearrange("p a l g -> p (a l g)"),
                          bank(("s5p",))[:, 0:3 * DEPTH * PAIRS]).then_inc(drained["V"], 1)
            wait_drained(dve, ("s5p",))
            V.memset(qk_pre[:, :, 0:CW - 1], 0.0)
            link(V.memset(v_aug[:, :, :, DH:DH + 1], 1.0))
            dve.wait_ge(consts, 1)
            prep(0)
            dve.wait_ge(s_x, 16)
            for l in range(DEPTH):
                norm(4 * l + 1)
                xT(l, 0)
                for i in range(PAIRS):
                    s5_tile(l, i)
                    if i % PPC == PPC - 1 and i // PPC:
                        y_tile(l, i // PPC - 1)
                    if i == 3:
                        arrived(dve, ("if", l))
                        gb = bank(("if", l))
                        V.tensor_copy(hm[0:NH, 0, :, :].rearrange("p a b -> p (a b)"),
                                      gb[0:NH, :]).then_inc(drained["V"], 1)
                    if i in (4, 6, 8, 10):
                        conv(l, (i - 4) // 2)
                y_tile(l, CT - 1)
                for c in range(CT):
                    dve.wait_ge(y_in, CT * l + c + 1)
                    link(V.tensor_scalar(gT[:, c, :], gT[:, c, :], GELU_A, 1.0, ALU.mult, ALU.add))
                    V.tensor_tensor(gT[:, c, :], gT[:, c, :], ysT[:, c, :], ALU.mult).then_inc(y_tanh, 1)
                    dve.wait_ge(y_ready, CT * l + c + 1)
                    V.scalar_tensor_tensor(out=gT[:, c, :], in0=gT[:, c, :], scalar=1.0, in1=ysT[:, c, :],
                                           op0=ALU.add, op1=ALU.mult).then_inc(glu_ready, 1)
                dve.wait_ge(back_used, PAIRS * (l + 1))
                wait_drained(dve, ("if", l))
                kept = v3(hm[0:NH, 0, :, :].rearrange("p a b -> p (a b)"), 2)
                V.tensor_copy(gates[0:NH, 9, :], kept[:, 0, :])
                link(V.tensor_copy(gates[0:NH, 0, :], kept[:, 1, :]))
                gate_sums(l)
                for t in range(NT):
                    wait_drained(dve, ("o", l, t))
                    link(V.tensor_scalar(o_gate[:, t, :], o_gate[:, t, :], 0.5, 0.5, ALU.mult, ALU.add))
                for i in range(2):
                    wait_drained(dve, ("z", l, i))
                    V.scalar_tensor_tensor(out=ysT[:, 2 * i:2 * i + 2, :].rearrange("p a b -> p (a b)"),
                                           in0=ysT[:, 2 * i:2 * i + 2, :].rearrange("p a b -> p (a b)"), scalar=1.0,
                                           in1=gT[:, 2 * i:2 * i + 2, :].rearrange("p a b -> p (a b)"),
                                           op0=ALU.add, op1=ALU.mult).then_inc(dve_chain, 1)
                    chain[0] += 1
                dve.wait_ge(dve_chain, chain[0])
                V.tensor_tensor(gT[:, :, :].rearrange("p a b -> p (a b)"), ysT[:, :, :].rearrange("p a b -> p (a b)"),
                                ysT[:, :, :].rearrange("p a b -> p (a b)"), ALU.mult)
                for c in range(CT):
                    col = vec_col(l, "norm_s5", c)
                    ins = V.tensor_scalar(mixT[:, CT + c, :], ysT[:, c, :], vec[:, col:col + 1], None, ALU.mult)
                ins.then_inc(mixed_s5, 1)
                for h in range(NH):
                    head(l, h)
                    if h:
                        head_out(l, h - 1)
                ins = head_out(l, NH - 1)
                link(ins)
                arrived(dve, ("ss", l))
                V.tensor_scalar(small[:, 8:8 + NT], bank(("ss", l))[:, 0:NT], 1.0 / DS5, 16.0 * EPS, ALU.mult,
                                ALU.add).then_inc(drained["V"], 1)
                V.tensor_scalar(small[:, 16:16 + NT * NH], small[:, 16:16 + NT * NH], 1.0 / DH, EPS, ALU.mult,
                                ALU.add).then_inc(ms_ready, 1)
                dve.wait_ge(rs_ready, 4 * l + 3)
                for t in range(NT):
                    for h in range(NH):
                        c = 16 + t * NH + h
                        ins = V.scalar_tensor_tensor(out=hm[:, t, h, :], in0=hm[:, t, h, :], scalar=small[:, c:c + 1],
                                                     in1=o_gate[:, t, h * DH:(h + 1) * DH], op0=ALU.mult, op1=ALU.mult)
                ins.then_inc(hm_ready, 1)
                for t in range(NT):
                    for c in range(2):
                        arrived(dve, ("os", l, t, c))
                        xs = x_res[:, t, 512 * c:512 * c + 512]
                        V.scalar_tensor_tensor(out=xs, in0=bank(("os", l, t, c))[:, :], scalar=small[:, 8 + t:9 + t],
                                               in1=xs, op0=ALU.mult, op1=ALU.add).then_inc(drained["V"], 1)
                for t in range(NT):
                    for c in range(2):
                        arrived(dve, ("oh", l, t, c))
                        xs = x_res[:, t, 512 * c:512 * c + 512]
                        wait_drained(dve, ("os", l, t, c))
                        V.tensor_tensor(xs, bank(("oh", l, t, c))[:, :], xs, ALU.add).then_inc(drained["V"], 1)
                wait_drained(dve, ("oh", l, NT - 1, 1))
                if l == 0:
                    prep(1)
                norm(4 * l + 4)
                xT(l, 1)
                if l == 0:
                    for f in range(FT):
                        dve.wait_ge(ffn_silu, f + 1)
                        if f >= 3:
                            arrived(dve, ("gu", f - 1))
                        V.tensor_tensor(f_hid[:, f % 3, :], f_silu[:, f % 2, :], bank(("gu", f))[:, SEQ:2 * SEQ],
                                        ALU.mult).then_inc(drained["V"], 1)
                    for t in range(NT):
                        for c in range(2):
                            arrived(dve, ("ffn", t, c))
                            xs = x_res[:, t, 512 * c:512 * c + 512]
                            V.tensor_tensor(xs, bank(("ffn", t, c))[:, :], xs, ALU.add).then_inc(drained["V"], 1)
                    wait_drained(dve, ("ffn", NT - 1, 1))

            R = lambda i: rt[:, i, :, :]
            R1 = lambda i: rt[:, i, :, 0:1]
            wide = lambda i: rt[:, i, :, 0:1].to_broadcast([P, NT, NE])
            row = lambda ap: ap.unsqueeze(1).to_broadcast([P, NT, NE])
            for e in range(NE):
                ins = V.memset(desc[:, e:e + 1], float(NE - e))
            link(ins)
            dve.wait_ge(s_rt_in, 32)
            arrived(dve, ("router",))
            V.tensor_tensor(R(0), bank(("router",))[:, 0:NT * NE].rearrange("p (t e) -> p t e", t=NT), row(b_rt[:, :]),
                            ALU.add).then_inc(drained["V"], 1)
            wait_drained(dve, ("router",))

            def first_max(src, top, hot):
                link(V.tensor_reduce(R1(top), R(src), AX, ALU.max))
                link(V.tensor_tensor(R(hot), R(src), wide(top), ALU.is_equal))
                link(V.tensor_tensor(R(hot), R(hot), row(desc), ALU.mult))
                link(V.tensor_reduce(R1(23), R(hot), AX, ALU.max))
                link(V.tensor_tensor(R(hot), R(hot), wide(23), ALU.is_equal))

            first_max(0, 1, 2)
            link(V.scalar_tensor_tensor(out=rt[:, 3, :, :], in0=R(2), scalar=-PICK, in1=R(0), op0=ALU.mult,
                                        op1=ALU.add))
            first_max(3, 4, 5)
            V.tensor_tensor(R1(7), R1(4), R1(1), ALU.subtract).then_inc(route_in, 1)
            V.tensor_tensor(R(6), R(2), R(5), ALU.add).then_inc(route_mask, 1)
            dve.wait_ge(route_exp, 1)
            link(V.tensor_scalar(R1(9), R1(8), 1.0, None, ALU.add))
            link(V.reciprocal(R1(9), R1(9)))
            link(V.tensor_tensor(R1(10), R1(9), R1(8), ALU.mult))
            V.tensor_tensor(R(11), R(2), wide(9), ALU.mult)
            link(V.tensor_tensor(R(12), R(5), wide(10), ALU.mult))
            link(V.tensor_tensor(R(11), R(11), R(12), ALU.add))
            arrived(dve, ("pos",))
            pos = bank(("pos",))
            link(V.scalar_tensor_tensor(out=rt[:, 13, :, :].rearrange("p t e -> p (t e)"), in0=pos[:, 0:NT * NE], scalar=1.0,
                                        in1=rt[:, 6, :, :].rearrange("p t e -> p (t e)"), op0=ALU.add, op1=ALU.mult))
            V.tensor_scalar(R(13), R(13), 1.0, None, ALU.subtract)
            O = lambda i: over[:, i, :]
            link(V.tensor_scalar(O(0), pos[:, NT * NE:NT * NE + NE], float(P), None, ALU.is_gt))
            link(V.tensor_tensor_scan(O(1), ones[:, 0:NE], O(0), 0.0, ALU.mult, ALU.add))
            link(V.tensor_scalar(O(7), desc, -1.0, float(NE), ALU.mult, ALU.add))
            V.tensor_copy(posI[:, :, 0:NE], R(13))
            V.memset(posI[:, :, NE:], -1.0)
            V.memset(gateI[:, :, NE:], 0.0)
            V.tensor_copy(gateI[:, :, 0:NE], R(11))
            link(V.tensor_copy(n_list[:, 0:1], O(1)[:, NE - 1:NE]))
            for k in range(3):
                link(V.tensor_scalar(O(2), O(1), float(k + 1), None, ALU.is_equal))
                link(V.tensor_tensor(O(2), O(2), O(0), ALU.mult))
                link(V.tensor_tensor(O(3), O(2), O(7), ALU.mult))
                link(V.tensor_reduce(O(4)[:, 0:1], O(3), AX, ALU.add))
                link(V.tensor_copy(n_list[:, k + 1:k + 2], O(4)[:, 0:1]))
                link(V.tensor_tensor(R(14), R(13), row(O(2)), ALU.mult))
                link(V.tensor_reduce(R1(15), R(14), AX, ALU.add))
                link(V.tensor_scalar(posI[:, :, NE + k:NE + k + 1], R1(15), float(P), None, ALU.subtract))
                link(V.tensor_tensor(R(14), R(11), row(O(2)), ALU.mult))
                ins = V.tensor_reduce(gateI[:, :, NE + k:NE + k + 1], R(14), AX, ALU.add)
                if k < 2:
                    link(ins)
            ins.then_inc(items_ready, 1)
            dve.wait_ge(items_ready, 1)

            def choose(nxt):
                for t in range(NT):
                    p = posI[:, t, nxt]
                    g = gateI[:, t, nxt]
                    V.tensor_scalar(pick[:, t, :], times[:, 0:P], p, None, ALU.is_equal)
                    ins = V.tensor_scalar(pickg[:, t, :], times[:, 0:P], p, g, ALU.is_equal, ALU.mult)
                ins.then_inc(v_pick, 1)

            gcol = vec_col(1, "norm_ffn")

            def take_tokens(it):
                for half, b in ((0, 5), (1, 2)):
                    dve.wait_ge(e_gather, 2 * it + (half + 1))
                    w = vec[:, gcol + 4 * half:gcol + 4 * half + 4].unsqueeze(2).to_broadcast([P, 4, P])
                    V.tensor_tensor(xe[:, 4 * half:4 * half + 4, :], v3(ps[b][:, :], 4), w,
                                    ALU.mult).then_inc(v_xe, 1)

            def add_out(it):
                for t in range(NT):
                    for c in range(2):
                        n = 2 * t + c
                        dve.wait_ge(e_sc, it * 4 + (n - 3))
                        xs = x_res[:, t, 512 * c:512 * c + 512]
                        V.tensor_tensor(xs, ps[4 + n][:, :], xs, ALU.add).then_inc(v_add, 1)

            def item(it, first=False):
                for j in range(NJ):
                    if j == 1 and not first:
                        add_out(it)
                    dve.wait_ge(e_up, it * NJ + (j + 1))
                    dve.wait_ge(a_silu, it * NJ + (j + 1))
                    V.tensor_tensor(e_hid[:, 2 if j == NJ - 1 else j % 2, :], e_silu[:, j % 2, :],
                                    ps[2 * (j % 2) + 1][:, :], ALU.mult).then_inc(v_hid, 1)
                    if j == 3:
                        dve.wait_ge(e_pt, it + 1)
                        choose(bass.ds(it + 1, 1))
                take_tokens(it + 1)

            choose(slice(0, 1))
            take_tokens(0)
            item(0, first=True)
            with dve.Fori(1, NE) as e:
                item(e)
            n_over = dve.value_load(n_list[0:1, 0:1], min_val=0, max_val=3)
            with dve.If(n_over > 0):
                with dve.Fori(0, n_over) as k:
                    item(k + NE)
            add_out(n_over + NE)
            dve.wait_ge(v_add, (n_over + NE) * 4)
            norm(4 * DEPTH + 1)
            dve.wait_ge(s_gfin, 16)
            for t in range(NT):
                V.scalar_tensor_tensor(out=hn[:, t, :], in0=x_res[:, t, :], scalar=small[:, t:t + 1], in1=gfin,
                                       op0=ALU.mult, op1=ALU.mult).then_inc(fin_ready, 1)

        @block.tensor
        def _(pe):
            M = nc.tensor.matmul

            def done(ins):
                ins.then_inc(product_ready, 1)

            def prep(l):
                pe.wait_ge(blk_ready, 2 * l + 1)
                for i, n in enumerate(("b_re", "b_im")):
                    open_bank(pe, (n, l))
                    for c in range(CT):
                        ins = nc.tensor.transpose(bank((n, l))[:, c * P:(c + 1) * P],
                                                  b_blk[:, i, PPC * c:PPC * c + PPC, :, :]
                                                  .rearrange("p a b c -> p (a b c)"), ident[:, :])
                    done(ins)
                pe.wait_ge(blk_ready, 2 * l + 2)
                for i, n in enumerate(("c_re", "c_im")):
                    open_bank(pe, (n, l))
                    for c in range(CT):
                        ins = nc.tensor.transpose(bank((n, l))[:, c * P:(c + 1) * P],
                                                  c_dup[:, i, c, :, :].rearrange("p a b -> p (a b)"), ident[:, :])
                    done(ins)

            def norm(l, what):
                pe.wait_ge(hn_ready, (2 * l + what + 1) * NT)
                for j in range(4):
                    n = ("xT", l, what, j)
                    open_bank(pe, n)
                    for k in range(2):
                        for t in range(NT):
                            a = (2 * j + k) * P
                            ins = nc.tensor.transpose(bank(n)[:, k * SEQ + t * P:k * SEQ + (t + 1) * P],
                                                      hn[:, t, a:a + P], ident[:, :])
                    done(ins)

            def have_hnT(l, what):
                for j in range(4):
                    wait_drained(pe, ("xT", l, what, j))

            def channels(name, w, cols, last_of=None):
                open_bank(pe, name)
                for i, a in enumerate(cols):
                    for k in range(KT):
                        ins = M(bank(name)[:, i * SEQ:(i + 1) * SEQ], w[:, k, a:a + P], hnT[:, k, :],
                                start=(k == 0), stop=(k == KT - 1))
                return ins

            def mixer(l):
                have_hnT(l, 0)
                chunk_wait(pe, ("u", l))
                for i in range(2):
                    ins = channels(("u", l, i), v3(chunk(("u", l)), KT), (2 * i * P, 2 * i * P + P))
                    done(ins)

                def bu(i):
                    n = ("bu", l, i)
                    open_bank(pe, n)
                    c, j = divmod(i, PPC)
                    r = slice(32 * j, 32 * j + 32)
                    for m in range(2):
                        ins = M(bank(n)[:, m * SEQ:(m + 1) * SEQ], bT[r, m, c, :], uT[r, c, :], start=True, stop=True)
                    done(ins)

                wait_drained(pe, ("u", l, 1))
                wait_drained(pe, ("b_im", l))
                for i in range(4):
                    bu(i)
                for i in range(PAIRS):
                    for n in mixer_steps(l).get(i, []):
                        if n[0] == "if":
                            pe.wait_ge(s_wif, 16 * (l + 1))
                            open_bank(pe, n)
                            for m in range(2):
                                for k in range(KT):
                                    ins = M(bank(n)[0:NH, m * SEQ:(m + 1) * SEQ], w_if[:, k, m * NH:(m + 1) * NH],
                                            hnT[:, k, :], start=(k == 0), stop=(k == KT - 1))
                            done(ins)
                        elif n[0] == "qk":
                            c = ("q" if n[2] < 2 else "k", l)
                            chunk_wait(pe, c)
                            a = (n[2] % 2) * 2 * P
                            done(channels(n, v3(chunk(c), KT), (a, a + P)))
                        else:
                            chunk_wait(pe, (n[0], l))
                            open_bank(pe, n)
                            for k in range(KT):
                                ins = M(bank(n)[:, :], hnT[:, k, n[2] * P:(n[2] + 1) * P],
                                        v3(chunk((n[0], l)), KT)[:, k, :], start=(k == 0), stop=(k == KT - 1))
                            done(ins)
                    if i + 4 < PAIRS:
                        bu(i + 4)
                    n = l * PAIRS + i
                    c, j = divmod(i, PPC)
                    if j == 0:
                        open_bank(pe, ("y", l, c))
                    if i == 0:
                        wait_drained(pe, ("c_im", l))
                    pe.wait_ge(tile_done, n + 1)
                    r = slice(32 * j, 32 * j + 32)
                    for q, (m, a, b) in enumerate(((0, 0, 0), (1, 0, 1), (2, 1, 0), (2, 1, 1))):
                        ins = M(bank(("y", l, c))[r, 0:SEQ], cT[:, m, c, 32 * j:32 * j + 32], back[:, n % 2, a, b, :],
                                start=(q == 0), stop=(q == 3))
                    ins.then_inc(back_used, 1)
                pe.wait_ge(gate_rows, l + 1)
                open_bank(pe, ("tr", l))
                for m, src in enumerate((6, 8)):
                    for t in range(NT):
                        a = (2 * m + t) * NH
                        ins = nc.tensor.transpose(bank(("tr", l))[:, a:a + NH],
                                                  gates[0:NH, src, t * P:(t + 1) * P], ident[0:NH, 0:NH])
                done(ins)
                chunk_wait(pe, ("glu", l))
                pe.wait_ge(glu_ready, CT * (l + 1))
                w = v3(chunk(("glu", l))[:, 0:DS5 * CT], CT)
                for i in range(2):
                    n = ("z", l, i)
                    open_bank(pe, n)
                    for m in range(2):
                        a = (2 * i + m) * P
                        for k in range(CT):
                            ins = M(bank(n)[:, m * SEQ:(m + 1) * SEQ], w[:, k, a:a + P], gT[:, k, :],
                                    start=(k == 0), stop=(k == CT - 1))
                    done(ins)

                def numerator(h):
                    n = ("num", l, h)
                    open_bank(pe, n)
                    wait_drained(pe, ("sc", l, h))
                    num = v3(bank(n)[:, :], 2)
                    s = scr[:, h % 2, :]
                    M(num[:, 0, 0:DH + 1], s[:, 0:P], v_aug[:, 0, h, :], start=True, stop=True)
                    M(num[:, 1, 0:DH + 1], s[:, P:SEQ], v_aug[:, 0, h, :], start=True, stop=False)
                    done(M(num[:, 1, 0:DH + 1], s[:, SEQ:], v_aug[:, 1, h, :], start=False, stop=True))

                pe.wait_ge(qk_ready, 4 * (l + 1))
                for h in range(NH):
                    n = ("mu", l, h)
                    open_bank(pe, n)
                    done(M(bank(n)[:, 0:SEQ], head_pick[:, h, :], gates[0:NH, 2, :], start=True, stop=True))
                    n = ("sc", l, h)
                    open_bank(pe, n)
                    M(bank(n)[:, 0:SEQ], qk[:, NH + h, 0:P], qk[:, h, :], start=True, stop=True)
                    done(M(bank(n)[:, SEQ:SEQ + P], qk[:, NH + h, P:SEQ], qk[:, h, P:SEQ], start=True, stop=True))
                    if h:
                        numerator(h - 1)
                numerator(NH - 1)
                pe.wait_ge(mixed_s5, l + 1)
                n = ("ss", l)
                open_bank(pe, n)
                for t in range(NT):
                    for c in range(CT):
                        ins = M(bank(n)[:, t:t + 1], gT[:, c, t * P:(t + 1) * P], ones[:, 0:1],
                                start=(c == 0), stop=(c == CT - 1))
                done(ins)
                for part, k0 in (("os", CT), ("oh", 0)):
                    if part == "oh":
                        pe.wait_ge(hm_ready, l + 1)
                        for i in range(2):
                            n = ("hmT", l, i)
                            open_bank(pe, n)
                            for k in range(2):
                                for t in range(NT):
                                    ins = nc.tensor.transpose(bank(n)[:, k * SEQ + t * P:k * SEQ + (t + 1) * P],
                                                              hm[:, t, 2 * i + k, :], ident[:, :])
                            done(ins)
                        for i in range(2):
                            wait_drained(pe, ("hmT", l, i))
                    for t in range(NT):
                        for c in range(2):
                            n = (part, l, t, c)
                            chunk_wait(pe, ("out", l, c))
                            open_bank(pe, n)
                            for k in range(4):
                                ins = M(bank(n)[:, :], mixT[:, k0 + k, t * P:(t + 1) * P],
                                        v3(chunk(("out", l, c)), KT)[:, k0 + k, :], start=(k == 0), stop=(k == 3))
                            done(ins)

            pe.wait_ge(consts, 1)
            pe.wait_ge(s_par, 16 * (2 * len(VEC_ROWS) + 5))
            done(nc.tensor.transpose(bank(("vec",))[:, 0:DEPTH * VEC_PER], vec_rows[0:DEPTH * VEC_PER, :],
                                     ident[0:DEPTH * VEC_PER, 0:DEPTH * VEC_PER]))
            pe.wait_ge(dt_wide, 1)
            done(nc.tensor.transpose(bank(("s5p",))[:, 0:96], s5_rows[0:96, :], ident[0:96, 0:96]))
            prep(0)
            for l in range(DEPTH):
                norm(l, 0)
                mixer(l)
                if l == 0:
                    prep(1)
                norm(l, 1)
                have_hnT(l, 1)
                if l == 0:
                    def down(f):
                        j, i = divmod(f, GW // P)
                        chunk_wait(pe, ("fd", j))
                        n = min(GW, FD - j * GW) // P
                        w = v3(chunk(("fd", j))[:, 0:n * DM], n)
                        wait_drained(pe, ("gu", f))
                        for t in range(NT):
                            for c in range(2):
                                if f == 0:
                                    open_bank(pe, ("ffn", t, c))
                                ins = M(bank(("ffn", t, c))[:, :], f_hid[:, f % 3, t * P:(t + 1) * P],
                                        w[:, i, 512 * c:512 * c + 512], start=(f == 0), stop=(f == FT - 1))
                                if f == FT - 1:
                                    done(ins)
                        if i == n - 1 and f < FT - 1:
                            ins.then_inc(ffn_down, 1)

                    for f in range(FT):
                        j, i = divmod(f, GW // P)
                        width = min(GW, FD - j * GW)
                        n = ("gu", f)
                        open_bank(pe, n)
                        for m, c in enumerate(("fg", "fu")):
                            chunk_wait(pe, (c, j))
                            w = v3(chunk((c, j))[:, 0:KT * width], KT)
                            for k in range(KT):
                                ins = M(bank(n)[:, m * SEQ:(m + 1) * SEQ], w[:, k, i * P:(i + 1) * P], hnT[:, k, :],
                                        start=(k == 0), stop=(k == KT - 1))
                        done(ins)
                        if f:
                            down(f - 1)
                    down(FT - 1)

            pe.wait_ge(s_rt_in, 32)
            open_bank(pe, ("router",))
            for t in range(NT):
                for k in range(KT):
                    ins = M(bank(("router",))[:, t * NE:(t + 1) * NE], hnT[:, k, t * P:(t + 1) * P], w_rt[:, k, :],
                            start=(k == 0), stop=(k == KT - 1))
            done(ins)
            pe.wait_ge(route_mask, 1)
            open_bank(pe, ("pos",))
            b = bank(("pos",))
            M(b[:, 0:NE], lower[:, :], rt[:, 6, 0, :], start=True, stop=True)
            M(b[:, NE:2 * NE], ones[:, :], rt[:, 6, 0, :], start=True, stop=False)
            M(b[:, NE:2 * NE], lower[:, :], rt[:, 6, 1, :], start=False, stop=True)
            M(b[:, 2 * NE:3 * NE], ones[:, :], rt[:, 6, 0, :], start=True, stop=False)
            done(M(b[:, 2 * NE:3 * NE], ones[:, :], rt[:, 6, 1, :], start=False, stop=True))

            order = []
            for j in range(NJ):
                order += [("g", j), ("u", j)] + ([("d", j - 1)] if j else [])
            order.append(("d", NJ - 1))
            place = {c: m for m, c in enumerate(order)}

            def slot_wait(it, c):
                m = place[c]
                pe.wait_ge(ring_full[m % MRING], it * 48 + 16 * (uses[m % MRING] + m // MRING + 1))

            def gather(it):
                pe.wait_ge(v_pick, it + 1)
                for half, b in ((0, 5), (1, 2)):
                    for k in range(4):
                        a = (4 * half + k) * P
                        for t in range(NT):
                            ins = M(ps[b][:, k * P:(k + 1) * P], hn[:, t, a:a + P], pick[:, t, :],
                                    start=(t == 0), stop=(t == NT - 1))
                    ins.then_inc(e_gather, 1)

            def half_swiglu(it, kind, j, b, signal):
                c = (kind, j)
                slot_wait(it, c)
                s = place[c] % MRING
                w = v3(m_ring[s], KT)
                for k in range(KT):
                    ins = M(ps[b][:, :], xe[:, k, :], w[:, k, :], start=(k == 0), stop=(k == KT - 1))
                ins.then_inc(signal, 1)
                return ins

            def transpose_hidden(j):
                for i in range(GW // P):
                    ins = nc.tensor.transpose(ps[4][:, i * P:(i + 1) * P],
                                              e_hid[:, 2 if j == NJ - 1 else j % 2, i * P:(i + 1) * P], ident[:, :])
                ins.then_inc(e_tr, 1)

            def down(it, j):
                c = ("d", j)
                slot_wait(it, c)
                s = place[c] % MRING
                w = v3(m_ring[s], GW // P)
                for i in range(GW // P):
                    for h in range(2):
                        ins = M(ps[6 + h][:, :], e_hidT[:, i, :], w[:, i, 512 * h:512 * h + 512],
                                start=(j == 0 and i == 0), stop=(j == NJ - 1 and i == GW // P - 1))
                ins.then_inc(e_down, 1)

            def finish(it):
                pe.wait_ge(a_hT, it * NJ)
                down(it - 1, NJ - 1)

            def scatter(it):
                pe.wait_ge(a_ye, it)
                pe.wait_ge(a_pt, it)
                for t in range(NT):
                    for c in range(2):
                        M(ps[4 + 2 * t + c][:, :], pickT[:, t, :], ye[:, 512 * c:512 * c + 512], start=True,
                          stop=True).then_inc(e_sc, 1)

            def item(it, first=False):
                for j in range(NJ):
                    b = 2 * (j % 2)
                    if j == 0:
                        if not first:
                            pe.wait_ge(v_hid, it * NJ)
                        pe.wait_ge(v_xe, it * 2 + 2)
                    elif j >= 2:
                        pe.wait_ge(v_hid, it * NJ + (j - 1))
                    half_swiglu(it, "g", j, b, e_gate)
                    if j == 1 and not first:
                        scatter(it)
                    if j == 0 and not first:
                        pe.wait_ge(a_hT, it * NJ - 1)
                        transpose_hidden(NJ - 1)
                    if j:
                        pe.wait_ge(v_hid, it * NJ + j)
                        if j >= 2:
                            pe.wait_ge(a_hT, it * NJ + (j - 1))
                        elif not first:
                            pe.wait_ge(v_add, it * 4 - 3)
                        transpose_hidden(j - 1)
                    half_swiglu(it, "u", j, b + 1, e_up)
                    if j == 1:
                        if not first:
                            pe.wait_ge(v_add, it * 4 - 2)
                        for t in range(NT):
                            ins = nc.tensor.transpose(ps[5][:, t * P:(t + 1) * P], pickg[:, t, :], ident[:, :])
                        ins.then_inc(e_pt, 1)
                    if j == NJ - 1:
                        pe.wait_ge(a_pt, it + 1)
                        pe.wait_ge(v_hid, it * NJ + (NJ - 1))
                        gather(it + 1)
                    if j == 0:
                        if not first:
                            finish(it)
                    else:
                        pe.wait_ge(a_hT, it * NJ + j)
                        if j == 1 and not first:
                            pe.wait_ge(v_add, it * 4)
                        down(it, j - 1)

            gather(0)
            item(0, first=True)
            with pe.Fori(1, NE) as e:
                item(e)
            pe.wait_ge(items_ready, 1)
            n_over = pe.value_load(n_list[0:1, 0:1], min_val=0, max_val=3)
            with pe.If(n_over > 0):
                with pe.Fori(0, n_over) as k:
                    item(k + NE)
            n = n_over + NE
            pe.wait_ge(v_hid, n * NJ)
            pe.wait_ge(v_xe, n * 2 + 2)
            pe.wait_ge(a_hT, n * NJ - 1)
            transpose_hidden(NJ - 1)
            finish(n)
            scatter(n)


_INS = ['x', 'norm_mix', 'w_in', 'conv_qk', 'b_igate', 'b_fgate', 'norm_mlstm', 's5_a_re', 's5_a_im', 's5_log_dt',
        's5_b_re', 's5_b_im', 's5_c_re', 's5_c_im', 's5_d', 'w_glu', 'norm_s5', 'w_out', 'norm_ffn', 'ffn_w_gate',
        'ffn_w_up', 'ffn_w_down', 'moe_w_router', 'moe_b_router', 'moe_w_gate', 'moe_w_up', 'moe_w_down',
        'norm_final']
_OUTS = [((1, SEQ, DM), 'float32')]


def kernel(**inputs):
    import numpy as _np
    import concourse.bacc as _bacc
    from concourse import mybir as _mybir
    from concourse.bass_utils import run_bass_kernel_spmd as _run

    nc = _bacc.Bacc("TRN2", target_bir_lowering=False, num_devices=1)
    arrays, args = {}, []
    for name in _INS:
        a = _np.ascontiguousarray(inputs[name])
        arrays[f"in_{name}_dram"] = a
        args.append(nc.dram_tensor(f"in_{name}_dram", a.shape, _mybir.dt.from_np(a.dtype), kind="ExternalInput").ap())
    for i, (shape, dtype) in enumerate(_OUTS):
        dt = _mybir.dt.from_np(_np.dtype(dtype))
        args.append(nc.dram_tensor(f"out_{i}_dram", shape, dt, kind="ExternalOutput").ap())
    trunk_kernel(nc, *args)
    r = _run(nc, [arrays], core_ids=[0])
    got = tuple(r.results[0][f"out_{i}_dram"] for i in range(len(_OUTS)))
    return got[0]
```

```python
from contextlib import ExitStack
import math

import numpy as np
import concourse.bass as bass
from concourse import mybir

F32 = mybir.dt.float32
F32R = mybir.dt.float32r
I32 = mybir.dt.int32
ALU = mybir.AluOpType
ACT = mybir.ActivationFunctionType
AX = mybir.AxisListType.X

P = 128
SEQ, DM = 256, 1024
NT = SEQ // P
KT = DM // P
DEPTH = 2
DH = 128
NH = 4
DML = NH * DH
DS5 = DM - DML
CW = 4
GP = 16
NS = 64
NG = DS5 // GP
CT = DS5 // P
PAIRS = NG // 2
PPC = PAIRS // CT
FD = 2816
FT = FD // P
NE = 8
FE = 3584
GW = 512
NJ = FE // GW
EPS = 1e-6
IF0 = 4 * DML
U0 = IF0 + 2 * NH
QK = 2 * DML // P

CHUNK = 8 * 512
RING = 5
HALF = CHUNK // 2
MRING = 7
PART = HALF // 2
SPLIT = 7
PER_ITEM = 6 * NJ
SPLITS = 2 * PER_ITEM


def item_halves():
    order = []
    for j in range(NJ):
        kinds = [("g", j), ("u", j)] + ([("d", j - 1)] if j else [])
        order += [(k, i, h) for k, i in kinds for h in range(2)]
    return order + [("d", NJ - 1, h) for h in range(2)]


SCATTER = (0, 1, 6, 7)


def part_no(kind, j, z=0):
    return 2 * item_halves().index((kind, j, z // 2)) + z % 2


def after_part(n):
    return n + 1 + SPLIT



TWO_PI = 2.0 * math.pi
PI_A = 6.28125
PI_B = float(np.float32(np.round((TWO_PI - PI_A) * 2.0**21) / 2.0**21))
PI_C = TWO_PI - PI_A - PI_B
ROUND_INT = 1.5 * 2.0**23
ROUND_12 = 1.5 * 2.0**11
SIN_SCALE = 6.283185
NEG = -1.0e30
PICK = 3.0e38
GELU_A = 0.044715
GELU_B = math.sqrt(2.0 / math.pi)

VEC_ROWS = [("norm_mix", KT), ("conv", CW * QK), ("norm_mlstm", NH), ("s5_d", CT), ("norm_s5", CT), ("norm_ffn", KT)]
VEC_PER = sum(n for _, n in VEC_ROWS)


def vec_col(l, name, i=0):
    at = l * VEC_PER
    for n, rows in VEC_ROWS:
        if n == name:
            return at + i
        at += rows
    raise KeyError(name)


def mixer_steps(l):
    proj = {0: [("if", l)], 2: [("qk", l, 0)], 4: [("qk", l, 1)], 6: [("qk", l, 2)], 8: [("qk", l, 3)],
            10: [("v", l, 0)], 12: [("v", l, 1)], 14: [("o", l, 0)], 15: [("o", l, 1)]}
    return proj


def products():
    out = [(("vec",), "V", 0), (("s5p",), "V", 1)]
    turn = {"lo": 0, "hi": 0}

    def lo(name, who):
        out.append((name, who, turn["lo"] % 4))
        turn["lo"] += 1

    def hi(name, who):
        out.append((name, who, 4 + turn["hi"] % 4))
        turn["hi"] += 1

    def norm(l, what):
        for j in range(4):
            lo(("xT", l, what, j), "VA"[j % 2])

    def prep(l):
        for n in ("b_re", "b_im"):
            hi((n, l), "A")
        for n in ("c_re", "c_im"):
            hi((n, l), "V")

    for l in range(DEPTH):
        if l == 0:
            prep(0)
        norm(l, 0)
        for i in range(2):
            hi(("u", l, i), "A")
        for i in range(4):
            lo(("bu", l, i), "V")
        y = 0
        for i in range(PAIRS):
            for n in mixer_steps(l).get(i, []):
                out.append((n, "V" if n[0] == "if" else "A", 4 + turn["hi"] % 2))
                turn["hi"] += 1
            if i + 4 < PAIRS:
                lo(("bu", l, i + 4), "V")
            if i % PPC == PPC - 1:
                out.append((("y", l, i // PPC), "V", 6 + y % 2))
                y += 1
        hi(("tr", l), "A")
        for i in range(2):
            lo(("z", l, i), "A")
        for h in range(NH):
            hi(("mu", l, h), "V")
            hi(("sc", l, h), "V")
            if h:
                lo(("num", l, h - 1), "V")
        lo(("num", l, NH - 1), "V")
        hi(("ss", l), "V")
        for t in range(NT):
            for c in range(2):
                hi(("os", l, t, c), "V")
        for i in range(2):
            lo(("hmT", l, i), "A")
        for t in range(NT):
            for c in range(2):
                lo(("oh", l, t, c), "V")
        if l == 0:
            prep(1)
        norm(l, 1)
        if l == 0:
            for f in range(FT):
                lo(("gu", f), "V")
            for t in range(NT):
                for c in range(2):
                    out.append((("ffn", t, c), "V", 4 + 2 * t + c))
        else:
            out.append((("router",), "V", 4))
            out.append((("pos",), "V", 5))
    return out


class Banks:

    def __init__(self):
        self.at, self.before = {}, {}
        last, count = {}, {"V": 0, "A": 0}
        n = 0
        for name, who, bank in products():
            count[who] += 1
            n += name[0] != "y"
            self.at[name] = (n, who, count[who], bank)
            self.before[name] = last.get(bank)
            last[bank] = name
        self.last = last


def chunk_plan():
    plan = []
    for l in range(DEPTH):
        plan += [("u", l), ("q", l), ("k", l), ("v", l), ("o", l), ("glu", l), ("out", l, 0), ("out", l, 1)]
        if l == 0:
            for j in range((FD + GW - 1) // GW):
                plan += [("fg", j), ("fu", j), ("fd", j)]
    return plan


def trunk_kernel(nc, x, norm_mix, w_in, conv_qk, b_igate, b_fgate, norm_mlstm, s5_a_re, s5_a_im, s5_log_dt,
                 s5_b_re, s5_b_im, s5_c_re, s5_c_im, s5_d, w_glu, norm_s5, w_out, norm_ffn, ffn_w_gate,
                 ffn_w_up, ffn_w_down, moe_w_router, moe_b_router, moe_w_gate, moe_w_up, moe_w_down,
                 norm_final, out):
    banks = Banks()
    plan = chunk_plan()
    chunk_no = {name: n for n, name in enumerate(plan)}

    ctx = ExitStack()
    with ctx:
        def sb(name, shape, dt=F32):
            return ctx.enter_context(nc.sbuf_tensor(name, shape, dt))

        def sem(name):
            return ctx.enter_context(nc.semaphore(name))

        ring = sb("ring", [P, RING, CHUNK])
        arena = sb("arena", [P, 20000])
        arena_end = nc.sbuf_base
        x_res = sb("x_res", [P, NT, DM])
        hn = sb("hn", [P, NT, DM])
        hnT = sb("hnT", [P, KT, SEQ])
        hnT_end = nc.sbuf_base
        ident = sb("ident", [P, P])
        ones = sb("ones", [P, P])
        lower = sb("lower", [P, P])
        cmask = sb("cmask", [P, SEQ])
        times = sb("times", [P, SEQ])
        head_pick = sb("head_pick", [NH, NH, P])
        neg_half = sb("neg_half", [P, NT * NH])
        half_pi = sb("half_pi", [P, 1])
        vec = sb("vec", [P, DEPTH * VEC_PER])
        s5p = sb("s5p", [P, 3, DEPTH, PAIRS])
        bT = sb("bT", [P, 2, CT, P])
        cT = sb("cT", [P, 3, CT, P])
        fac = sb("fac", [P, 24, PAIRS])
        w_if = sb("w_if", [P, KT, 2 * NH])
        w_rt = sb("w_rt", [P, KT, NE])
        b_rt = sb("b_rt", [P, NE])
        b_if = sb("b_if", [NH, DEPTH, 2])
        small = sb("small", [P, 64])

        at = [0]

        def carve(shape, base=None):
            n = int(np.prod(shape))
            a = at[0] if base is None else base
            if base is None:
                at[0] += n
            assert a + n <= 20000, (a, n)
            v = arena[:, a:a + n]
            letters = "abcd"[:len(shape)]
            if len(shape) > 1:
                v = v.rearrange(f"p ({' '.join(letters)}) -> p {' '.join(letters)}",
                                **{k: s for k, s in zip(letters[1:], shape[1:])})
            return v

        qk_pre = carve([QK, SEQ + CW - 1])
        qk = carve([QK, SEQ])
        v_aug = carve([NT, NH, DH + 1])
        o_gate = carve([NT, DML])
        uT = carve([CT, SEQ])
        gT = carve([CT, SEQ])
        ysT = carve([CT, SEQ])
        hm = carve([NT, NH, DH])
        trig_at = at[0]
        trig = carve([2, 2, 3, SEQ])
        turn = carve([3, 2, SEQ])
        phase = carve([2, 2, SEQ])
        rot = carve([2, 2, SEQ])
        drive = carve([2, SEQ])
        state = carve([2, SEQ])
        back = carve([2, 2, 2, SEQ])
        mix_end = at[0]
        mixT = hn[:, :, :].rearrange("p t d -> p (t d)").rearrange("p (k t) -> p k t", t=SEQ)
        sbase = mix_end - 2 * 2 * 2 * SEQ
        dec = carve([2, SEQ + P], sbase)
        scr = carve([2, SEQ + P], sbase + 2 * (SEQ + P))
        gates = carve([10, SEQ], trig_at)
        pbase = mix_end - 8 * SEQ - 2 * SEQ - 2 * SEQ - 4 * SEQ
        b_raw = sb("b_raw", [P, 2, PAIRS, GP])
        c_raw = sb("c_raw", [P, 2, CT, NS])
        b_blk = carve([2, PAIRS, 2, GP], pbase)
        b_tmp = carve([4, PAIRS, GP], pbase + 4 * PAIRS * GP)
        c_dup = carve([2, CT, 2, NS], pbase + 8 * PAIRS * GP)
        vec_rows = carve([P], 0)
        s5_rows = carve([P], P)
        dt_rows = carve([2], 2 * P)
        assert pbase + 8 * PAIRS * GP + 4 * CT * NS <= mix_end
        fbase = QK * (SEQ + CW - 1)
        f_silu = carve([2, SEQ], fbase)
        f_hid = carve([3, SEQ], fbase + 2 * SEQ)
        sq = hn[:, :, :]
        ring_flat = ring[:, :, :].rearrange("p s n -> p (s n)")
        m_ring = [ring_flat[:, s * HALF:(s + 1) * HALF] for s in range(MRING)]

        split_bytes = 4 * SPLIT * PART
        w_hi = nc.alloc_sbuf_tensor_at("w_hi", [P, SPLIT, PART], F32R, offset=arena_end - 2 * split_bytes)
        w_lo = nc.alloc_sbuf_tensor_at("w_lo", [P, SPLIT, PART], F32R, offset=arena_end - split_bytes)
        hidT_at = arena_end - 2 * split_bytes - 8 * GW
        hidT_hi = nc.alloc_sbuf_tensor_at("hidT_hi", [P, GW // P, P], F32R, offset=hidT_at)
        hidT_lo = nc.alloc_sbuf_tensor_at("hidT_lo", [P, GW // P, P], F32R, offset=hidT_at + 4 * GW)
        xe_hi = nc.alloc_sbuf_tensor_at("xe_hi", [P, KT, P], F32R, offset=hnT_end - 8 * KT * P)
        xe_lo = nc.alloc_sbuf_tensor_at("xe_lo", [P, KT, P], F32R, offset=hnT_end - 4 * KT * P)

        def behind(shape, a):
            n = int(np.prod(shape))
            v = ring_flat[:, MRING * HALF + a:MRING * HALF + a + n]
            return v if len(shape) == 1 else v.rearrange("p (a b) -> p a b", a=shape[0])

        e_silu = behind([2, GW], 0)
        e_hid = behind([3, GW], 1024)
        ye = behind([DM], 3072)
        xe = behind([KT, P], 4096)
        gfin = behind([DM], 5120)
        items = NE + 4
        pick = carve([NT, P], 0)
        pickg = carve([NT, P], 256)
        pickT = carve([NT, P], 512)
        rt = carve([24, NT, NE], 768)
        posI = carve([NT, items], 1152)
        gateI = carve([NT, items], 1176)
        over = carve([8, NE], 1200)
        desc = carve([NE], 1264)
        n_list = sb("n_list", [P, 4], I32)

        ps = [ctx.enter_context(nc.psum_tensor(f"ps{i}", [P, 512], F32)) for i in range(8)]

        s_x = sem("s_x")
        s_par = sem("s_par")
        s_bc = sem("s_bc")
        s_wif = sem("s_wif")
        s_rt_in = sem("s_rt_in")
        s_gfin = sem("s_gfin")
        ring_full = [sem(f"ring_full{i}") for i in range(RING)]
        half_full = [sem(f"half_full{i}") for i in range(MRING)]
        ffn_down = sem("ffn_down")
        product_ready = sem("product_ready")
        drained = {"V": sem("drained_v"), "A": sem("drained_a")}
        consts = sem("consts")
        dve_chain = sem("dve_chain")
        act_chain = sem("act_chain")
        pool_chain = sem("pool_chain")
        ms_ready = sem("ms_ready")
        rs_ready = sem("rs_ready")
        hn_ready = sem("hn_ready")
        dt_wide = sem("dt_wide")
        prep_in = sem("prep_in")
        fac_act = sem("fac_act")
        blk_ready = sem("blk_ready")
        fac_ready = sem("fac_ready")
        phase_ready = sem("phase_ready")
        trig_ready = sem("trig_ready")
        tile_done = sem("tile_done")
        back_used = sem("back_used")
        conv_ready = sem("conv_ready")
        qk_ready = sem("qk_ready")
        g_in = sem("g_in")
        g_out = sem("g_out")
        gate_rows = sem("gate_rows")
        y_in = sem("y_in")
        y_tanh = sem("y_tanh")
        y_ready = sem("y_ready")
        glu_ready = sem("glu_ready")
        dec_ready = sem("dec_ready")
        score_ready = sem("score_ready")
        hm_ready = sem("hm_ready")
        mixed_s5 = sem("mixed_s5")
        ffn_silu = sem("ffn_silu")
        route_in = sem("route_in")
        route_exp = sem("route_exp")
        route_mask = sem("route_mask")
        items_ready = sem("items_ready")
        hi_ready = sem("hi_ready")
        lo_ready = sem("lo_ready")
        split_used = sem("split_used")
        e_tr = sem("e_tr")
        e_sc = sem("e_sc")
        e_gather = sem("e_gather")
        e_pt = sem("e_pt")
        a_silu = sem("a_silu")
        a_hT = sem("a_hT")
        a_ye = sem("a_ye")
        a_pt = sem("a_pt")
        v_hid = sem("v_hid")
        v_hT = sem("v_hT")
        v_xe = sem("v_xe")
        xe_steps = sem("xe_steps")
        v_add = sem("v_add")
        v_pick = sem("v_pick")
        fin_ready = sem("fin_ready")
        s_out = sem("s_out")

        def bank(name):
            return ps[banks.at[name][3]]

        def arrived(eng, name):
            if name[0] == "y":
                eng.wait_ge(back_used, PAIRS * name[1] + PPC * (name[2] + 1))
            else:
                eng.wait_ge(product_ready, banks.at[name][0])

        def wait_drained(eng, name):
            _, who, n, _ = banks.at[name]
            eng.wait_ge(drained[who], n)

        def open_bank(eng, name):
            if banks.before[name]:
                wait_drained(eng, banks.before[name])

        def chunk(name):
            return ring[:, chunk_no[name] % RING, :]

        def chunk_wait(eng, name):
            n = chunk_no[name]
            eng.wait_ge(ring_full[n % RING], 16 * (n // RING + 1))

        def wait_unused(eng, c):
            kind, i = c[0], c[1]
            if kind == "fd" and i < FD // GW:
                eng.wait_ge(ffn_down, i + 1)
                return
            last = {"u": ("u", i, 1), "q": ("qk", i, 1), "k": ("qk", i, 3), "v": ("v", i, 1), "o": ("o", i, 1),
                    "glu": ("z", i, 1), "out": ("oh", i, NT - 1, c[-1]), "fd": ("ffn", NT - 1, 1),
                    "fg": ("gu", min(4 * i + 3, FT - 1)), "fu": ("gu", min(4 * i + 3, FT - 1))}[kind]
            arrived(eng, last)

        halves = item_halves()
        place = {c: m for m, c in enumerate(halves)}
        def half_wait(eng, it, c):
            m = place[c]
            eng.wait_ge(half_full[m % MRING], it * (16 * PER_ITEM // MRING) + 16 * (m // MRING + 1))

        def raw_part(q):
            return m_ring[q // 2 % MRING][:, q % 2 * PART:(q % 2 + 1) * PART]

        def part_used(eng, it, kind, j, z=3):
            eng.wait_ge(split_used, it * SPLITS + (part_no(kind, j, z) + 1))

        def v3(ap, k):
            return ap.rearrange("p (k n) -> p k n", k=k)

        block = ctx.enter_context(nc.Block())

        @block.sync
        def _(sp):
            sp.dma_start(x_res[:, :, :], x.rearrange("b (t p) d -> p (b t) d", p=P)).then_inc(s_x, 16)
            rows = {"norm_mix": norm_mix, "norm_mlstm": norm_mlstm, "s5_d": s5_d, "norm_s5": norm_s5,
                    "norm_ffn": norm_ffn}
            for l in range(DEPTH):
                for name, n in VEC_ROWS:
                    a = vec_col(l, name)
                    if name == "conv":
                        src = conv_qk[l].rearrange("w (k p) -> (w k) p", p=P)
                    else:
                        src = rows[name][l].rearrange("(k p) -> k p", p=P)
                    sp.dma_start(vec_rows[a:a + n, :], src).then_inc(s_par, 16)
            for i, a in enumerate((s5_a_re, s5_a_im)):
                sp.dma_start(s5_rows[32 * i:32 * i + 32, :],
                             a.rearrange("l (g h) s -> (l g) (h s)", h=2)).then_inc(s_par, 16)
            sp.dma_start(dt_rows[64:96, :], s5_log_dt.rearrange("l (g h) -> (l g) h", h=2)).then_inc(s_par, 16)
            for i, b in enumerate((b_igate, b_fgate)):
                sp.dma_start(b_if[:, :, i], b.rearrange("l h -> h l"),
                             allow_slow_non_contiguous=True).then_inc(s_par, 16)

            def layer_params(l):
                for i, b in enumerate((s5_b_re, s5_b_im)):
                    sp.dma_start(b_raw[:, i, :, :],
                                 b[l].rearrange("(g h) s c -> (h s) g c", h=2)).then_inc(s_bc, 16)
                for i, c in enumerate((s5_c_re, s5_c_im)):
                    sp.dma_start(c_raw[:, i, :, :],
                                 c[l].rearrange("(k g) c s -> (g c) k s", k=CT)).then_inc(s_bc, 16)
                if l:
                    wait_drained(sp, ("if", l - 1))
                sp.dma_start(w_if[:, :, :],
                             w_in[l, :, IF0:U0].rearrange("(k p) n -> p k n", p=P)).then_inc(s_wif, 16)

            layer_params(0)
            sp.dma_start(w_rt[:, :, :], moe_w_router[0].rearrange("(k p) n -> p k n", p=P)).then_inc(s_rt_in, 16)
            sp.dma_start(b_rt[:, :], moe_b_router[0:1, :].to_broadcast([P, NE])).then_inc(s_rt_in, 16)
            wcol = {"q": 0, "k": DML, "v": 2 * DML, "o": 3 * DML, "u": U0}
            for n, c in enumerate(plan):
                if n >= RING:
                    wait_unused(sp, plan[n - RING])
                if c == ("out", 0, 0):
                    sp.wait_ge(blk_ready, 2)
                    layer_params(1)
                slot = ring[:, n % RING, :]
                kind = c[0]
                if kind in wcol:
                    a = wcol[kind]
                    dst, src = v3(slot, KT), w_in[c[1], :, a:a + 512]
                elif kind == "glu":
                    dst, src = v3(slot[:, 0:DS5 * CT], CT), w_glu[c[1]]
                elif kind == "out":
                    dst, src = v3(slot, KT), w_out[c[1], :, 512 * c[2]:512 * c[2] + 512]
                else:
                    a, b = c[1] * GW, min(c[1] * GW + GW, FD)
                    if kind == "fd":
                        dst = v3(slot[:, 0:(b - a) // P * DM], (b - a) // P)
                        src = ffn_w_down[0, a:b, :]
                    else:
                        dst = v3(slot[:, 0:KT * (b - a)], KT)
                        src = (ffn_w_gate if kind == "fg" else ffn_w_up)[0, :, a:b]
                sp.dma_start(dst, src.rearrange("(k p) n -> p k n", p=P)).then_inc(ring_full[n % RING], 16)

            def load_item(e, it, first=False):
                for m, (kind, j, h) in enumerate(halves):
                    s = m % MRING
                    if m < MRING and first:
                        wait_unused(sp, plan[max(n for n in range(len(plan)) if n % RING == s * HALF // CHUNK)])
                    else:
                        sp.wait_ge(lo_ready, it * SPLITS + 2 * (m - MRING + 1))
                    a = j * GW
                    if kind == "d":
                        a += h * GW // 2
                        src = moe_w_down[0, bass.ds(e, 1), a:a + GW // 2, :]
                        dst = v3(m_ring[s], GW // P // 2)
                    else:
                        src = (moe_w_gate if kind == "g" else moe_w_up)[0, bass.ds(e, 1),
                                                                        h * DM // 2:(h + 1) * DM // 2, a:a + GW]
                        dst = v3(m_ring[s], KT // 2)
                    sp.dma_start(dst, src.rearrange("e (k p) n -> p (e k) n", p=P)).then_inc(half_full[s], 16)
                    if first and m == MRING - 1:
                        wait_drained(sp, ("oh", 1, NT - 1, 1))
                        sp.dma_start(gfin, norm_final.rearrange("(a n) -> a n", a=1)
                                     .to_broadcast([P, DM])).then_inc(s_gfin, 16)

            load_item(0, 0, first=True)
            with sp.Fori(1, NE) as e:
                load_item(e, e)
            sp.wait_ge(items_ready, 1)
            n_over = sp.value_load(n_list[0:1, 0:1], min_val=0, max_val=3)
            with sp.If(n_over > 0):
                with sp.Fori(0, n_over) as k:
                    e = sp.value_load(n_list[0:1, bass.ds(k + 1, 1)], min_val=0, max_val=NE - 1)
                    load_item(e, k + NE)
            for t in range(NT):
                sp.wait_ge(fin_ready, t + 1)
                sp.dma_start(out[0, t * P:(t + 1) * P, :], hn[:, t, :]).then_inc(s_out, 16)
            sp.wait_ge(s_out, 16 * NT)

        @block.gpsimd
        def _(pool):
            chain = [0]

            def link(ins):
                chain[0] += 1
                ins.then_inc(pool_chain, 1)
                pool.wait_ge(pool_chain, chain[0])

            nc.gpsimd.memset(neg_half[:, :], -0.5)
            nc.gpsimd.memset(half_pi[:, :], math.pi / 2)
            nc.gpsimd.memset(ident[:, :], 0.0)
            nc.gpsimd.memset(lower[:, :], 1.0)
            nc.gpsimd.memset(cmask[:, :], 0.0)
            nc.gpsimd.memset(head_pick[:, :, :], 0.0)
            link(nc.gpsimd.memset(ones[:, :], 1.0))
            nc.gpsimd.affine_select(out=ident[:, :], in_=ident[:, :], compare_op=ALU.not_equal, fill=1.0, base=0,
                                    pattern=[[-1, P]], channel_multiplier=1)
            nc.gpsimd.affine_select(out=lower[:, :], in_=lower[:, :], compare_op=ALU.is_gt, fill=0.0, base=0,
                                    pattern=[[1, P]], channel_multiplier=-1)
            nc.gpsimd.affine_select(out=cmask[:, :], in_=cmask[:, :], compare_op=ALU.is_ge, fill=NEG, base=0,
                                    pattern=[[1, SEQ]], channel_multiplier=-1)
            nc.gpsimd.affine_select(out=head_pick[:, :, :], in_=head_pick[:, :, :], compare_op=ALU.not_equal,
                                    fill=-1.0, base=0, pattern=[[-1, NH], [0, P]], channel_multiplier=1)
            nc.gpsimd.iota(times[:, :], pattern=[[1, SEQ]], base=0, channel_multiplier=0,
                           allow_small_or_imprecise_dtypes=True).then_inc(consts, 1)
            pool.wait_ge(consts, 1)

            def rsqrt(cols):
                nc.gpsimd.tensor_tensor(small[:, cols], small[:, cols], neg_half[:, 0:cols.stop - cols.start],
                                        ALU.pow).then_inc(rs_ready, 1)

            def phases(l, i2):
                n = l * PAIRS // 2 + i2
                if n:
                    pool.wait_ge(phase_ready, n)
                for k in range(2):
                    i = 2 * i2 + k
                    nc.gpsimd.tensor_scalar(turn[:, 0, k, :], times[:, :], fac[:, 20, i:i + 1], None, ALU.mult)
                    ins = nc.gpsimd.tensor_scalar(turn[:, 2, k, :], times[:, :], fac[:, 21, i:i + 1], None, ALU.mult)
                link(ins)
                link(nc.gpsimd.tensor_scalar(turn[:, 1, :, :], turn[:, 0, :, :], ROUND_INT, ROUND_INT,
                                             ALU.add, ALU.subtract))
                link(nc.gpsimd.tensor_tensor(turn[:, 0, :, :], turn[:, 0, :, :], turn[:, 1, :, :], ALU.subtract))
                link(nc.gpsimd.tensor_tensor(turn[:, 0, :, :], turn[:, 0, :, :], turn[:, 2, :, :], ALU.add))
                link(nc.gpsimd.tensor_scalar(turn[:, 1, :, :], turn[:, 0, :, :], ROUND_INT, ROUND_INT,
                                             ALU.add, ALU.subtract))
                if n:
                    pool.wait_ge(trig_ready, n)
                nc.gpsimd.tensor_tensor(phase[:, 0, :, :], turn[:, 0, :, :], turn[:, 1, :, :],
                                        ALU.subtract).then_inc(phase_ready, 1)

            for l in range(DEPTH):
                pool.wait_ge(ms_ready, 3 * l + 1)
                rsqrt(slice(0, NT))
                pool.wait_ge(fac_ready, l + 1)
                for i2 in range(PAIRS // 2):
                    phases(l, i2)
                wait_drained(pool, ("ss", l))
                rsqrt(slice(8, 8 + NT))
                pool.wait_ge(ms_ready, 3 * l + 2)
                rsqrt(slice(16, 16 + NT * NH))
                pool.wait_ge(ms_ready, 3 * l + 3)
                rsqrt(slice(0, NT))
            pool.wait_ge(ms_ready, 3 * DEPTH + 1)
            rsqrt(slice(0, NT))

        @block.scalar
        def _(act):
            chain = [0]

            def link(ins):
                chain[0] += 1
                ins.then_inc(act_chain, 1)
                act.wait_ge(act_chain, chain[0])

            def prep(l):
                act.wait_ge(prep_in, 3 * l + 1)
                nc.scalar.activation(fac[:, 0, :], s5p[:, 2, l, :], ACT.Exp).then_inc(fac_act, 1)
                act.wait_ge(prep_in, 3 * l + 2)
                nc.scalar.activation(fac[:, 1, :], fac[:, 4, :], ACT.Exp).then_inc(fac_act, 1)
                act.wait_ge(prep_in, 3 * l + 3)
                nc.scalar.activation(fac[:, 2, :], fac[:, 5, :], ACT.Sin).then_inc(fac_act, 1)
                nc.scalar.activation(fac[:, 3, :], fac[:, 6, :], ACT.Sin, scale=-1.0,
                                     bias=half_pi[:, 0:1]).then_inc(fac_act, 1)
                for i, n in enumerate(("b_re", "b_im")):
                    arrived(act, (n, l))
                    nc.scalar.activation(bT[:, i, :, :], v3(bank((n, l))[:, :], CT),
                                         ACT.Copy).then_inc(drained["A"], 1)

            def xT(l, what):
                for j in (1, 3):
                    arrived(act, ("xT", l, what, j))
                    for k in range(2):
                        c = vec_col(l, ("norm_mix", "norm_ffn")[what], 2 * j + k)
                        ins = nc.scalar.activation(hnT[:, 2 * j + k, :], bank(("xT", l, what, j))[:, k * SEQ:(k + 1) * SEQ],
                                                   ACT.Copy, scale=vec[:, c:c + 1])
                    ins.then_inc(drained["A"], 1)

            def trig_pair(l, i2):
                n = l * PAIRS // 2 + i2
                act.wait_ge(phase_ready, n + 1)
                if n >= 2:
                    act.wait_ge(tile_done, 2 * (n - 1))
                b = i2 % 2
                link(nc.scalar.activation(phase[:, 1, :, :], phase[:, 0, :, :], ACT.Abs))
                nc.scalar.activation(trig[:, b, :, 1, :], phase[:, 0, :, :], ACT.Sin, scale=SIN_SCALE)
                nc.scalar.activation(trig[:, b, :, 0, :], phase[:, 1, :, :], ACT.Sin, scale=-SIN_SCALE,
                                     bias=half_pi[:, 0:1])
                ins = nc.scalar.activation(trig[:, b, :, 2, :], phase[:, 1, :, :], ACT.Sin, scale=-SIN_SCALE,
                                           bias=half_pi[:, 0:1])
                ins.then_inc(trig_ready, 1)

            def mixer(l):
                for i in range(2):
                    arrived(act, ("u", l, i))
                    nc.scalar.activation(uT[:, 2 * i:2 * i + 2, :], v3(bank(("u", l, i))[:, :], 2),
                                         ACT.Copy).then_inc(drained["A"], 1)
                trig_pair(l, 0)
                trig_pair(l, 1)
                for i in range(PAIRS):
                    for n in mixer_steps(l).get(i, []):
                        if n[0] == "if":
                            continue
                        arrived(act, n)
                        src = bank(n)[:, :]
                        if n[0] == "qk":
                            dst = qk_pre[:, 2 * n[2]:2 * n[2] + 2, CW - 1:]
                            nc.scalar.activation(dst, v3(src, 2), ACT.Copy).then_inc(drained["A"], 1)
                        elif n[0] == "v":
                            nc.scalar.activation(v_aug[:, n[2], :, 0:DH], v3(src, NH),
                                                 ACT.Copy).then_inc(drained["A"], 1)
                        else:
                            nc.scalar.activation(o_gate[:, n[2], :], src, ACT.Tanh,
                                                 scale=0.5).then_inc(drained["A"], 1)
                    if i % 2 == 1 and i // 2 + 2 < PAIRS // 2:
                        trig_pair(l, i // 2 + 2)
                    if i in (5, 7, 9, 11):
                        m = (i - 5) // 2
                        act.wait_ge(conv_ready, 4 * l + m + 1)
                        nc.scalar.activation(qk[:, 2 * m:2 * m + 2, :], qk[:, 2 * m:2 * m + 2, :],
                                             ACT.Silu).then_inc(qk_ready, 1)
                for c in range(CT):
                    wait_drained(act, ("y", l, c))
                    nc.scalar.activation(gT[:, c, :], ysT[:, c, :], ACT.Square).then_inc(y_in, 1)
                    act.wait_ge(y_tanh, CT * l + c + 1)
                    nc.scalar.activation(gT[:, c, :], gT[:, c, :], ACT.Tanh, scale=GELU_B).then_inc(y_ready, 1)
                act.wait_ge(g_in, 2 * l + 1)
                link(nc.scalar.activation(gates[0:NH, 2, :], gates[0:NH, 1, :], ACT.Exp))
                nc.scalar.activation(gates[0:NH, 3, :], gates[0:NH, 2, :], ACT.Ln, bias=1.0).then_inc(g_out, 1)
                act.wait_ge(g_in, 2 * l + 2)
                nc.scalar.activation(gates[0:NH, 8, :], gates[0:NH, 7, :], ACT.Exp).then_inc(gate_rows, 1)
                arrived(act, ("tr", l))
                nc.scalar.activation(small[:, 32:32 + 4 * NH], bank(("tr", l))[:, 0:4 * NH],
                                     ACT.Copy).then_inc(drained["A"], 1)
                for i in range(2):
                    arrived(act, ("z", l, i))
                    nc.scalar.activation(ysT[:, 2 * i:2 * i + 2, :], v3(bank(("z", l, i))[:, :], 2), ACT.Tanh,
                                         scale=0.25).then_inc(drained["A"], 1)
                for h in range(NH):
                    wait_drained(act, ("mu", l, h))
                    nc.scalar.activation(dec[:, h % 2, :], dec[:, h % 2, :], ACT.Exp).then_inc(dec_ready, 1)
                for i in range(2):
                    arrived(act, ("hmT", l, i))
                    for k in range(2):
                        c = vec_col(l, "norm_mlstm", 2 * i + k)
                        ins = nc.scalar.activation(mixT[:, 2 * i + k, :], bank(("hmT", l, i))[:, k * SEQ:(k + 1) * SEQ],
                                                   ACT.Copy, scale=vec[:, c:c + 1])
                    ins.then_inc(drained["A"], 1)

            prep(0)
            for l in range(DEPTH):
                xT(l, 0)
                mixer(l)
                if l == 0:
                    prep(1)
                xT(l, 1)
                if l == 0:
                    for f in range(FT):
                        arrived(act, ("gu", f))
                        if f >= 2:
                            wait_drained(act, ("gu", f - 2))
                        nc.scalar.activation(f_silu[:, f % 2, :], bank(("gu", f))[:, 0:SEQ],
                                             ACT.Silu).then_inc(ffn_silu, 1)
            act.wait_ge(route_in, 1)
            nc.scalar.activation(rt[:, 8, :, 0:1], rt[:, 7, :, 0:1], ACT.Exp).then_inc(route_exp, 1)

            def silu(it, j):
                part_used(act, it, "g", j)
                if type(it) is not int or it * NJ + j > 1:
                    act.wait_ge(v_hid, it * NJ + (j - 1 + (j == 0)))
                nc.scalar.activation(e_silu[:, j % 2, :], ps[2 * (j % 2)][:, :], ACT.Silu).then_inc(a_silu, 1)

            def hidden_out(it, j):
                act.wait_ge(e_tr, it * NJ + (j + 1))
                nc.scalar.activation(hidT_hi[:, :, :], v3(ps[4][:, :], 4), ACT.Copy).then_inc(a_hT, 1)

            def y_out(it):
                part_used(act, it, "d", NJ - 1)
                nc.scalar.activation(ye[:, 0:512], ps[6][:, :], ACT.Copy)
                nc.scalar.activation(ye[:, 512:1024], ps[7][:, :], ACT.Copy).then_inc(a_ye, 1)

            def split(it, q, first):
                if q % 2 == 0:
                    half_wait(act, it, halves[q // 2])
                if q >= SPLIT or not first:
                    act.wait_ge(split_used, it * SPLITS + (q - SPLIT + 1))
                nc.scalar.activation(w_hi[:, q % SPLIT, :], raw_part(q), ACT.Copy).then_inc(hi_ready, 1)

            def item(it, first=False):
                for q in range(SPLITS):
                    if not first:
                        if q == after_part(part_no("d", NJ - 2, 3)) - SPLITS:
                            hidden_out(it - 1, NJ - 1)
                        if q == after_part(part_no("d", NJ - 1, 3)) - SPLITS:
                            y_out(it - 1)
                    for j in range(NJ):
                        if q == after_part(part_no("g", j, 3)) - 1:
                            silu(it, j)
                            if j:
                                hidden_out(it, j - 1)
                    if q == after_part(part_no("u", 1, 3)):
                        act.wait_ge(e_pt, it + 1)
                        nc.scalar.activation(pickT, v3(ps[5][:, 0:SEQ], NT), ACT.Copy).then_inc(a_pt, 1)
                    split(it, q, first)

            wait_drained(act, ("oh", 1, NT - 1, 1))
            item(0, first=True)
            with act.Fori(1, NE) as e:
                item(e)
            act.wait_ge(items_ready, 1)
            n_over = act.value_load(n_list[0:1, 0:1], min_val=0, max_val=3)
            with act.If(n_over > 0):
                with act.Fori(0, n_over) as k:
                    item(k + NE)
            last = n_over + (NE - 1)
            hidden_out(last, NJ - 1)
            y_out(last)

        @block.vector
        def _(dve):
            V = nc.vector
            chain = [0]

            def link(ins):
                chain[0] += 1
                ins.then_inc(dve_chain, 1)
                dve.wait_ge(dve_chain, chain[0])

            def norm(n):
                for t in range(NT):
                    ins = V.tensor_tensor_reduce(out=hn[:, t, :], in0=x_res[:, t, :], in1=x_res[:, t, :], scale=1.0,
                                                 scalar=0.0, op0=ALU.mult, op1=ALU.add, accum_out=small[:, t:t + 1])
                link(ins)
                V.tensor_scalar(small[:, 0:NT], small[:, 0:NT], 1.0 / DM, EPS, ALU.mult, ALU.add).then_inc(ms_ready, 1)
                dve.wait_ge(rs_ready, n)
                for t in range(NT):
                    if n == 4 * DEPTH + 1:
                        continue
                    V.tensor_scalar(hn[:, t, :], x_res[:, t, :], small[:, t:t + 1], None,
                                    ALU.mult).then_inc(hn_ready, 1)

            def xT(l, what):
                for j in (0, 2):
                    arrived(dve, ("xT", l, what, j))
                    for k in range(2):
                        c = vec_col(l, ("norm_mix", "norm_ffn")[what], 2 * j + k)
                        ins = V.tensor_scalar(hnT[:, 2 * j + k, :], bank(("xT", l, what, j))[:, k * SEQ:(k + 1) * SEQ],
                                              vec[:, c:c + 1], None, ALU.mult)
                    ins.then_inc(drained["V"], 1)

            def prep(l):
                a_re, a_im = s5p[:, 0, l, :], s5p[:, 1, l, :]
                F = lambda i: fac[:, i, :]
                V.tensor_copy(F(7), a_re).then_inc(prep_in, 1)
                dve.wait_ge(fac_act, 4 * l + 1)
                V.tensor_tensor(F(4), a_re, F(0), ALU.mult).then_inc(prep_in, 1)
                link(V.tensor_tensor(F(8), a_im, F(0), ALU.mult))
                link(V.tensor_scalar(F(9), F(8), 1.0 / TWO_PI, ROUND_INT, ALU.mult, ALU.add))
                link(V.tensor_scalar(F(9), F(9), ROUND_INT, None, ALU.subtract))
                link(V.scalar_tensor_tensor(out=F(8), in0=F(9), scalar=-PI_A, in1=F(8), op0=ALU.mult, op1=ALU.add))
                link(V.scalar_tensor_tensor(out=F(8), in0=F(9), scalar=-PI_B, in1=F(8), op0=ALU.mult, op1=ALU.add))
                link(V.scalar_tensor_tensor(out=F(8), in0=F(9), scalar=-PI_C, in1=F(8), op0=ALU.mult, op1=ALU.add))
                link(V.tensor_scalar(F(5), F(8), 3.1415925, -3.1415925, ALU.min, ALU.max))
                V.scalar_tensor_tensor(out=F(6), in0=F(5), scalar=-1.0, in1=F(5), op0=ALU.mult,
                                       op1=ALU.max).then_inc(prep_in, 1)
                link(V.tensor_scalar(F(9), F(8), 1.0 / TWO_PI, None, ALU.mult))
                link(V.tensor_scalar(F(20), F(9), ROUND_12, ROUND_12, ALU.add, ALU.subtract))
                V.tensor_tensor(F(21), F(9), F(20), ALU.subtract)
                link(V.tensor_tensor(F(10), a_re, a_re, ALU.mult))
                link(V.tensor_tensor(F(11), a_im, a_im, ALU.mult))
                link(V.tensor_tensor(F(10), F(10), F(11), ALU.add))
                link(V.reciprocal(F(10), F(10)))
                dve.wait_ge(fac_act, 4 * l + 4)
                link(V.tensor_tensor(F(12), F(1), F(3), ALU.mult))
                link(V.tensor_scalar(F(12), F(12), 1.0, None, ALU.subtract))
                link(V.tensor_tensor(F(13), F(1), F(2), ALU.mult))
                V.tensor_tensor(F(14), F(12), a_re, ALU.mult)
                link(V.tensor_tensor(F(15), F(13), a_im, ALU.mult))
                link(V.tensor_tensor(F(14), F(14), F(15), ALU.add))
                V.tensor_tensor(F(15), F(13), a_re, ALU.mult)
                link(V.tensor_tensor(F(16), F(12), a_im, ALU.mult))
                link(V.tensor_tensor(F(15), F(15), F(16), ALU.subtract))
                V.tensor_tensor(F(17), F(14), F(10), ALU.mult)
                link(V.tensor_tensor(F(18), F(15), F(10), ALU.mult))
                V.tensor_copy(F(19), F(1)).then_inc(fac_ready, 1)
                f_re = F(17).unsqueeze(2).to_broadcast([P, PAIRS, GP])
                f_im = F(18).unsqueeze(2).to_broadcast([P, PAIRS, GP])
                dve.wait_ge(s_bc, 64 * (l + 1))
                V.memset(b_blk, 0.0)
                V.tensor_tensor(b_tmp[:, 0], b_raw[:, 0], f_re, ALU.mult)
                V.tensor_tensor(b_tmp[:, 1], b_raw[:, 1], f_im, ALU.mult)
                V.tensor_tensor(b_tmp[:, 2], b_raw[:, 1], f_re, ALU.mult)
                link(V.tensor_tensor(b_tmp[:, 3], b_raw[:, 0], f_im, ALU.mult))
                for g in range(2):
                    r = slice(NS * g, NS * g + NS)
                    V.tensor_tensor(b_blk[r, 0, :, g, :], b_tmp[r, 0], b_tmp[r, 1], ALU.subtract)
                    ins = V.tensor_tensor(b_blk[r, 1, :, g, :], b_tmp[r, 2], b_tmp[r, 3], ALU.add)
                ins.then_inc(blk_ready, 1)
                for g in range(2):
                    ins = V.tensor_copy(c_dup[:, :, :, g, :].rearrange("p a b c -> p (a b) c"),
                                        c_raw[:, :, :, :].rearrange("p a b c -> p (a b) c"))
                ins.then_inc(blk_ready, 1)
                link(V.memset(cT[:, :, :, :], 0.0))
                for i, n in enumerate(("c_re", "c_im")):
                    arrived(dve, (n, l))
                    src = bank((n, l))[:, :].rearrange("p (k g c) -> p k g c", g=2, c=GP)
                    for g in range(2):
                        r = slice(NS * g, NS * g + NS)
                        for m, sign in ((0, 1.0), (1, -1.0)) if i == 0 else ((2, -1.0),):
                            dst = cT[r, m, :, :].rearrange("p a b -> p (a b)") \
                                .rearrange("p (k g c) -> p k g c", g=2, c=GP)[:, :, g, :]
                            ins = V.tensor_scalar(dst, src[r, :, g, :], sign, None, ALU.mult)
                    ins.then_inc(drained["V"], 1)

            def s5_tile(l, i):
                n = l * PAIRS + i
                b, k = (i // 2) % 2, i % 2
                dve.wait_ge(trig_ready, n // 2 + 1)
                arrived(dve, ("bu", l, i))
                bu = v3(bank(("bu", l, i))[:, :], 2)
                V.tensor_tensor(rot[:, 0, :, :], bu, trig[:, b, k, 0:2, :], ALU.mult)
                ins = V.tensor_tensor(rot[:, 1, :, :], bu, trig[:, b, k, 1:3, :], ALU.mult)
                ins.then_inc(drained["V"], 1)
                wait_drained(dve, ("bu", l, i))
                V.tensor_tensor(drive[:, 0, :], rot[:, 0, 0, :], rot[:, 0, 1, :], ALU.add)
                link(V.tensor_tensor(drive[:, 1, :], rot[:, 1, 1, :], rot[:, 1, 0, :], ALU.subtract))
                decay = fac[:, 19, i:i + 1].to_broadcast([P, SEQ])
                V.tensor_tensor_scan(state[:, 0, :], decay, drive[:, 0, :], 0.0, ALU.mult, ALU.add)
                link(V.tensor_tensor_scan(state[:, 1, :], decay, drive[:, 1, :], 0.0, ALU.mult, ALU.add))
                if n >= 2:
                    dve.wait_ge(back_used, n - 1)
                V.tensor_tensor(back[:, n % 2, 0, :, :], state[:, :, :], trig[:, b, k, 0:2, :], ALU.mult)
                V.tensor_tensor(back[:, n % 2, 1, :, :], state[:, :, :], trig[:, b, k, 1:3, :],
                                ALU.mult).then_inc(tile_done, 1)

            def y_tile(l, c):
                arrived(dve, ("y", l, c))
                col = vec_col(l, "s5_d", c)
                V.scalar_tensor_tensor(out=ysT[:, c, :], in0=uT[:, c, :], scalar=vec[:, col:col + 1],
                                       in1=bank(("y", l, c))[:, 0:SEQ], op0=ALU.mult,
                                       op1=ALU.add).then_inc(drained["V"], 1)

            def conv(l, m):
                wait_drained(dve, ("qk", l, m))
                for w in range(CW):
                    for k in (2 * m, 2 * m + 1):
                        col = vec_col(l, "conv", w * QK + k)
                        src = qk_pre[:, k, w:w + SEQ]
                        if w == 0:
                            ins = V.tensor_scalar(qk[:, k, :], src, vec[:, col:col + 1], None, ALU.mult)
                        else:
                            ins = V.scalar_tensor_tensor(out=qk[:, k, :], in0=src, scalar=vec[:, col:col + 1],
                                                         in1=qk[:, k, :], op0=ALU.mult, op1=ALU.add)
                    if w < CW - 1:
                        link(ins)
                ins.then_inc(conv_ready, 1)

            def gate_sums(l):
                G = lambda i: gates[0:NH, i, :]
                link(V.tensor_scalar(G(0), G(0), b_if[:, l, 1:2], None, ALU.add))
                V.scalar_tensor_tensor(out=G(1), in0=G(0), scalar=-1.0, in1=G(0), op0=ALU.mult,
                                       op1=ALU.min).then_inc(g_in, 1)
                dve.wait_ge(g_out, l + 1)
                link(V.scalar_tensor_tensor(out=G(4), in0=G(0), scalar=0.0, in1=G(3), op0=ALU.min,
                                            op1=ALU.subtract))
                link(V.tensor_tensor_scan(G(5), ones[0:NH, 0:1].to_broadcast([NH, SEQ]), G(4), 0.0,
                                          ALU.mult, ALU.add))
                link(V.scalar_tensor_tensor(out=G(6), in0=G(9), scalar=b_if[:, l, 0:1], in1=G(5), op0=ALU.add,
                                            op1=ALU.subtract))
                link(V.tensor_tensor_scan(G(2), G(6), G(6), 0.0, ALU.max, ALU.max))
                V.scalar_tensor_tensor(out=G(7), in0=G(5), scalar=-1.0, in1=G(2), op0=ALU.mult,
                                       op1=ALU.subtract).then_inc(g_in, 1)

            def head(l, h):
                arrived(dve, ("mu", l, h))
                mu = bank(("mu", l, h))
                if h >= 2:
                    arrived(dve, ("num", l, h - 2))
                a0, a1 = small[:, 32 + h:33 + h], small[:, 32 + NH + h:33 + NH + h]
                if h == 0:
                    wait_drained(dve, ("tr", l))
                V.scalar_tensor_tensor(out=dec[:, h % 2, 0:SEQ], in0=mu[:, 0:SEQ], scalar=a0, in1=cmask[:, :],
                                       op0=ALU.add, op1=ALU.min)
                V.scalar_tensor_tensor(out=dec[:, h % 2, SEQ:], in0=mu[:, P:SEQ], scalar=a1, in1=cmask[:, 0:P],
                                       op0=ALU.add, op1=ALU.min).then_inc(drained["V"], 1)
                arrived(dve, ("sc", l, h))
                dve.wait_ge(dec_ready, NH * l + h + 1)
                V.scalar_tensor_tensor(out=scr[:, h % 2, :], in0=bank(("sc", l, h))[:, 0:SEQ + P], scalar=DH ** -0.5,
                                       in1=dec[:, h % 2, :], op0=ALU.mult, op1=ALU.mult).then_inc(drained["V"], 1)

            def head_out(l, h):
                arrived(dve, ("num", l, h))
                num = v3(bank(("num", l, h))[:, :], 2)
                e = small[:, 32 + 2 * NH:32 + 4 * NH].rearrange("p (t h) -> p t h", t=NT)[:, :, h:h + 1]
                d = small[:, 48 + 2 * h:50 + 2 * h].unsqueeze(2)
                link(V.scalar_tensor_tensor(out=d, in0=num[:, :, DH:DH + 1], scalar=-1.0, in1=e, op0=ALU.mult,
                                            op1=ALU.max))
                link(V.scalar_tensor_tensor(out=d, in0=num[:, :, DH:DH + 1], scalar=1.0, in1=d, op0=ALU.mult,
                                            op1=ALU.max))
                link(V.reciprocal(d, d))
                for t in range(NT):
                    ins = V.tensor_scalar(hm[:, t, h, :], num[:, t, 0:DH], small[:, 48 + 2 * h + t:49 + 2 * h + t],
                                          None, ALU.mult)
                ins.then_inc(drained["V"], 1)
                wait_drained(dve, ("num", l, h))
                for t in range(NT):
                    ins = V.tensor_tensor_reduce(out=rot[:, 0, 0, t * P:(t + 1) * P], in0=hm[:, t, h, :],
                                                 in1=hm[:, t, h, :], scale=1.0, scalar=0.0, op0=ALU.mult,
                                                 op1=ALU.add, accum_out=small[:, 16 + t * NH + h:17 + t * NH + h])
                return ins

            dve.wait_ge(s_par, 16 * (2 * len(VEC_ROWS) + 5))
            V.tensor_copy(s5_rows[64:96, :].rearrange("p (h s) -> p h s", h=2),
                          dt_rows[64:96, :].unsqueeze(2).to_broadcast([32, 2, NS])).then_inc(dt_wide, 1)
            arrived(dve, ("vec",))
            V.tensor_copy(vec[:, :], bank(("vec",))[:, 0:DEPTH * VEC_PER]).then_inc(drained["V"], 1)
            arrived(dve, ("s5p",))
            V.tensor_copy(s5p[:, :, :, :].rearrange("p a l g -> p (a l g)"),
                          bank(("s5p",))[:, 0:3 * DEPTH * PAIRS]).then_inc(drained["V"], 1)
            wait_drained(dve, ("s5p",))
            V.memset(qk_pre[:, :, 0:CW - 1], 0.0)
            link(V.memset(v_aug[:, :, :, DH:DH + 1], 1.0))
            dve.wait_ge(consts, 1)
            prep(0)
            dve.wait_ge(s_x, 16)
            for l in range(DEPTH):
                norm(4 * l + 1)
                xT(l, 0)
                for i in range(PAIRS):
                    s5_tile(l, i)
                    if i % PPC == PPC - 1 and i // PPC:
                        y_tile(l, i // PPC - 1)
                    if i == 3:
                        arrived(dve, ("if", l))
                        gb = bank(("if", l))
                        V.tensor_copy(hm[0:NH, 0, :, :].rearrange("p a b -> p (a b)"),
                                      gb[0:NH, :]).then_inc(drained["V"], 1)
                    if i in (4, 6, 8, 10):
                        conv(l, (i - 4) // 2)
                y_tile(l, CT - 1)
                for c in range(CT):
                    dve.wait_ge(y_in, CT * l + c + 1)
                    link(V.tensor_scalar(gT[:, c, :], gT[:, c, :], GELU_A, 1.0, ALU.mult, ALU.add))
                    V.tensor_tensor(gT[:, c, :], gT[:, c, :], ysT[:, c, :], ALU.mult).then_inc(y_tanh, 1)
                    dve.wait_ge(y_ready, CT * l + c + 1)
                    V.scalar_tensor_tensor(out=gT[:, c, :], in0=gT[:, c, :], scalar=1.0, in1=ysT[:, c, :],
                                           op0=ALU.add, op1=ALU.mult).then_inc(glu_ready, 1)
                dve.wait_ge(back_used, PAIRS * (l + 1))
                wait_drained(dve, ("if", l))
                kept = v3(hm[0:NH, 0, :, :].rearrange("p a b -> p (a b)"), 2)
                V.tensor_copy(gates[0:NH, 9, :], kept[:, 0, :])
                link(V.tensor_copy(gates[0:NH, 0, :], kept[:, 1, :]))
                gate_sums(l)
                for t in range(NT):
                    wait_drained(dve, ("o", l, t))
                    link(V.tensor_scalar(o_gate[:, t, :], o_gate[:, t, :], 0.5, 0.5, ALU.mult, ALU.add))
                for i in range(2):
                    wait_drained(dve, ("z", l, i))
                    V.scalar_tensor_tensor(out=ysT[:, 2 * i:2 * i + 2, :].rearrange("p a b -> p (a b)"),
                                           in0=ysT[:, 2 * i:2 * i + 2, :].rearrange("p a b -> p (a b)"), scalar=1.0,
                                           in1=gT[:, 2 * i:2 * i + 2, :].rearrange("p a b -> p (a b)"),
                                           op0=ALU.add, op1=ALU.mult).then_inc(dve_chain, 1)
                    chain[0] += 1
                dve.wait_ge(dve_chain, chain[0])
                V.tensor_tensor(gT[:, :, :].rearrange("p a b -> p (a b)"), ysT[:, :, :].rearrange("p a b -> p (a b)"),
                                ysT[:, :, :].rearrange("p a b -> p (a b)"), ALU.mult)
                for c in range(CT):
                    col = vec_col(l, "norm_s5", c)
                    ins = V.tensor_scalar(mixT[:, CT + c, :], ysT[:, c, :], vec[:, col:col + 1], None, ALU.mult)
                ins.then_inc(mixed_s5, 1)
                for h in range(NH):
                    head(l, h)
                    if h:
                        head_out(l, h - 1)
                ins = head_out(l, NH - 1)
                link(ins)
                arrived(dve, ("ss", l))
                V.tensor_scalar(small[:, 8:8 + NT], bank(("ss", l))[:, 0:NT], 1.0 / DS5, 16.0 * EPS, ALU.mult,
                                ALU.add).then_inc(drained["V"], 1)
                V.tensor_scalar(small[:, 16:16 + NT * NH], small[:, 16:16 + NT * NH], 1.0 / DH, EPS, ALU.mult,
                                ALU.add).then_inc(ms_ready, 1)
                dve.wait_ge(rs_ready, 4 * l + 3)
                for t in range(NT):
                    for h in range(NH):
                        c = 16 + t * NH + h
                        ins = V.scalar_tensor_tensor(out=hm[:, t, h, :], in0=hm[:, t, h, :], scalar=small[:, c:c + 1],
                                                     in1=o_gate[:, t, h * DH:(h + 1) * DH], op0=ALU.mult, op1=ALU.mult)
                ins.then_inc(hm_ready, 1)
                for t in range(NT):
                    for c in range(2):
                        arrived(dve, ("os", l, t, c))
                        xs = x_res[:, t, 512 * c:512 * c + 512]
                        V.scalar_tensor_tensor(out=xs, in0=bank(("os", l, t, c))[:, :], scalar=small[:, 8 + t:9 + t],
                                               in1=xs, op0=ALU.mult, op1=ALU.add).then_inc(drained["V"], 1)
                for t in range(NT):
                    for c in range(2):
                        arrived(dve, ("oh", l, t, c))
                        xs = x_res[:, t, 512 * c:512 * c + 512]
                        wait_drained(dve, ("os", l, t, c))
                        V.tensor_tensor(xs, bank(("oh", l, t, c))[:, :], xs, ALU.add).then_inc(drained["V"], 1)
                wait_drained(dve, ("oh", l, NT - 1, 1))
                if l == 0:
                    prep(1)
                norm(4 * l + 4)
                xT(l, 1)
                if l == 0:
                    for f in range(FT):
                        dve.wait_ge(ffn_silu, f + 1)
                        if f >= 3:
                            arrived(dve, ("gu", f - 1))
                        V.tensor_tensor(f_hid[:, f % 3, :], f_silu[:, f % 2, :], bank(("gu", f))[:, SEQ:2 * SEQ],
                                        ALU.mult).then_inc(drained["V"], 1)
                    for t in range(NT):
                        for c in range(2):
                            arrived(dve, ("ffn", t, c))
                            xs = x_res[:, t, 512 * c:512 * c + 512]
                            V.tensor_tensor(xs, bank(("ffn", t, c))[:, :], xs, ALU.add).then_inc(drained["V"], 1)
                    wait_drained(dve, ("ffn", NT - 1, 1))

            R = lambda i: rt[:, i, :, :]
            R1 = lambda i: rt[:, i, :, 0:1]
            wide = lambda i: rt[:, i, :, 0:1].to_broadcast([P, NT, NE])
            row = lambda ap: ap.unsqueeze(1).to_broadcast([P, NT, NE])
            for e in range(NE):
                ins = V.memset(desc[:, e:e + 1], float(NE - e))
            link(ins)
            dve.wait_ge(s_rt_in, 32)
            arrived(dve, ("router",))
            V.tensor_tensor(R(0), bank(("router",))[:, 0:NT * NE].rearrange("p (t e) -> p t e", t=NT), row(b_rt[:, :]),
                            ALU.add).then_inc(drained["V"], 1)
            wait_drained(dve, ("router",))

            def first_max(src, top, hot):
                link(V.tensor_reduce(R1(top), R(src), AX, ALU.max))
                link(V.tensor_tensor(R(hot), R(src), wide(top), ALU.is_equal))
                link(V.tensor_tensor(R(hot), R(hot), row(desc), ALU.mult))
                link(V.tensor_reduce(R1(23), R(hot), AX, ALU.max))
                link(V.tensor_tensor(R(hot), R(hot), wide(23), ALU.is_equal))

            first_max(0, 1, 2)
            link(V.scalar_tensor_tensor(out=rt[:, 3, :, :], in0=R(2), scalar=-PICK, in1=R(0), op0=ALU.mult,
                                        op1=ALU.add))
            first_max(3, 4, 5)
            V.tensor_tensor(R1(7), R1(4), R1(1), ALU.subtract).then_inc(route_in, 1)
            V.tensor_tensor(R(6), R(2), R(5), ALU.add).then_inc(route_mask, 1)
            dve.wait_ge(route_exp, 1)
            link(V.tensor_scalar(R1(9), R1(8), 1.0, None, ALU.add))
            link(V.reciprocal(R1(9), R1(9)))
            link(V.tensor_tensor(R1(10), R1(9), R1(8), ALU.mult))
            V.tensor_tensor(R(11), R(2), wide(9), ALU.mult)
            link(V.tensor_tensor(R(12), R(5), wide(10), ALU.mult))
            link(V.tensor_tensor(R(11), R(11), R(12), ALU.add))
            arrived(dve, ("pos",))
            pos = bank(("pos",))
            link(V.scalar_tensor_tensor(out=rt[:, 13, :, :].rearrange("p t e -> p (t e)"), in0=pos[:, 0:NT * NE], scalar=1.0,
                                        in1=rt[:, 6, :, :].rearrange("p t e -> p (t e)"), op0=ALU.add, op1=ALU.mult))
            V.tensor_scalar(R(13), R(13), 1.0, None, ALU.subtract)
            O = lambda i: over[:, i, :]
            link(V.tensor_scalar(O(0), pos[:, NT * NE:NT * NE + NE], float(P), None, ALU.is_gt))
            link(V.tensor_tensor_scan(O(1), ones[:, 0:NE], O(0), 0.0, ALU.mult, ALU.add))
            link(V.tensor_scalar(O(7), desc, -1.0, float(NE), ALU.mult, ALU.add))
            V.tensor_copy(posI[:, :, 0:NE], R(13))
            V.memset(posI[:, :, NE:], -1.0)
            V.memset(gateI[:, :, NE:], 0.0)
            V.tensor_copy(gateI[:, :, 0:NE], R(11))
            link(V.tensor_copy(n_list[:, 0:1], O(1)[:, NE - 1:NE]))
            for k in range(3):
                link(V.tensor_scalar(O(2), O(1), float(k + 1), None, ALU.is_equal))
                link(V.tensor_tensor(O(2), O(2), O(0), ALU.mult))
                link(V.tensor_tensor(O(3), O(2), O(7), ALU.mult))
                link(V.tensor_reduce(O(4)[:, 0:1], O(3), AX, ALU.add))
                link(V.tensor_copy(n_list[:, k + 1:k + 2], O(4)[:, 0:1]))
                link(V.tensor_tensor(R(14), R(13), row(O(2)), ALU.mult))
                link(V.tensor_reduce(R1(15), R(14), AX, ALU.add))
                link(V.tensor_scalar(posI[:, :, NE + k:NE + k + 1], R1(15), float(P), None, ALU.subtract))
                link(V.tensor_tensor(R(14), R(11), row(O(2)), ALU.mult))
                ins = V.tensor_reduce(gateI[:, :, NE + k:NE + k + 1], R(14), AX, ALU.add)
                if k < 2:
                    link(ins)
            ins.then_inc(items_ready, 1)
            dve.wait_ge(items_ready, 1)

            def choose(nxt):
                for t in range(NT):
                    p = posI[:, t, nxt]
                    g = gateI[:, t, nxt]
                    V.tensor_scalar(pick[:, t, :], times[:, 0:P], p, None, ALU.is_equal)
                    ins = V.tensor_scalar(pickg[:, t, :], times[:, 0:P], p, g, ALU.is_equal, ALU.mult)
                ins.then_inc(v_pick, 1)

            gcol = vec_col(1, "norm_ffn")

            def take_tokens(it):
                for half, b in ((0, 5), (1, 2)):
                    dve.wait_ge(e_gather, it * 2 + (half + 1))
                    k = slice(4 * half, 4 * half + 4)
                    w = vec[:, gcol + 4 * half:gcol + 4 * half + 4].unsqueeze(2).to_broadcast([P, 4, P])
                    V.tensor_tensor(xe[:, k, :], v3(ps[b][:, :], 4), w, ALU.mult).then_inc(xe_steps, 1)
                    dve.wait_ge(xe_steps, it * 4 + (2 * half + 1))
                    V.tensor_copy(xe_hi[:, k, :], xe[:, k, :]).then_inc(xe_steps, 1)
                    dve.wait_ge(xe_steps, it * 4 + (2 * half + 2))
                    V.tensor_tensor(xe_lo[:, k, :], xe[:, k, :], xe_hi[:, k, :].bitcast(F32),
                                    ALU.subtract).then_inc(v_xe, 1)

            def add_out(it):
                for t in range(NT):
                    for c in range(2):
                        n = 2 * t + c
                        dve.wait_ge(e_sc, it * 4 + (n - 3))
                        xs = x_res[:, t, 512 * c:512 * c + 512]
                        V.tensor_tensor(xs, ps[SCATTER[n]][:, :], xs, ALU.add).then_inc(v_add, 1)

            def hidden(it, j):
                part_used(dve, it, "u", j)
                dve.wait_ge(a_silu, it * NJ + (j + 1))
                V.tensor_tensor(e_hid[:, 2 if j == NJ - 1 else j % 2, :], e_silu[:, j % 2, :],
                                ps[2 * (j % 2) + 1][:, :], ALU.mult).then_inc(v_hid, 1)

            def hidden_low(it, j):
                dve.wait_ge(a_hT, it * NJ + (j + 1))
                V.tensor_tensor(hidT_lo[:, :, :], v3(ps[4][:, :], 4), hidT_hi[:, :, :].bitcast(F32),
                                ALU.subtract).then_inc(v_hT, 1)

            def item(it, first=False):
                for q in range(SPLITS):
                    if q == after_part(part_no("d", NJ - 2, 3)) - SPLITS:
                        if not first:
                            hidden_low(it - 1, NJ - 1)
                        take_tokens(it)
                    for j in range(NJ):
                        if q == after_part(part_no("u", j, 3)):
                            hidden(it, j)
                        if j and q == after_part(part_no("u", j, 0)):
                            hidden_low(it, j - 1)
                    if q == after_part(part_no("g", 1, 3)) + 1 and not first:
                        add_out(it)
                    if q == after_part(part_no("u", 2, 3)) + 2:
                        dve.wait_ge(e_pt, it + 1)
                        choose(bass.ds(it + 1, 1))
                    dve.wait_ge(hi_ready, it * SPLITS + (q + 1))
                    V.tensor_tensor(w_lo[:, q % SPLIT, :], raw_part(q), w_hi[:, q % SPLIT, :].bitcast(F32),
                                    ALU.subtract).then_inc(lo_ready, 1)

            choose(slice(0, 1))
            item(0, first=True)
            with dve.Fori(1, NE) as e:
                item(e)
            n_over = dve.value_load(n_list[0:1, 0:1], min_val=0, max_val=3)
            with dve.If(n_over > 0):
                with dve.Fori(0, n_over) as k:
                    item(k + NE)
            hidden_low(n_over + (NE - 1), NJ - 1)
            add_out(n_over + NE)
            dve.wait_ge(v_add, (n_over + NE) * 4)
            norm(4 * DEPTH + 1)
            dve.wait_ge(s_gfin, 16)
            for t in range(NT):
                V.scalar_tensor_tensor(out=hn[:, t, :], in0=x_res[:, t, :], scalar=small[:, t:t + 1], in1=gfin,
                                       op0=ALU.mult, op1=ALU.mult).then_inc(fin_ready, 1)

        @block.tensor
        def _(pe):
            M = nc.tensor.matmul

            def done(ins):
                ins.then_inc(product_ready, 1)

            def prep(l):
                pe.wait_ge(blk_ready, 2 * l + 1)
                for i, n in enumerate(("b_re", "b_im")):
                    open_bank(pe, (n, l))
                    for c in range(CT):
                        ins = nc.tensor.transpose(bank((n, l))[:, c * P:(c + 1) * P],
                                                  b_blk[:, i, PPC * c:PPC * c + PPC, :, :]
                                                  .rearrange("p a b c -> p (a b c)"), ident[:, :])
                    done(ins)
                pe.wait_ge(blk_ready, 2 * l + 2)
                for i, n in enumerate(("c_re", "c_im")):
                    open_bank(pe, (n, l))
                    for c in range(CT):
                        ins = nc.tensor.transpose(bank((n, l))[:, c * P:(c + 1) * P],
                                                  c_dup[:, i, c, :, :].rearrange("p a b -> p (a b)"), ident[:, :])
                    done(ins)

            def norm(l, what):
                pe.wait_ge(hn_ready, (2 * l + what + 1) * NT)
                for j in range(4):
                    n = ("xT", l, what, j)
                    open_bank(pe, n)
                    for k in range(2):
                        for t in range(NT):
                            a = (2 * j + k) * P
                            ins = nc.tensor.transpose(bank(n)[:, k * SEQ + t * P:k * SEQ + (t + 1) * P],
                                                      hn[:, t, a:a + P], ident[:, :])
                    done(ins)

            def have_hnT(l, what):
                for j in range(4):
                    wait_drained(pe, ("xT", l, what, j))

            def channels(name, w, cols, last_of=None):
                open_bank(pe, name)
                for i, a in enumerate(cols):
                    for k in range(KT):
                        ins = M(bank(name)[:, i * SEQ:(i + 1) * SEQ], w[:, k, a:a + P], hnT[:, k, :],
                                start=(k == 0), stop=(k == KT - 1))
                return ins

            def mixer(l):
                have_hnT(l, 0)
                chunk_wait(pe, ("u", l))
                for i in range(2):
                    ins = channels(("u", l, i), v3(chunk(("u", l)), KT), (2 * i * P, 2 * i * P + P))
                    done(ins)

                def bu(i):
                    n = ("bu", l, i)
                    open_bank(pe, n)
                    c, j = divmod(i, PPC)
                    r = slice(32 * j, 32 * j + 32)
                    for m in range(2):
                        ins = M(bank(n)[:, m * SEQ:(m + 1) * SEQ], bT[r, m, c, :], uT[r, c, :], start=True, stop=True)
                    done(ins)

                wait_drained(pe, ("u", l, 1))
                wait_drained(pe, ("b_im", l))
                for i in range(4):
                    bu(i)
                for i in range(PAIRS):
                    for n in mixer_steps(l).get(i, []):
                        if n[0] == "if":
                            pe.wait_ge(s_wif, 16 * (l + 1))
                            open_bank(pe, n)
                            for m in range(2):
                                for k in range(KT):
                                    ins = M(bank(n)[0:NH, m * SEQ:(m + 1) * SEQ], w_if[:, k, m * NH:(m + 1) * NH],
                                            hnT[:, k, :], start=(k == 0), stop=(k == KT - 1))
                            done(ins)
                        elif n[0] == "qk":
                            c = ("q" if n[2] < 2 else "k", l)
                            chunk_wait(pe, c)
                            a = (n[2] % 2) * 2 * P
                            done(channels(n, v3(chunk(c), KT), (a, a + P)))
                        else:
                            chunk_wait(pe, (n[0], l))
                            open_bank(pe, n)
                            for k in range(KT):
                                ins = M(bank(n)[:, :], hnT[:, k, n[2] * P:(n[2] + 1) * P],
                                        v3(chunk((n[0], l)), KT)[:, k, :], start=(k == 0), stop=(k == KT - 1))
                            done(ins)
                    if i + 4 < PAIRS:
                        bu(i + 4)
                    n = l * PAIRS + i
                    c, j = divmod(i, PPC)
                    if j == 0:
                        open_bank(pe, ("y", l, c))
                    if i == 0:
                        wait_drained(pe, ("c_im", l))
                    pe.wait_ge(tile_done, n + 1)
                    r = slice(32 * j, 32 * j + 32)
                    for q, (m, a, b) in enumerate(((0, 0, 0), (1, 0, 1), (2, 1, 0), (2, 1, 1))):
                        ins = M(bank(("y", l, c))[r, 0:SEQ], cT[:, m, c, 32 * j:32 * j + 32], back[:, n % 2, a, b, :],
                                start=(q == 0), stop=(q == 3))
                    ins.then_inc(back_used, 1)
                pe.wait_ge(gate_rows, l + 1)
                open_bank(pe, ("tr", l))
                for m, src in enumerate((6, 8)):
                    for t in range(NT):
                        a = (2 * m + t) * NH
                        ins = nc.tensor.transpose(bank(("tr", l))[:, a:a + NH],
                                                  gates[0:NH, src, t * P:(t + 1) * P], ident[0:NH, 0:NH])
                done(ins)
                chunk_wait(pe, ("glu", l))
                pe.wait_ge(glu_ready, CT * (l + 1))
                w = v3(chunk(("glu", l))[:, 0:DS5 * CT], CT)
                for i in range(2):
                    n = ("z", l, i)
                    open_bank(pe, n)
                    for m in range(2):
                        a = (2 * i + m) * P
                        for k in range(CT):
                            ins = M(bank(n)[:, m * SEQ:(m + 1) * SEQ], w[:, k, a:a + P], gT[:, k, :],
                                    start=(k == 0), stop=(k == CT - 1))
                    done(ins)

                def numerator(h):
                    n = ("num", l, h)
                    open_bank(pe, n)
                    wait_drained(pe, ("sc", l, h))
                    num = v3(bank(n)[:, :], 2)
                    s = scr[:, h % 2, :]
                    M(num[:, 0, 0:DH + 1], s[:, 0:P], v_aug[:, 0, h, :], start=True, stop=True)
                    M(num[:, 1, 0:DH + 1], s[:, P:SEQ], v_aug[:, 0, h, :], start=True, stop=False)
                    done(M(num[:, 1, 0:DH + 1], s[:, SEQ:], v_aug[:, 1, h, :], start=False, stop=True))

                pe.wait_ge(qk_ready, 4 * (l + 1))
                for h in range(NH):
                    n = ("mu", l, h)
                    open_bank(pe, n)
                    done(M(bank(n)[:, 0:SEQ], head_pick[:, h, :], gates[0:NH, 2, :], start=True, stop=True))
                    n = ("sc", l, h)
                    open_bank(pe, n)
                    M(bank(n)[:, 0:SEQ], qk[:, NH + h, 0:P], qk[:, h, :], start=True, stop=True)
                    done(M(bank(n)[:, SEQ:SEQ + P], qk[:, NH + h, P:SEQ], qk[:, h, P:SEQ], start=True, stop=True))
                    if h:
                        numerator(h - 1)
                numerator(NH - 1)
                pe.wait_ge(mixed_s5, l + 1)
                n = ("ss", l)
                open_bank(pe, n)
                for t in range(NT):
                    for c in range(CT):
                        ins = M(bank(n)[:, t:t + 1], gT[:, c, t * P:(t + 1) * P], ones[:, 0:1],
                                start=(c == 0), stop=(c == CT - 1))
                done(ins)
                for part, k0 in (("os", CT), ("oh", 0)):
                    if part == "oh":
                        pe.wait_ge(hm_ready, l + 1)
                        for i in range(2):
                            n = ("hmT", l, i)
                            open_bank(pe, n)
                            for k in range(2):
                                for t in range(NT):
                                    ins = nc.tensor.transpose(bank(n)[:, k * SEQ + t * P:k * SEQ + (t + 1) * P],
                                                              hm[:, t, 2 * i + k, :], ident[:, :])
                            done(ins)
                        for i in range(2):
                            wait_drained(pe, ("hmT", l, i))
                    for t in range(NT):
                        for c in range(2):
                            n = (part, l, t, c)
                            chunk_wait(pe, ("out", l, c))
                            open_bank(pe, n)
                            for k in range(4):
                                ins = M(bank(n)[:, :], mixT[:, k0 + k, t * P:(t + 1) * P],
                                        v3(chunk(("out", l, c)), KT)[:, k0 + k, :], start=(k == 0), stop=(k == 3))
                            done(ins)

            pe.wait_ge(consts, 1)
            pe.wait_ge(s_par, 16 * (2 * len(VEC_ROWS) + 5))
            done(nc.tensor.transpose(bank(("vec",))[:, 0:DEPTH * VEC_PER], vec_rows[0:DEPTH * VEC_PER, :],
                                     ident[0:DEPTH * VEC_PER, 0:DEPTH * VEC_PER]))
            pe.wait_ge(dt_wide, 1)
            done(nc.tensor.transpose(bank(("s5p",))[:, 0:96], s5_rows[0:96, :], ident[0:96, 0:96]))
            prep(0)
            for l in range(DEPTH):
                norm(l, 0)
                mixer(l)
                if l == 0:
                    prep(1)
                norm(l, 1)
                have_hnT(l, 1)
                if l == 0:
                    def down(f):
                        j, i = divmod(f, GW // P)
                        chunk_wait(pe, ("fd", j))
                        n = min(GW, FD - j * GW) // P
                        w = v3(chunk(("fd", j))[:, 0:n * DM], n)
                        wait_drained(pe, ("gu", f))
                        for t in range(NT):
                            for c in range(2):
                                if f == 0:
                                    open_bank(pe, ("ffn", t, c))
                                ins = M(bank(("ffn", t, c))[:, :], f_hid[:, f % 3, t * P:(t + 1) * P],
                                        w[:, i, 512 * c:512 * c + 512], start=(f == 0), stop=(f == FT - 1))
                                if f == FT - 1:
                                    done(ins)
                        if i == n - 1 and f < FT - 1:
                            ins.then_inc(ffn_down, 1)

                    for f in range(FT):
                        j, i = divmod(f, GW // P)
                        width = min(GW, FD - j * GW)
                        n = ("gu", f)
                        open_bank(pe, n)
                        for m, c in enumerate(("fg", "fu")):
                            chunk_wait(pe, (c, j))
                            w = v3(chunk((c, j))[:, 0:KT * width], KT)
                            for k in range(KT):
                                ins = M(bank(n)[:, m * SEQ:(m + 1) * SEQ], w[:, k, i * P:(i + 1) * P], hnT[:, k, :],
                                        start=(k == 0), stop=(k == KT - 1))
                        done(ins)
                        if f:
                            down(f - 1)
                    down(FT - 1)

            pe.wait_ge(s_rt_in, 32)
            open_bank(pe, ("router",))
            for t in range(NT):
                for k in range(KT):
                    ins = M(bank(("router",))[:, t * NE:(t + 1) * NE], hnT[:, k, t * P:(t + 1) * P], w_rt[:, k, :],
                            start=(k == 0), stop=(k == KT - 1))
            done(ins)
            pe.wait_ge(route_mask, 1)
            open_bank(pe, ("pos",))
            b = bank(("pos",))
            M(b[:, 0:NE], lower[:, :], rt[:, 6, 0, :], start=True, stop=True)
            M(b[:, NE:2 * NE], ones[:, :], rt[:, 6, 0, :], start=True, stop=False)
            M(b[:, NE:2 * NE], lower[:, :], rt[:, 6, 1, :], start=False, stop=True)
            M(b[:, 2 * NE:3 * NE], ones[:, :], rt[:, 6, 0, :], start=True, stop=False)
            done(M(b[:, 2 * NE:3 * NE], ones[:, :], rt[:, 6, 1, :], start=False, stop=True))

            def gather(it):
                pe.wait_ge(v_pick, it + 1)
                for half, b in ((0, 5), (1, 2)):
                    for k in range(4):
                        a = (4 * half + k) * P
                        for t in range(NT):
                            ins = M(ps[b][:, k * P:(k + 1) * P], hn[:, t, a:a + P], pick[:, t, :],
                                    start=(t == 0), stop=(t == NT - 1))
                    ins.then_inc(e_gather, 1)

            def swiglu(it, kind, j, b):
                for z in range(4):
                    q = part_no(kind, j, z)
                    pe.wait_ge(lo_ready, it * SPLITS + (q + 1))
                    hi, lo = v3(w_hi[:, q % SPLIT, :], 2), v3(w_lo[:, q % SPLIT, :], 2)
                    if j == 0 and kind == "g" and z % 2 == 0:
                        pe.wait_ge(v_xe, it * 2 + (z // 2 + 1))
                    for i in range(2):
                        k = 2 * z + i
                        M(ps[b][:, :], xe_hi[:, k, :], hi[:, i, :], start=(k == 0), stop=False)
                        M(ps[b][:, :], xe_lo[:, k, :], hi[:, i, :], start=False, stop=False)
                        ins = M(ps[b][:, :], xe_hi[:, k, :], lo[:, i, :], start=False, stop=(k == KT - 1))
                    ins.then_inc(split_used, 1)

            def transpose_hidden(it, j):
                pe.wait_ge(v_hid, it * NJ + (j + 1))
                for i in range(GW // P):
                    ins = nc.tensor.transpose(ps[4][:, i * P:(i + 1) * P],
                                              e_hid[:, 2 if j == NJ - 1 else j % 2, i * P:(i + 1) * P], ident[:, :])
                ins.then_inc(e_tr, 1)

            def down(it, j):
                pe.wait_ge(v_hT, it * NJ + (j + 1))
                for z in range(4):
                    q = part_no("d", j, z)
                    pe.wait_ge(lo_ready, it * SPLITS + (q + 1))
                    for n in range(2):
                        y = ps[6 + n][:, :]
                        cols = slice(512 * n, 512 * n + 512)
                        M(y, hidT_hi[:, z, :], w_hi[:, q % SPLIT, cols], start=(j == 0 and z == 0), stop=False)
                        M(y, hidT_lo[:, z, :], w_hi[:, q % SPLIT, cols], start=False, stop=False)
                        ins = M(y, hidT_hi[:, z, :], w_lo[:, q % SPLIT, cols], start=False,
                                stop=(j == NJ - 1 and z == 3))
                    ins.then_inc(split_used, 1)

            def scatter(it):
                pe.wait_ge(a_ye, it)
                pe.wait_ge(a_pt, it)
                for t in range(NT):
                    for c in range(2):
                        M(ps[SCATTER[2 * t + c]][:, :], pickT[:, t, :], ye[:, 512 * c:512 * c + 512], start=True,
                          stop=True).then_inc(e_sc, 1)

            def item(it, first=False):
                for j in range(NJ):
                    b = 2 * (j % 2)
                    if j == 2 and not first:
                        pe.wait_ge(v_add, it * 4)
                    swiglu(it, "g", j, b)
                    if j:
                        transpose_hidden(it, j - 1)
                    if j == 1 and not first:
                        scatter(it)
                    swiglu(it, "u", j, b + 1)
                    if j == 1:
                        for t in range(NT):
                            ins = nc.tensor.transpose(ps[5][:, t * P:(t + 1) * P], pickg[:, t, :], ident[:, :])
                        ins.then_inc(e_pt, 1)
                    if j:
                        if j == 1 and not first:
                            pe.wait_ge(v_add, it * 4)
                        down(it, j - 1)
                transpose_hidden(it, NJ - 1)
                pe.wait_ge(a_pt, it + 1)
                gather(it + 1)
                down(it, NJ - 1)

            gather(0)
            item(0, first=True)
            with pe.Fori(1, NE) as e:
                item(e)
            pe.wait_ge(items_ready, 1)
            n_over = pe.value_load(n_list[0:1, 0:1], min_val=0, max_val=3)
            with pe.If(n_over > 0):
                with pe.Fori(0, n_over) as k:
                    item(k + NE)
            n = n_over + NE
            scatter(n)


_INS = ['x', 'norm_mix', 'w_in', 'conv_qk', 'b_igate', 'b_fgate', 'norm_mlstm', 's5_a_re', 's5_a_im', 's5_log_dt',
        's5_b_re', 's5_b_im', 's5_c_re', 's5_c_im', 's5_d', 'w_glu', 'norm_s5', 'w_out', 'norm_ffn', 'ffn_w_gate',
        'ffn_w_up', 'ffn_w_down', 'moe_w_router', 'moe_b_router', 'moe_w_gate', 'moe_w_up', 'moe_w_down',
        'norm_final']
_OUTS = [((1, SEQ, DM), 'float32')]


def kernel(**inputs):
    import numpy as _np
    import concourse.bacc as _bacc
    from concourse import mybir as _mybir
    from concourse.bass_utils import run_bass_kernel_spmd as _run

    nc = _bacc.Bacc("TRN2", target_bir_lowering=False, num_devices=1)
    arrays, args = {}, []
    for name in _INS:
        a = _np.ascontiguousarray(inputs[name])
        arrays[f"in_{name}_dram"] = a
        args.append(nc.dram_tensor(f"in_{name}_dram", a.shape, _mybir.dt.from_np(a.dtype), kind="ExternalInput").ap())
    for i, (shape, dtype) in enumerate(_OUTS):
        dt = _mybir.dt.from_np(_np.dtype(dtype))
        args.append(nc.dram_tensor(f"out_{i}_dram", shape, dt, kind="ExternalOutput").ap())
    trunk_kernel(nc, *args)
    r = _run(nc, [arrays], core_ids=[0])
    got = tuple(r.results[0][f"out_{i}_dram"] for i in range(len(_OUTS)))
    return got[0]
```

```python
from contextlib import ExitStack
import math

import numpy as np
import concourse.bass as bass
from concourse import mybir

F32 = mybir.dt.float32
F32R = mybir.dt.float32r
I32 = mybir.dt.int32
ALU = mybir.AluOpType
ACT = mybir.ActivationFunctionType
AX = mybir.AxisListType.X

P = 128
SEQ, DM = 256, 1024
NT = SEQ // P
KT = DM // P
DEPTH = 2
DH = 128
NH = 4
DML = NH * DH
DS5 = DM - DML
CW = 4
GP = 16
NS = 64
NG = DS5 // GP
CT = DS5 // P
PAIRS = NG // 2
PPC = PAIRS // CT
FD = 2816
FT = FD // P
NE = 8
FE = 3584
GW = 512
NJ = FE // GW
EPS = 1e-6
IF0 = 4 * DML
U0 = IF0 + 2 * NH
F_ROW = 32
QK = 2 * DML // P

CHUNK = 8 * 512
RING = 5
HALF = CHUNK // 2
MRING = 7
PART = HALF // 2
FIRST = 7
SPLIT = 7
PER_ITEM = 6 * NJ
SPLITS = 2 * PER_ITEM


def item_halves():
    order = []
    for j in range(NJ):
        kinds = [("g", j), ("u", j)] + ([("d", j - 1)] if j else [])
        order += [(k, i, h) for k, i in kinds for h in range(2)]
    return order + [("d", NJ - 1, h) for h in range(2)]


SCATTER = (0, 1, 6, 7)


def part_no(kind, j, z=0):
    return 2 * item_halves().index((kind, j, z // 2)) + z % 2


def ffn_parts():
    order = []
    for f in range(FT):
        order += [("fg", f), ("fu", f)] + ([("fd", f - 1)] if f else [])
    return order + [("fd", FT - 1)]


def after_part(n):
    return n + 1 + SPLIT



TWO_PI = 2.0 * math.pi
PI_A = 6.28125
PI_B = float(np.float32(np.round((TWO_PI - PI_A) * 2.0**21) / 2.0**21))
PI_C = TWO_PI - PI_A - PI_B
ROUND_INT = 1.5 * 2.0**23
ROUND_12 = 1.5 * 2.0**11
SIN_SCALE = 6.283185
ROOTS = 2 * NT + 2
NEG = -1.0e30
PICK = 3.0e38
GELU_A = 0.044715
GELU_B = math.sqrt(2.0 / math.pi)

VEC_ROWS = [("norm_mix", KT), ("conv", CW * QK), ("norm_mlstm", NH), ("s5_d", CT), ("norm_s5", CT), ("norm_ffn", KT)]
VEC_PER = sum(n for _, n in VEC_ROWS)


def vec_col(l, name, i=0):
    at = l * VEC_PER
    for n, rows in VEC_ROWS:
        if n == name:
            return at + i
        at += rows
    raise KeyError(name)


def mixer_steps(l):
    proj = {0: [("if", l)], 2: [("qk", l, 0)], 4: [("qk", l, 1)], 6: [("qk", l, 2)], 8: [("qk", l, 3)],
            10: [("v", l, 0)], 11: [("tr", l)], 12: [("v", l, 1)], 14: [("o", l, 0)], 15: [("o", l, 1)]}
    return proj


def mixer_tail(l):
    order = [("mu", l, 0), ("mu", l, 1), ("sc", l, 0), ("sc", l, 1), ("z", l, 0), ("z", l, 1), ("num", l, 0),
             ("mu", l, 2), ("sc", l, 2), ("num", l, 1), ("mu", l, 3), ("sc", l, 3), ("num", l, 2), ("os", l, 0, 0),
             ("ss", l), ("num", l, 3), ("os", l, 0, 1), ("os", l, 1, 0), ("os", l, 1, 1)]
    return order + [("hmT", l, i) for i in range(2)] + [("oh", l, t, c) for t in range(NT) for c in range(2)]


def products():
    out = [(("vec",), "V", 0), (("s5p",), "V", 1)]
    turn = {"lo": 0, "hi": 0}

    def lo(name, who):
        out.append((name, who, turn["lo"] % 4))
        turn["lo"] += 1

    def hi(name, who):
        out.append((name, who, 4 + turn["hi"] % 4))
        turn["hi"] += 1

    def norm(l, what):
        for j in range(4):
            lo(("xT", l, what, j), "VA"[j % 2])

    def prep(l):
        for n in ("b_re", "b_im"):
            hi((n, l), "A")
        for n in ("c_re", "c_im"):
            hi((n, l), "V")

    for l in range(DEPTH):
        norm(l, 0)
        for i in range(2):
            hi(("u", l, i), "A")
        if l == 0:
            prep(0)
        for i in range(4):
            lo(("bu", l, i), "V")
        y = 0
        for i in range(PAIRS):
            for n in mixer_steps(l).get(i, []):
                out.append((n, "V" if n[0] == "if" else "A", 4 + turn["hi"] % 2))
                turn["hi"] += 1
            if i + 4 < PAIRS:
                lo(("bu", l, i + 4), "V")
            if i % PPC == PPC - 1:
                out.append((("y", l, i // PPC), "Y", 6 + y % 2))
                y += 1
        for n in mixer_tail(l):
            kind = n[0]
            (lo if kind in ("z", "num", "os") else hi)(n, "A" if kind in ("z", "ss", "hmT") else "V")
        if l == 0:
            prep(1)
        norm(l, 1)
        if l == 0:
            for f in range(FT):
                lo(("gu", f), "V")
            for t in range(NT):
                for c in range(2):
                    out.append((("ffn", t, c), "V", 4 + 2 * t + c))
        else:
            out.append((("logits",), "A", 5))
            out.append((("router",), "V", 4))
            out.append((("pos",), "V", 5))
    return out


class Banks:

    def __init__(self):
        self.at, self.before = {}, {}
        last, count = {}, {"V": 0, "A": 0, "Y": 0}
        n = 0
        for name, who, bank in products():
            count[who] += 1
            n += name[0] != "y"
            self.at[name] = (n, who, count[who], bank)
            self.before[name] = last.get(bank)
            last[bank] = name
        self.last = last


def chunk_plan():
    plan = []
    for l in range(DEPTH):
        plan += [("u", l), ("q", l), ("k", l), ("v", l), ("o", l), ("glu", l), ("out", l, 0), ("out", l, 1)]
        if l == 0:
            for j in range((FD + GW - 1) // GW):
                plan += [("fg", j), ("fu", j), ("fd", j)]
    return plan


def trunk_kernel(nc, x, norm_mix, w_in, conv_qk, b_igate, b_fgate, norm_mlstm, s5_a_re, s5_a_im, s5_log_dt,
                 s5_b_re, s5_b_im, s5_c_re, s5_c_im, s5_d, w_glu, norm_s5, w_out, norm_ffn, ffn_w_gate,
                 ffn_w_up, ffn_w_down, moe_w_router, moe_b_router, moe_w_gate, moe_w_up, moe_w_down,
                 norm_final, out):
    banks = Banks()
    plan = chunk_plan()
    chunk_no = {name: n for n, name in enumerate(plan)}

    ctx = ExitStack()
    with ctx:
        def sb(name, shape, dt=F32):
            return ctx.enter_context(nc.sbuf_tensor(name, shape, dt))

        def sem(name):
            return ctx.enter_context(nc.semaphore(name))

        ring = sb("ring", [P, RING, CHUNK])
        arena = sb("arena", [P, 20000])
        arena_end = nc.sbuf_base
        x_res = sb("x_res", [P, NT, DM])
        hn = sb("hn", [P, NT, DM])
        hnT = sb("hnT", [P, KT, SEQ])
        hnT_end = nc.sbuf_base
        ident = sb("ident", [P, P])
        ones = sb("ones", [P, P])
        lower = sb("lower", [P, P])
        cmask = sb("cmask", [P, SEQ])
        times = sb("times", [P, SEQ])
        gate_max = sb("gate_max", [NH, SEQ])
        head_pick = sb("head_pick", [NH, NH, P])
        neg_half = sb("neg_half", [P, NT * NH])
        half_pi = sb("half_pi", [P, 1])
        vec = sb("vec", [P, DEPTH * VEC_PER])
        s5p = sb("s5p", [P, 3, DEPTH, PAIRS])
        bT = sb("bT", [P, 2, CT, P])
        cT = sb("cT", [P, 3, CT, P])
        fac = sb("fac", [P, 24, PAIRS])
        w_if = sb("w_if", [P, KT, F_ROW + NH])
        w_rt = sb("w_rt", [P, KT, NE])
        b_rt = sb("b_rt", [P, NE])
        b_if = sb("b_if", [NH, DEPTH, 2])
        small = sb("small", [P, 64])

        at = [0]

        def carve(shape, base=None):
            n = int(np.prod(shape))
            a = at[0] if base is None else base
            if base is None:
                at[0] += n
            assert a + n <= 20000, (a, n)
            v = arena[:, a:a + n]
            letters = "abcd"[:len(shape)]
            if len(shape) > 1:
                v = v.rearrange(f"p ({' '.join(letters)}) -> p {' '.join(letters)}",
                                **{k: s for k, s in zip(letters[1:], shape[1:])})
            return v

        qk_pre = carve([QK, SEQ + CW - 1])
        turn = carve([3, 2, SEQ])
        phase = carve([2, 2, SEQ])
        shared = at[0]
        qk = carve([QK, SEQ])
        v_aug = carve([NT, NH, DH + 1])
        o_gate = carve([NT, DML])
        uT = carve([CT, SEQ])
        gT = carve([CT, SEQ])
        ysT = carve([CT, SEQ])
        hm = carve([NT, NH, DH])
        trig = carve([2, 2, 3, SEQ])
        rot = carve([2, 2, SEQ])
        drive = carve([2, SEQ])
        state = carve([2, SEQ])
        back = carve([2, 2, 2, SEQ])
        mix_end = at[0]
        mixT = hn[:, :, :].rearrange("p t d -> p (t d)").rearrange("p (k t) -> p k t", t=SEQ)
        sbase = mix_end - 2 * 2 * 2 * SEQ
        dec = carve([2, SEQ + P], sbase)
        scr = carve([2, SEQ + P], sbase + 2 * (SEQ + P))
        gates = hm[0:NH, :, :, :].rearrange("p a b c -> p (a b c)") \
            .rearrange("p (r t) -> p r t", r=4)
        pbase = mix_end - 8 * SEQ - 2 * SEQ - 2 * SEQ - 4 * SEQ
        b_raw = sb("b_raw", [P, 2, PAIRS, GP])
        c_raw = sb("c_raw", [P, 2, CT, NS])
        b_blk = carve([2, PAIRS, 2, GP], pbase)
        b_tmp = carve([4, PAIRS, GP], pbase + 4 * PAIRS * GP)
        c_dup = carve([2, CT, 2, NS], pbase + 8 * PAIRS * GP)
        vec_rows = carve([P], 0)
        s5_rows = carve([P], P)
        dt_rows = carve([2], 2 * P)
        assert pbase + 8 * PAIRS * GP + 4 * CT * NS <= mix_end
        ring_flat = ring[:, :, :].rearrange("p s n -> p (s n)")
        m_ring = [ring_flat[:, s * HALF:(s + 1) * HALF] for s in range(MRING)]

        split_bytes = 4 * SPLIT * PART
        w_hi = nc.alloc_sbuf_tensor_at("w_hi", [P, SPLIT, PART], F32R, offset=arena_end - 2 * split_bytes)
        w_lo = nc.alloc_sbuf_tensor_at("w_lo", [P, SPLIT, PART], F32R, offset=arena_end - split_bytes)
        assert KT * SEQ <= QK * (SEQ + CW - 1) and 4 * (20000 - shared - 3 * SEQ) >= 2 * split_bytes
        spare = arena[:, 0:DM]
        hnT_hi = nc.alloc_sbuf_tensor_at("hnT_hi", [P, KT, SEQ], F32R, offset=arena_end - 4 * 20000)
        hnT_lo = nc.alloc_sbuf_tensor_at("hnT_lo", [P, KT, SEQ], F32R, offset=hnT_end - 4 * KT * SEQ)
        hn_at = hnT_end - 4 * KT * SEQ - 4 * NT * DM
        f_hid_hi = nc.alloc_sbuf_tensor_at("f_hid_hi", [P, 3, SEQ], F32R, offset=hn_at)
        f_hid_lo = nc.alloc_sbuf_tensor_at("f_hid_lo", [P, 3, SEQ], F32R, offset=hn_at + 4 * 3 * SEQ)
        f_silu = carve([2, SEQ], shared)
        f_hid = carve([SEQ], shared + 2 * SEQ)
        hidT_at = arena_end - 2 * split_bytes - 8 * GW
        hidT_hi = nc.alloc_sbuf_tensor_at("hidT_hi", [P, GW // P, P], F32R, offset=hidT_at)
        hidT_lo = nc.alloc_sbuf_tensor_at("hidT_lo", [P, GW // P, P], F32R, offset=hidT_at + 4 * GW)
        xe_hi = nc.alloc_sbuf_tensor_at("xe_hi", [P, KT, P], F32R, offset=hnT_end - 8 * KT * P)
        xe_lo = nc.alloc_sbuf_tensor_at("xe_lo", [P, KT, P], F32R, offset=hnT_end - 4 * KT * P)

        def behind(shape, a):
            n = int(np.prod(shape))
            v = ring_flat[:, MRING * HALF + a:MRING * HALF + a + n]
            return v if len(shape) == 1 else v.rearrange("p (a b) -> p a b", a=shape[0])

        e_silu = behind([2, GW], 0)
        e_hid = behind([3, GW], 1024)
        ye = behind([DM], 3072)
        xe = behind([KT, P], 4096)
        gfin = behind([DM], 5120)
        items = NE + 4
        pick = carve([NT, P], 0)
        pickg = carve([NT, P], 256)
        pickT = carve([NT, P], 512)
        rt = carve([24, NT, NE], 768)
        posI = carve([NT, items], 1152)
        gateI = carve([NT, items], 1176)
        over = carve([8, NE], 1200)
        desc = carve([NE], 1264)
        logitsT = carve([SEQ], 1280)
        n_list = sb("n_list", [P, 4], I32)

        ps = [ctx.enter_context(nc.psum_tensor(f"ps{i}", [P, 512], F32)) for i in range(8)]

        s_x = sem("s_x")
        s_par = sem("s_par")
        s_bc = sem("s_bc")
        s_wif = sem("s_wif")
        w_if_zero = sem("w_if_zero")
        s_rt_in = sem("s_rt_in")
        s_gfin = sem("s_gfin")
        ring_full = [sem(f"ring_full{i}") for i in range(RING)]
        half_full = [sem(f"half_full{i}") for i in range(MRING)]
        ffn_x_hi = sem("ffn_x_hi")
        ffn_x_lo = sem("ffn_x_lo")
        ffn_hi = sem("ffn_hi")
        ffn_lo = sem("ffn_lo")
        ffn_used = sem("ffn_used")
        ffn_hid = sem("ffn_hid")
        product_ready = sem("product_ready")
        drained = {"V": sem("drained_v"), "A": sem("drained_a"), "Y": sem("drained_y")}
        consts = sem("consts")
        dve_chain = sem("dve_chain")
        act_chain = sem("act_chain")
        pool_chain = sem("pool_chain")
        ms_ready = sem("ms_ready")
        rs_ready = sem("rs_ready")
        hn_ready = sem("hn_ready")
        dt_wide = sem("dt_wide")
        prep_in = sem("prep_in")
        fac_act = sem("fac_act")
        blk_ready = sem("blk_ready")
        fac_ready = sem("fac_ready")
        turn_ready = sem("turn_ready")
        turn_used = sem("turn_used")
        phase_ready = sem("phase_ready")
        trig_ready = sem("trig_ready")
        tile_done = sem("tile_done")
        back_used = sem("back_used")
        conv_ready = sem("conv_ready")
        qk_ready = sem("qk_ready")
        g_in = sem("g_in")
        g_out = sem("g_out")
        gate_rows = sem("gate_rows")
        y_in = sem("y_in")
        y_tanh = sem("y_tanh")
        y_ready = sem("y_ready")
        glu_ready = sem("glu_ready")
        dec_ready = sem("dec_ready")
        score_ready = sem("score_ready")
        hm_ready = sem("hm_ready")
        mixed_s5 = sem("mixed_s5")
        squares_s5 = sem("squares_s5")
        ffn_silu = sem("ffn_silu")
        route_in = sem("route_in")
        route_exp = sem("route_exp")
        route_mask = sem("route_mask")
        items_ready = sem("items_ready")
        hi_ready = sem("hi_ready")
        lo_ready = sem("lo_ready")
        split_used = sem("split_used")
        e_tr = sem("e_tr")
        e_sc = sem("e_sc")
        e_gather = sem("e_gather")
        e_pt = sem("e_pt")
        a_silu = sem("a_silu")
        a_hT = sem("a_hT")
        a_ye = sem("a_ye")
        a_pt = sem("a_pt")
        v_hid = sem("v_hid")
        v_hT = sem("v_hT")
        v_xe = sem("v_xe")
        xe_steps = sem("xe_steps")
        v_add = sem("v_add")
        v_pick = sem("v_pick")
        fin_ready = sem("fin_ready")
        s_out = sem("s_out")

        def bank(name):
            return ps[banks.at[name][3]]

        def arrived(eng, name):
            if name[0] == "y":
                eng.wait_ge(back_used, PAIRS * name[1] + PPC * (name[2] + 1))
            else:
                eng.wait_ge(product_ready, banks.at[name][0])

        def wait_drained(eng, name):
            _, who, n, _ = banks.at[name]
            eng.wait_ge(drained[who], n)

        def open_bank(eng, name):
            if banks.before[name]:
                wait_drained(eng, banks.before[name])

        def chunk(name):
            return ring[:, chunk_no[name] % RING, :]

        def chunk_wait(eng, name):
            n = chunk_no[name]
            eng.wait_ge(ring_full[n % RING], 16 * (n // RING + 1))

        def wait_unused(eng, c):
            kind, i = c[0], c[1]
            if kind in ("fg", "fu", "fd"):
                f = min((i + 1) * GW // P, FT) - 1
                eng.wait_ge(ffn_lo, f_parts.index((kind, f)) + 1)
                return
            last = {"u": ("u", i, 1), "q": ("qk", i, 1), "k": ("qk", i, 3), "v": ("v", i, 1), "o": ("o", i, 1),
                    "glu": ("z", i, 1), "out": ("oh", i, NT - 1, c[-1])}[kind]
            arrived(eng, last)

        f_parts = ffn_parts()

        def ffn_raw(n):
            kind, f = f_parts[n]
            j, i = divmod(f, GW // P)
            width = min(GW, FD - j * GW)
            if kind == "fd":
                return chunk((kind, j))[:, i * DM:(i + 1) * DM]
            return v3(chunk((kind, j))[:, 0:KT * width], KT)[:, :, i * P:(i + 1) * P]

        def ffn_split(n, w):
            part = w[:, n % SPLIT, :]
            return part if f_parts[n][0] == "fd" else v3(part, KT)

        halves = item_halves()
        place = {c: m for m, c in enumerate(halves)}
        def half_wait(eng, it, c):
            m = place[c]
            eng.wait_ge(half_full[m % MRING], it * (16 * PER_ITEM // MRING) + 16 * (m // MRING + 1))

        def raw_part(q):
            return m_ring[q // 2 % MRING][:, q % 2 * PART:(q % 2 + 1) * PART]

        def part_used(eng, it, kind, j, z=3):
            eng.wait_ge(split_used, it * SPLITS + (part_no(kind, j, z) + 1))

        def v3(ap, k):
            return ap.rearrange("p (k n) -> p k n", k=k)

        block = ctx.enter_context(nc.Block())

        @block.sync
        def _(sp):
            sp.dma_start(x_res[:, :, :], x.rearrange("b (t p) d -> p (b t) d", p=P)).then_inc(s_x, 16)
            u_cols = w_in[0, :, U0:U0 + DS5].rearrange("(k p) n -> p k n", p=P)
            sp.dma_start(v3(ring[:, 0, :], KT), u_cols).then_inc(ring_full[0], 16)
            rows = {"norm_mix": norm_mix, "norm_mlstm": norm_mlstm, "s5_d": s5_d, "norm_s5": norm_s5,
                    "norm_ffn": norm_ffn}
            for l in range(DEPTH):
                for name, n in VEC_ROWS:
                    a = vec_col(l, name)
                    if name == "conv":
                        src = conv_qk[l].rearrange("w (k p) -> (w k) p", p=P)
                    else:
                        src = rows[name][l].rearrange("(k p) -> k p", p=P)
                    sp.dma_start(vec_rows[a:a + n, :], src).then_inc(s_par, 16)
            for i, a in enumerate((s5_a_re, s5_a_im)):
                sp.dma_start(s5_rows[32 * i:32 * i + 32, :],
                             a.rearrange("l (g h) s -> (l g) (h s)", h=2)).then_inc(s_par, 16)
            sp.dma_start(dt_rows[64:96, :], s5_log_dt.rearrange("l (g h) -> (l g) h", h=2)).then_inc(s_par, 16)
            for i, b in enumerate((b_igate, b_fgate)):
                sp.dma_start(b_if[:, :, i], b.rearrange("l h -> h l"),
                             allow_slow_non_contiguous=True).then_inc(s_par, 16)

            def layer_params(l):
                for i, b in enumerate((s5_b_re, s5_b_im)):
                    sp.dma_start(b_raw[:, i, :, :],
                                 b[l].rearrange("(g h) s c -> (h s) g c", h=2)).then_inc(s_bc, 16)
                for i, c in enumerate((s5_c_re, s5_c_im)):
                    sp.dma_start(c_raw[:, i, :, :],
                                 c[l].rearrange("(k g) c s -> (g c) k s", k=CT)).then_inc(s_bc, 16)
                if l:
                    wait_drained(sp, ("if", l - 1))
                else:
                    sp.wait_ge(w_if_zero, 1)
                for i, a in enumerate((0, F_ROW)):
                    c = IF0 + i * NH
                    sp.dma_start(w_if[:, :, a:a + NH],
                                 w_in[l, :, c:c + NH].rearrange("(k p) n -> p k n", p=P)).then_inc(s_wif, 16)

            layer_params(0)
            sp.dma_start(w_rt[:, :, :], moe_w_router[0].rearrange("(k p) n -> p k n", p=P)).then_inc(s_rt_in, 16)
            sp.dma_start(b_rt[:, :], moe_b_router[0:1, :].to_broadcast([P, NE])).then_inc(s_rt_in, 16)
            wcol = {"q": 0, "k": DML, "v": 2 * DML, "o": 3 * DML, "u": U0}
            for n, c in enumerate(plan):
                if n == 0:
                    continue
                if n >= RING:
                    wait_unused(sp, plan[n - RING])
                if c == ("out", 0, 0):
                    sp.wait_ge(blk_ready, 2)
                    layer_params(1)
                slot = ring[:, n % RING, :]
                kind = c[0]
                if kind in wcol:
                    a = wcol[kind]
                    dst, src = v3(slot, KT), w_in[c[1], :, a:a + 512]
                elif kind == "glu":
                    dst, src = v3(slot[:, 0:DS5 * CT], CT), w_glu[c[1]]
                elif kind == "out":
                    dst, src = v3(slot, KT), w_out[c[1], :, 512 * c[2]:512 * c[2] + 512]
                else:
                    a, b = c[1] * GW, min(c[1] * GW + GW, FD)
                    if kind == "fd":
                        dst = v3(slot[:, 0:(b - a) // P * DM], (b - a) // P)
                        src = ffn_w_down[0, a:b, :]
                    else:
                        dst = v3(slot[:, 0:KT * (b - a)], KT)
                        src = (ffn_w_gate if kind == "fg" else ffn_w_up)[0, :, a:b]
                sp.dma_start(dst, src.rearrange("(k p) n -> p k n", p=P)).then_inc(ring_full[n % RING], 16)

            def load_item(e, it, first=False):
                for m, (kind, j, h) in enumerate(halves):
                    s = m % MRING
                    if m < MRING and first:
                        wait_unused(sp, plan[max(n for n in range(len(plan)) if n % RING == s * HALF // CHUNK)])
                    else:
                        sp.wait_ge(lo_ready, it * SPLITS + 2 * (m - MRING + 1))
                    a = j * GW
                    if kind == "d":
                        a += h * GW // 2
                        src = moe_w_down[0, bass.ds(e, 1), a:a + GW // 2, :]
                        dst = v3(m_ring[s], GW // P // 2)
                    else:
                        src = (moe_w_gate if kind == "g" else moe_w_up)[0, bass.ds(e, 1),
                                                                        h * DM // 2:(h + 1) * DM // 2, a:a + GW]
                        dst = v3(m_ring[s], KT // 2)
                    sp.dma_start(dst, src.rearrange("e (k p) n -> p (e k) n", p=P)).then_inc(half_full[s], 16)
                    if first and m == MRING - 1:
                        wait_drained(sp, ("oh", 1, NT - 1, 1))
                        sp.dma_start(gfin, norm_final.rearrange("(a n) -> a n", a=1)
                                     .to_broadcast([P, DM])).then_inc(s_gfin, 16)

            load_item(0, 0, first=True)
            with sp.Fori(1, NE) as e:
                load_item(e, e)
            sp.wait_ge(items_ready, 1)
            n_over = sp.value_load(n_list[0:1, 0:1], min_val=0, max_val=3)
            with sp.If(n_over > 0):
                with sp.Fori(0, n_over) as k:
                    e = sp.value_load(n_list[0:1, bass.ds(k + 1, 1)], min_val=0, max_val=NE - 1)
                    load_item(e, k + NE)
            for t in range(NT):
                sp.wait_ge(fin_ready, t + 1)
                sp.dma_start(out[0, t * P:(t + 1) * P, :], hn[:, t, :]).then_inc(s_out, 16)
            sp.wait_ge(s_out, 16 * NT)

        @block.gpsimd
        def _(pool):
            chain = [0]

            def link(ins):
                chain[0] += 1
                ins.then_inc(pool_chain, 1)
                pool.wait_ge(pool_chain, chain[0])

            nc.gpsimd.memset(w_if[:, :, :], 0.0).then_inc(w_if_zero, 1)
            nc.gpsimd.memset(neg_half[:, :], -0.5)
            nc.gpsimd.memset(half_pi[:, :], math.pi / 2)
            nc.gpsimd.memset(ident[:, :], 0.0)
            nc.gpsimd.memset(lower[:, :], 1.0)
            nc.gpsimd.memset(cmask[:, :], 0.0)
            nc.gpsimd.memset(head_pick[:, :, :], 0.0)
            link(nc.gpsimd.memset(ones[:, :], 1.0))
            nc.gpsimd.affine_select(out=ident[:, :], in_=ident[:, :], compare_op=ALU.not_equal, fill=1.0, base=0,
                                    pattern=[[-1, P]], channel_multiplier=1)
            nc.gpsimd.affine_select(out=lower[:, :], in_=lower[:, :], compare_op=ALU.is_gt, fill=0.0, base=0,
                                    pattern=[[1, P]], channel_multiplier=-1)
            nc.gpsimd.affine_select(out=cmask[:, :], in_=cmask[:, :], compare_op=ALU.is_ge, fill=NEG, base=0,
                                    pattern=[[1, SEQ]], channel_multiplier=-1)
            nc.gpsimd.affine_select(out=head_pick[:, :, :], in_=head_pick[:, :, :], compare_op=ALU.not_equal,
                                    fill=-1.0, base=0, pattern=[[-1, NH], [0, P]], channel_multiplier=1)
            nc.gpsimd.iota(times[:, :], pattern=[[1, SEQ]], base=0, channel_multiplier=0,
                           allow_small_or_imprecise_dtypes=True).then_inc(consts, 1)
            pool.wait_ge(consts, 1)

            def rsqrt(cols):
                nc.gpsimd.tensor_tensor(small[:, cols], small[:, cols], neg_half[:, 0:cols.stop - cols.start],
                                        ALU.pow).then_inc(rs_ready, 1)

            def phases(l, i2):
                n = l * PAIRS // 2 + i2
                pool.wait_ge(turn_ready, n + 1)
                link(nc.gpsimd.tensor_scalar(turn[:, 1, :, :], turn[:, 0, :, :], ROUND_INT, ROUND_INT,
                                             ALU.add, ALU.subtract))
                link(nc.gpsimd.tensor_tensor(turn[:, 0, :, :], turn[:, 0, :, :], turn[:, 1, :, :], ALU.subtract))
                nc.gpsimd.tensor_tensor(turn[:, 1, :, :], turn[:, 0, :, :], turn[:, 2, :, :],
                                        ALU.add).then_inc(turn_used, 1)
                pool.wait_ge(turn_used, n + 1)
                if n:
                    pool.wait_ge(trig_ready, n)
                link(nc.gpsimd.tensor_scalar(phase[:, 0, :, :], turn[:, 1, :, :], ROUND_INT, ROUND_INT,
                                             ALU.add, ALU.subtract))
                nc.gpsimd.tensor_tensor(phase[:, 0, :, :], turn[:, 1, :, :], phase[:, 0, :, :],
                                        ALU.subtract).then_inc(phase_ready, 1)
                pool.wait_ge(phase_ready, n + 1)

            for l in range(DEPTH):
                for t in range(NT):
                    pool.wait_ge(ms_ready, (2 * NT + 1) * l + t + 1)
                    rsqrt(slice(t, t + 1))
                for i2 in range(PAIRS // 2):
                    phases(l, i2)
                wait_drained(pool, ("ss", l))
                rsqrt(slice(8, 8 + NT))
                pool.wait_ge(ms_ready, (2 * NT + 1) * l + NT + 1)
                rsqrt(slice(16, 16 + NT * NH))
                for t in range(NT):
                    pool.wait_ge(ms_ready, (2 * NT + 1) * l + NT + 2 + t)
                    rsqrt(slice(t, t + 1))
            for t in range(NT):
                pool.wait_ge(ms_ready, (2 * NT + 1) * DEPTH + t + 1)
                rsqrt(slice(t, t + 1))

        @block.scalar
        def _(act):
            chain = [0]

            def link(ins):
                chain[0] += 1
                ins.then_inc(act_chain, 1)
                act.wait_ge(act_chain, chain[0])

            def prep_factors(l):
                act.wait_ge(prep_in, 3 * l + 1)
                nc.scalar.activation(fac[:, 0, :], s5p[:, 2, l, :], ACT.Exp).then_inc(fac_act, 1)
                act.wait_ge(prep_in, 3 * l + 2)
                nc.scalar.activation(fac[:, 1, :], fac[:, 4, :], ACT.Exp).then_inc(fac_act, 1)
                act.wait_ge(prep_in, 3 * l + 3)
                nc.scalar.activation(fac[:, 2, :], fac[:, 5, :], ACT.Sin).then_inc(fac_act, 1)
                nc.scalar.activation(fac[:, 3, :], fac[:, 6, :], ACT.Sin, scale=-1.0,
                                     bias=half_pi[:, 0:1]).then_inc(fac_act, 1)

            def prep_blocks(l):
                for i, n in enumerate(("b_re", "b_im")):
                    arrived(act, (n, l))
                    nc.scalar.activation(bT[:, i, :, :], v3(bank((n, l))[:, :], CT),
                                         ACT.Copy).then_inc(drained["A"], 1)

            def xT(l, what):
                for j in (1, 3):
                    arrived(act, ("xT", l, what, j))
                    for k in range(2):
                        c = vec_col(l, ("norm_mix", "norm_ffn")[what], 2 * j + k)
                        ins = nc.scalar.activation(hnT[:, 2 * j + k, :], bank(("xT", l, what, j))[:, k * SEQ:(k + 1) * SEQ],
                                                   ACT.Copy, scale=vec[:, c:c + 1])
                    ins.then_inc(drained["A"], 1)

            def turns(l, i2):
                if i2 == 0:
                    act.wait_ge(consts, 1)
                    act.wait_ge(fac_ready, l + 1)
                for k in range(2):
                    i = 2 * i2 + k
                    nc.scalar.activation(turn[:, 0, k, :], times[:, :], ACT.Copy, scale=fac[:, 20, i:i + 1])
                    ins = nc.scalar.activation(turn[:, 2, k, :], times[:, :], ACT.Copy, scale=fac[:, 21, i:i + 1])
                ins.then_inc(turn_ready, 1)

            def trig_pair(l, i2):
                n = l * PAIRS // 2 + i2
                if i2 + 1 < PAIRS // 2:
                    act.wait_ge(turn_used, n + 1)
                    turns(l, i2 + 1)
                act.wait_ge(phase_ready, n + 1)
                if n >= 2:
                    act.wait_ge(tile_done, 2 * (n - 1))
                b = i2 % 2
                link(nc.scalar.activation(phase[:, 1, :, :], phase[:, 0, :, :], ACT.Abs))
                nc.scalar.activation(trig[:, b, :, 1, :], phase[:, 0, :, :], ACT.Sin, scale=SIN_SCALE)
                nc.scalar.activation(trig[:, b, :, 0, :], phase[:, 1, :, :], ACT.Sin, scale=-SIN_SCALE,
                                     bias=half_pi[:, 0:1])
                ins = nc.scalar.activation(trig[:, b, :, 2, :], phase[:, 1, :, :], ACT.Sin, scale=-SIN_SCALE,
                                           bias=half_pi[:, 0:1])
                ins.then_inc(trig_ready, 1)

            def gelu_square(l, c):
                wait_drained(act, ("y", l, c))
                nc.scalar.activation(gT[:, c, :], ysT[:, c, :], ACT.Square).then_inc(y_in, 1)

            def gelu_tanh(l, c):
                act.wait_ge(y_tanh, CT * l + c + 1)
                nc.scalar.activation(gT[:, c, :], gT[:, c, :], ACT.Tanh, scale=GELU_B).then_inc(y_ready, 1)

            def dec_exp(l, h):
                wait_drained(act, ("mu", l, h))
                nc.scalar.activation(dec[:, h % 2, :], dec[:, h % 2, :], ACT.Exp).then_inc(dec_ready, 1)

            def mixer(l):
                if l == 0:
                    prep_factors(0)
                    turns(0, 0)
                else:
                    trig_pair(l, 0)
                for i in range(2):
                    arrived(act, ("u", l, i))
                    nc.scalar.activation(uT[:, 2 * i:2 * i + 2, :], v3(bank(("u", l, i))[:, :], 2),
                                         ACT.Copy).then_inc(drained["A"], 1)
                if l == 0:
                    prep_blocks(0)
                if l == 0:
                    trig_pair(l, 0)
                trig_pair(l, 1)
                for i in range(PAIRS):
                    for n in mixer_steps(l).get(i, []):
                        if n[0] == "if":
                            continue
                        arrived(act, n)
                        src = bank(n)[:, :]
                        if n[0] == "qk":
                            dst = qk_pre[:, 2 * n[2]:2 * n[2] + 2, CW - 1:]
                            nc.scalar.activation(dst, v3(src, 2), ACT.Copy).then_inc(drained["A"], 1)
                        elif n[0] == "tr":
                            nc.scalar.activation(small[:, 32:32 + 4 * NH], src[:, 0:4 * NH],
                                                 ACT.Copy).then_inc(drained["A"], 1)
                        elif n[0] == "v":
                            nc.scalar.activation(v_aug[:, n[2], :, 0:DH], v3(src, NH),
                                                 ACT.Copy).then_inc(drained["A"], 1)
                        else:
                            nc.scalar.activation(o_gate[:, n[2], :], src, ACT.Tanh,
                                                 scale=0.5).then_inc(drained["A"], 1)
                    if i in (5, 7, 9, 11):
                        m = (i - 5) // 2
                        act.wait_ge(conv_ready, 4 * l + m + 1)
                        nc.scalar.activation(qk[:, 2 * m:2 * m + 2, :], qk[:, 2 * m:2 * m + 2, :],
                                             ACT.Silu).then_inc(qk_ready, 1)
                    if i == 3:
                        act.wait_ge(g_in, 2 * l + 1)
                        link(nc.scalar.activation(gates[:, 1, :], gates[:, 1, :], ACT.Exp))
                        nc.scalar.activation(gates[:, 1, :], gates[:, 1, :], ACT.Ln, bias=1.0).then_inc(g_out, 1)
                    if i == 5:
                        act.wait_ge(g_in, 2 * l + 2)
                        nc.scalar.activation(gates[:, 0, :], gates[:, 0, :], ACT.Exp).then_inc(gate_rows, 1)
                    if i % PPC == 1 and i > PPC:
                        gelu_square(l, i // PPC - 1)
                    if i % PPC == 3 and i > PPC:
                        gelu_tanh(l, i // PPC - 1)
                    if i % 2 == 1 and i // 2 + 2 < PAIRS // 2:
                        trig_pair(l, i // 2 + 2)
                gelu_square(l, CT - 1)
                gelu_tanh(l, CT - 1)
                dec_exp(l, 0)
                dec_exp(l, 1)
                for i in range(2):
                    arrived(act, ("z", l, i))
                    nc.scalar.activation(ysT[:, 2 * i:2 * i + 2, :], v3(bank(("z", l, i))[:, :], 2), ACT.Tanh,
                                         scale=0.25).then_inc(drained["A"], 1)
                dec_exp(l, 2)
                arrived(act, ("ss", l))
                nc.scalar.activation(small[:, 8:8 + NT], bank(("ss", l))[:, 0:NT], ACT.Copy, scale=1.0 / DS5,
                                     bias=16.0 * EPS).then_inc(drained["A"], 1)
                dec_exp(l, 3)
                if l == 0:
                    prep_factors(1)
                for i in range(2):
                    arrived(act, ("hmT", l, i))
                    for k in range(2):
                        c = vec_col(l, "norm_mlstm", 2 * i + k)
                        ins = nc.scalar.activation(mixT[:, 2 * i + k, :], bank(("hmT", l, i))[:, k * SEQ:(k + 1) * SEQ],
                                                   ACT.Copy, scale=vec[:, c:c + 1])
                    ins.then_inc(drained["A"], 1)

            def split(it, q, first):
                if q % 2 == 0:
                    half_wait(act, it, halves[q // 2])
                if q >= SPLIT or not first:
                    act.wait_ge(split_used, it * SPLITS + (q - SPLIT + 1))
                nc.scalar.activation(w_hi[:, q % SPLIT, :], raw_part(q), ACT.Copy).then_inc(hi_ready, 1)

            def ffn_high(n):
                kind, f = f_parts[n]
                chunk_wait(act, (kind, f * P // GW))
                if n >= SPLIT:
                    if f_parts[n - SPLIT][0] == "fu":
                        arrived(act, ("gu", f_parts[n - SPLIT][1]))
                    else:
                        act.wait_ge(ffn_used, sum(c[0] != "fu" for c in f_parts[:n - SPLIT + 1]))
                nc.scalar.activation(ffn_split(n, w_hi), ffn_raw(n), ACT.Copy).then_inc(ffn_hi, 1)

            for l in range(DEPTH):
                if l:
                    turns(l, 0)
                xT(l, 0)
                mixer(l)
                if l == 0:
                    for n in range(SPLIT):
                        ffn_high(n)
                    prep_blocks(1)
                else:
                    for q in range(SPLIT):
                        split(0, q, True)
                xT(l, 1)
                if l == 0:
                    for j in range(4):
                        wait_drained(act, ("xT", 0, 1, j))
                        k = slice(2 * j, 2 * j + 2)
                        nc.scalar.activation(hnT_hi[:, k, :], hnT[:, k, :], ACT.Copy).then_inc(ffn_x_hi, 1)
                    for n in range(SPLIT, len(f_parts) + SPLIT):
                        kind, f = f_parts[n - SPLIT]
                        if kind == "fu":
                            arrived(act, ("gu", f))
                            if f >= 2:
                                wait_drained(act, ("gu", f - 2))
                            nc.scalar.activation(f_silu[:, f % 2, :], bank(("gu", f))[:, 0:SEQ],
                                                 ACT.Silu).then_inc(ffn_silu, 1)
                        if n < len(f_parts):
                            ffn_high(n)
            arrived(act, ("logits",))
            nc.scalar.activation(logitsT[0:NE, :], bank(("logits",))[0:NE, 0:SEQ], ACT.Copy).then_inc(drained["A"], 1)
            act.wait_ge(route_in, 1)
            nc.scalar.activation(rt[:, 8, :, 0:1], rt[:, 7, :, 0:1], ACT.Exp).then_inc(route_exp, 1)

            def silu(it, j):
                part_used(act, it, "g", j)
                if type(it) is not int or it * NJ + j > 1:
                    act.wait_ge(v_hid, it * NJ + (j - 1 + (j == 0)))
                nc.scalar.activation(e_silu[:, j % 2, :], ps[2 * (j % 2)][:, :], ACT.Silu).then_inc(a_silu, 1)

            def hidden_out(it, j):
                act.wait_ge(e_tr, it * NJ + (j + 1))
                nc.scalar.activation(hidT_hi[:, :, :], v3(ps[4][:, :], 4), ACT.Copy).then_inc(a_hT, 1)

            def y_out(it):
                part_used(act, it, "d", NJ - 1)
                nc.scalar.activation(ye[:, 0:512], ps[6][:, :], ACT.Copy)
                nc.scalar.activation(ye[:, 512:1024], ps[7][:, :], ACT.Copy).then_inc(a_ye, 1)

            def item(it, first=False):
                for q in range(SPLITS):
                    if not first:
                        if q == after_part(part_no("d", NJ - 2, 3)) - SPLITS:
                            hidden_out(it - 1, NJ - 1)
                        if q == after_part(part_no("d", NJ - 1, 3)) - SPLITS:
                            y_out(it - 1)
                    for j in range(NJ):
                        if q == after_part(part_no("g", j, 3)) - 1:
                            silu(it, j)
                            if j:
                                hidden_out(it, j - 1)
                    if q == after_part(part_no("u", 1, 3)):
                        act.wait_ge(e_pt, it + 1)
                        nc.scalar.activation(pickT, v3(ps[5][:, 0:SEQ], NT), ACT.Copy).then_inc(a_pt, 1)
                    if q >= SPLIT or not first:
                        split(it, q, first)

            item(0, first=True)
            with act.Fori(1, NE) as e:
                item(e)
            act.wait_ge(items_ready, 1)
            n_over = act.value_load(n_list[0:1, 0:1], min_val=0, max_val=3)
            with act.If(n_over > 0):
                with act.Fori(0, n_over) as k:
                    item(k + NE)
            last = n_over + (NE - 1)
            hidden_out(last, NJ - 1)
            y_out(last)

        @block.vector
        def _(dve):
            V = nc.vector
            chain = [0]

            def link(ins):
                chain[0] += 1
                ins.then_inc(dve_chain, 1)
                dve.wait_ge(dve_chain, chain[0])

            def norm_sum(t, scratch):
                link(V.tensor_tensor_reduce(out=scratch, in0=x_res[:, t, :], in1=x_res[:, t, :], scale=1.0,
                                            scalar=0.0, op0=ALU.mult, op1=ALU.add, accum_out=small[:, t:t + 1]))
                V.tensor_scalar(small[:, t:t + 1], small[:, t:t + 1], 1.0 / DM, EPS, ALU.mult,
                                ALU.add).then_inc(ms_ready, 1)

            def norm_scale(before, meanwhile=None):
                for t in range(NT):
                    if t == NT - 1 and meanwhile:
                        meanwhile()
                    dve.wait_ge(rs_ready, before + t + 1)
                    V.tensor_scalar(hn[:, t, :], x_res[:, t, :], small[:, t:t + 1], None,
                                    ALU.mult).then_inc(hn_ready, 1)

            def xT(l, what):
                for j in (0, 2):
                    arrived(dve, ("xT", l, what, j))
                    for k in range(2):
                        c = vec_col(l, ("norm_mix", "norm_ffn")[what], 2 * j + k)
                        ins = V.tensor_scalar(hnT[:, 2 * j + k, :], bank(("xT", l, what, j))[:, k * SEQ:(k + 1) * SEQ],
                                              vec[:, c:c + 1], None, ALU.mult)
                    ins.then_inc(drained["V"], 1)

            def prep_factors(l):
                a_re, a_im = s5p[:, 0, l, :], s5p[:, 1, l, :]
                F = lambda i: fac[:, i, :]
                V.tensor_copy(F(7), a_re).then_inc(prep_in, 1)
                dve.wait_ge(fac_act, 4 * l + 1)
                V.tensor_tensor(F(4), a_re, F(0), ALU.mult).then_inc(prep_in, 1)
                link(V.tensor_tensor(F(8), a_im, F(0), ALU.mult))
                link(V.tensor_scalar(F(9), F(8), 1.0 / TWO_PI, ROUND_INT, ALU.mult, ALU.add))
                link(V.tensor_scalar(F(9), F(9), ROUND_INT, None, ALU.subtract))
                link(V.scalar_tensor_tensor(out=F(8), in0=F(9), scalar=-PI_A, in1=F(8), op0=ALU.mult, op1=ALU.add))
                link(V.scalar_tensor_tensor(out=F(8), in0=F(9), scalar=-PI_B, in1=F(8), op0=ALU.mult, op1=ALU.add))
                link(V.scalar_tensor_tensor(out=F(8), in0=F(9), scalar=-PI_C, in1=F(8), op0=ALU.mult, op1=ALU.add))
                link(V.tensor_scalar(F(5), F(8), 3.1415925, -3.1415925, ALU.min, ALU.max))
                V.scalar_tensor_tensor(out=F(6), in0=F(5), scalar=-1.0, in1=F(5), op0=ALU.mult,
                                       op1=ALU.max).then_inc(prep_in, 1)
                link(V.tensor_scalar(F(9), F(8), 1.0 / TWO_PI, None, ALU.mult))
                link(V.tensor_scalar(F(20), F(9), ROUND_12, ROUND_12, ALU.add, ALU.subtract))
                V.tensor_tensor(F(21), F(9), F(20), ALU.subtract)
                link(V.tensor_tensor(F(10), a_re, a_re, ALU.mult))
                link(V.tensor_tensor(F(11), a_im, a_im, ALU.mult))
                link(V.tensor_tensor(F(10), F(10), F(11), ALU.add))
                link(V.reciprocal(F(10), F(10)))
                dve.wait_ge(fac_act, 4 * l + 4)
                link(V.tensor_tensor(F(12), F(1), F(3), ALU.mult))
                link(V.tensor_scalar(F(12), F(12), 1.0, None, ALU.subtract))
                link(V.tensor_tensor(F(13), F(1), F(2), ALU.mult))
                V.tensor_tensor(F(14), F(12), a_re, ALU.mult)
                link(V.tensor_tensor(F(15), F(13), a_im, ALU.mult))
                link(V.tensor_tensor(F(14), F(14), F(15), ALU.add))
                V.tensor_tensor(F(15), F(13), a_re, ALU.mult)
                link(V.tensor_tensor(F(16), F(12), a_im, ALU.mult))
                link(V.tensor_tensor(F(15), F(15), F(16), ALU.subtract))
                V.tensor_tensor(F(17), F(14), F(10), ALU.mult)
                link(V.tensor_tensor(F(18), F(15), F(10), ALU.mult))
                V.tensor_copy(F(19), F(1)).then_inc(fac_ready, 1)

            def prep_blocks(l):
                F = lambda i: fac[:, i, :]
                f_re = F(17).unsqueeze(2).to_broadcast([P, PAIRS, GP])
                f_im = F(18).unsqueeze(2).to_broadcast([P, PAIRS, GP])
                dve.wait_ge(s_bc, 64 * (l + 1))
                V.memset(b_blk, 0.0)
                V.tensor_tensor(b_tmp[:, 0], b_raw[:, 0], f_re, ALU.mult)
                V.tensor_tensor(b_tmp[:, 1], b_raw[:, 1], f_im, ALU.mult)
                V.tensor_tensor(b_tmp[:, 2], b_raw[:, 1], f_re, ALU.mult)
                link(V.tensor_tensor(b_tmp[:, 3], b_raw[:, 0], f_im, ALU.mult))
                for g in range(2):
                    r = slice(NS * g, NS * g + NS)
                    V.tensor_tensor(b_blk[r, 0, :, g, :], b_tmp[r, 0], b_tmp[r, 1], ALU.subtract)
                    ins = V.tensor_tensor(b_blk[r, 1, :, g, :], b_tmp[r, 2], b_tmp[r, 3], ALU.add)
                ins.then_inc(blk_ready, 1)
                for g in range(2):
                    ins = V.tensor_copy(c_dup[:, :, :, g, :].rearrange("p a b c -> p (a b) c"),
                                        c_raw[:, :, :, :].rearrange("p a b c -> p (a b) c"))
                ins.then_inc(blk_ready, 1)
                link(V.memset(cT[:, :, :, :], 0.0))

            def prep_c(l):
                for i, n in enumerate(("c_re", "c_im")):
                    arrived(dve, (n, l))
                    src = bank((n, l))[:, :].rearrange("p (k g c) -> p k g c", g=2, c=GP)
                    for g in range(2):
                        r = slice(NS * g, NS * g + NS)
                        for m, sign in ((0, 1.0), (1, -1.0)) if i == 0 else ((2, -1.0),):
                            dst = cT[r, m, :, :].rearrange("p a b -> p (a b)") \
                                .rearrange("p (k g c) -> p k g c", g=2, c=GP)[:, :, g, :]
                            ins = V.tensor_scalar(dst, src[r, :, g, :], sign, None, ALU.mult)
                    ins.then_inc(drained["V"], 1)

            def s5_tile(l, i):
                n = l * PAIRS + i
                b, k = (i // 2) % 2, i % 2
                dve.wait_ge(trig_ready, n // 2 + 1)
                arrived(dve, ("bu", l, i))
                bu = v3(bank(("bu", l, i))[:, :], 2)
                V.tensor_tensor(rot[:, 0, :, :], bu, trig[:, b, k, 0:2, :], ALU.mult)
                ins = V.tensor_tensor(rot[:, 1, :, :], bu, trig[:, b, k, 1:3, :], ALU.mult)
                ins.then_inc(drained["V"], 1)
                wait_drained(dve, ("bu", l, i))
                V.tensor_tensor(drive[:, 0, :], rot[:, 0, 0, :], rot[:, 0, 1, :], ALU.add)
                link(V.tensor_tensor(drive[:, 1, :], rot[:, 1, 1, :], rot[:, 1, 0, :], ALU.subtract))
                decay = fac[:, 19, i:i + 1].to_broadcast([P, SEQ])
                V.tensor_tensor_scan(state[:, 0, :], decay, drive[:, 0, :], 0.0, ALU.mult, ALU.add)
                link(V.tensor_tensor_scan(state[:, 1, :], decay, drive[:, 1, :], 0.0, ALU.mult, ALU.add))
                if n >= 2:
                    dve.wait_ge(back_used, n - 1)
                V.tensor_tensor(back[:, n % 2, 0, :, :], state[:, :, :], trig[:, b, k, 0:2, :], ALU.mult)
                V.tensor_tensor(back[:, n % 2, 1, :, :], state[:, :, :], trig[:, b, k, 1:3, :],
                                ALU.mult).then_inc(tile_done, 1)

            def y_tile(l, c):
                arrived(dve, ("y", l, c))
                col = vec_col(l, "s5_d", c)
                V.scalar_tensor_tensor(out=ysT[:, c, :], in0=uT[:, c, :], scalar=vec[:, col:col + 1],
                                       in1=bank(("y", l, c))[:, 0:SEQ], op0=ALU.mult,
                                       op1=ALU.add).then_inc(drained["Y"], 1)

            def gelu_inner(l, c):
                dve.wait_ge(y_in, CT * l + c + 1)
                link(V.tensor_scalar(gT[:, c, :], gT[:, c, :], GELU_A, 1.0, ALU.mult, ALU.add))
                V.tensor_tensor(gT[:, c, :], gT[:, c, :], ysT[:, c, :], ALU.mult).then_inc(y_tanh, 1)

            def gelu_outer(l, c):
                dve.wait_ge(y_ready, CT * l + c + 1)
                V.scalar_tensor_tensor(out=gT[:, c, :], in0=gT[:, c, :], scalar=1.0, in1=ysT[:, c, :],
                                       op0=ALU.add, op1=ALU.mult).then_inc(glu_ready, 1)

            def conv(l, m):
                wait_drained(dve, ("qk", l, m))
                for w in range(CW):
                    for k in (2 * m, 2 * m + 1):
                        col = vec_col(l, "conv", w * QK + k)
                        src = qk_pre[:, k, w:w + SEQ]
                        if w == 0:
                            ins = V.tensor_scalar(qk[:, k, :], src, vec[:, col:col + 1], None, ALU.mult)
                        else:
                            ins = V.scalar_tensor_tensor(out=qk[:, k, :], in0=src, scalar=vec[:, col:col + 1],
                                                         in1=qk[:, k, :], op0=ALU.mult, op1=ALU.add)
                    if w < CW - 1:
                        link(ins)
                ins.then_inc(conv_ready, 1)

            def gate_start(l):
                G = lambda i: gates[:, i, :]
                arrived(dve, ("if", l))
                rows = bank(("if", l))
                V.tensor_copy(G(3), rows[0:NH, 0:SEQ])
                V.tensor_copy(G(0), rows[F_ROW:F_ROW + NH, 0:SEQ]).then_inc(drained["V"], 1)
                wait_drained(dve, ("if", l))
                link(V.tensor_scalar(G(0), G(0), b_if[:, l, 1:2], None, ALU.add))
                V.scalar_tensor_tensor(out=G(1), in0=G(0), scalar=-1.0, in1=G(0), op0=ALU.mult,
                                       op1=ALU.min).then_inc(g_in, 1)

            def gate_sums(l):
                G = lambda i: gates[:, i, :]
                dve.wait_ge(g_out, l + 1)
                link(V.scalar_tensor_tensor(out=G(0), in0=G(0), scalar=0.0, in1=G(1), op0=ALU.min,
                                            op1=ALU.subtract))
                link(V.tensor_tensor_scan(G(2), ones[0:NH, 0:1].to_broadcast([NH, SEQ]), G(0), 0.0,
                                          ALU.mult, ALU.add))
                link(V.scalar_tensor_tensor(out=G(3), in0=G(3), scalar=b_if[:, l, 0:1], in1=G(2), op0=ALU.add,
                                            op1=ALU.subtract))
                link(V.tensor_tensor_scan(gate_max[:, :], G(3), G(3), 0.0, ALU.max, ALU.max))
                V.scalar_tensor_tensor(out=G(0), in0=G(2), scalar=-1.0, in1=gate_max[:, :], op0=ALU.mult,
                                       op1=ALU.subtract).then_inc(g_in, 1)

            def head_decay(l, h):
                arrived(dve, ("mu", l, h))
                mu = bank(("mu", l, h))
                if h >= 2:
                    arrived(dve, ("num", l, h - 2))
                a0, a1 = small[:, 32 + h:33 + h], small[:, 32 + NH + h:33 + NH + h]
                if h == 0:
                    wait_drained(dve, ("tr", l))
                    arrived(dve, ("y", l, CT - 1))
                V.scalar_tensor_tensor(out=dec[:, h % 2, 0:SEQ], in0=mu[:, 0:SEQ], scalar=a0, in1=cmask[:, :],
                                       op0=ALU.add, op1=ALU.min)
                V.scalar_tensor_tensor(out=dec[:, h % 2, SEQ:], in0=mu[:, P:SEQ], scalar=a1, in1=cmask[:, 0:P],
                                       op0=ALU.add, op1=ALU.min).then_inc(drained["V"], 1)

            def head_score(l, h):
                arrived(dve, ("sc", l, h))
                dve.wait_ge(dec_ready, NH * l + h + 1)
                V.scalar_tensor_tensor(out=scr[:, h % 2, :], in0=bank(("sc", l, h))[:, 0:SEQ + P], scalar=DH ** -0.5,
                                       in1=dec[:, h % 2, :], op0=ALU.mult, op1=ALU.mult).then_inc(drained["V"], 1)

            def head_out(l, h):
                arrived(dve, ("num", l, h))
                num = v3(bank(("num", l, h))[:, :], 2)
                e = small[:, 32 + 2 * NH:32 + 4 * NH].rearrange("p (t h) -> p t h", t=NT)[:, :, h:h + 1]
                d = small[:, 48 + 2 * h:50 + 2 * h].unsqueeze(2)
                link(V.scalar_tensor_tensor(out=d, in0=num[:, :, DH:DH + 1], scalar=-1.0, in1=e, op0=ALU.mult,
                                            op1=ALU.max))
                link(V.scalar_tensor_tensor(out=d, in0=num[:, :, DH:DH + 1], scalar=1.0, in1=d, op0=ALU.mult,
                                            op1=ALU.max))
                link(V.reciprocal(d, d))
                for t in range(NT):
                    ins = V.tensor_scalar(hm[:, t, h, :], num[:, t, 0:DH], small[:, 48 + 2 * h + t:49 + 2 * h + t],
                                          None, ALU.mult)
                ins.then_inc(drained["V"], 1)
                wait_drained(dve, ("num", l, h))
                for t in range(NT):
                    ins = V.tensor_tensor_reduce(out=rot[:, 0, 0, t * P:(t + 1) * P], in0=hm[:, t, h, :],
                                                 in1=hm[:, t, h, :], scale=1.0, scalar=0.0, op0=ALU.mult,
                                                 op1=ALU.add, accum_out=small[:, 16 + t * NH + h:17 + t * NH + h])
                return ins

            def mixer_pads():
                V.memset(qk_pre[:, :, 0:CW - 1], 0.0)
                link(V.memset(v_aug[:, :, :, DH:DH + 1], 1.0))

            def low(it, q):
                dve.wait_ge(hi_ready, it * SPLITS + (q + 1))
                V.tensor_tensor(w_lo[:, q % SPLIT, :], raw_part(q), w_hi[:, q % SPLIT, :].bitcast(F32),
                                ALU.subtract).then_inc(lo_ready, 1)

            def ffn_low(n):
                dve.wait_ge(ffn_hi, n + 1)
                V.tensor_tensor(ffn_split(n, w_lo), ffn_raw(n), ffn_split(n, w_hi).bitcast(F32),
                                ALU.subtract).then_inc(ffn_lo, 1)

            def ffn_hidden(f):
                dve.wait_ge(ffn_silu, f + 1)
                if f >= 3:
                    arrived(dve, ("gu", f - 1))
                if f:
                    dve.wait_ge(ffn_hid, f)
                V.tensor_tensor(f_hid, f_silu[:, f % 2, :], bank(("gu", f))[:, SEQ:2 * SEQ],
                                ALU.mult).then_inc(drained["V"], 1)
                wait_drained(dve, ("gu", f))
                link(V.tensor_copy(f_hid_hi[:, f % 3, :], f_hid))
                V.tensor_tensor(f_hid_lo[:, f % 3, :], f_hid, f_hid_hi[:, f % 3, :].bitcast(F32),
                                ALU.subtract).then_inc(ffn_hid, 1)

            def out_s5(l, t, c):
                arrived(dve, ("os", l, t, c))
                dve.wait_ge(rs_ready, ROOTS * l + NT + 1)
                xs = x_res[:, t, 512 * c:512 * c + 512]
                V.scalar_tensor_tensor(out=xs, in0=bank(("os", l, t, c))[:, :], scalar=small[:, 8 + t:9 + t],
                                       in1=xs, op0=ALU.mult, op1=ALU.add).then_inc(drained["V"], 1)

            dve.wait_ge(s_x, 16)
            for t in range(NT):
                norm_sum(t, hn[:, t, :])
            norm_scale(0)
            dve.wait_ge(s_par, 16 * (2 * len(VEC_ROWS) + 5))
            V.tensor_copy(s5_rows[64:96, :].rearrange("p (h s) -> p h s", h=2),
                          dt_rows[64:96, :].unsqueeze(2).to_broadcast([32, 2, NS])).then_inc(dt_wide, 1)
            arrived(dve, ("vec",))
            V.tensor_copy(vec[:, :], bank(("vec",))[:, 0:DEPTH * VEC_PER]).then_inc(drained["V"], 1)
            arrived(dve, ("s5p",))
            V.tensor_copy(s5p[:, :, :, :].rearrange("p a l g -> p (a l g)"),
                          bank(("s5p",))[:, 0:3 * DEPTH * PAIRS]).then_inc(drained["V"], 1)
            wait_drained(dve, ("s5p",))
            mixer_pads()
            dve.wait_ge(consts, 1)
            for l in range(DEPTH):
                xT(l, 0)
                if l == 0:
                    prep_factors(0)
                    prep_blocks(0)
                    prep_c(0)
                for i in range(PAIRS):
                    s5_tile(l, i)
                    c = i // PPC - 1
                    if c >= 0 and i % PPC == 1:
                        y_tile(l, c)
                    if c >= 0 and i % PPC == 2:
                        gelu_inner(l, c)
                    if c >= 0 and i % PPC == 3:
                        gelu_outer(l, c)
                    if i == 3:
                        gate_start(l)
                    if i == 5:
                        gate_sums(l)
                    if i in (4, 6, 8, 10):
                        conv(l, (i - 4) // 2)
                y_tile(l, CT - 1)
                head_decay(l, 0)
                gelu_inner(l, CT - 1)
                head_decay(l, 1)
                gelu_outer(l, CT - 1)
                head_score(l, 0)
                head_score(l, 1)
                head_out(l, 0)
                head_decay(l, 2)
                for i in range(2):
                    wait_drained(dve, ("z", l, i))
                    V.scalar_tensor_tensor(out=ysT[:, 2 * i:2 * i + 2, :].rearrange("p a b -> p (a b)"),
                                           in0=ysT[:, 2 * i:2 * i + 2, :].rearrange("p a b -> p (a b)"), scalar=1.0,
                                           in1=gT[:, 2 * i:2 * i + 2, :].rearrange("p a b -> p (a b)"),
                                           op0=ALU.add, op1=ALU.mult).then_inc(dve_chain, 1)
                    chain[0] += 1
                dve.wait_ge(dve_chain, chain[0])
                for c in range(CT):
                    col = vec_col(l, "norm_s5", c)
                    ins = V.tensor_scalar(mixT[:, CT + c, :], ysT[:, c, :], vec[:, col:col + 1], None, ALU.mult)
                ins.then_inc(mixed_s5, 1)
                V.tensor_tensor(gT[:, :, :].rearrange("p a b -> p (a b)"), ysT[:, :, :].rearrange("p a b -> p (a b)"),
                                ysT[:, :, :].rearrange("p a b -> p (a b)"), ALU.mult).then_inc(squares_s5, 1)
                head_score(l, 2)
                head_out(l, 1)
                head_decay(l, 3)
                head_score(l, 3)
                head_out(l, 2)
                for t in range(NT):
                    wait_drained(dve, ("o", l, t))
                    ins = V.tensor_scalar(o_gate[:, t, :], o_gate[:, t, :], 0.5, 0.5, ALU.mult, ALU.add)
                link(ins)
                out_s5(l, 0, 0)
                link(head_out(l, NH - 1))
                V.tensor_scalar(small[:, 16:16 + NT * NH], small[:, 16:16 + NT * NH], 1.0 / DH, EPS, ALU.mult,
                                ALU.add).then_inc(ms_ready, 1)
                out_s5(l, 0, 1)
                dve.wait_ge(rs_ready, ROOTS * l + NT + 2)
                for t in range(NT):
                    for h in range(NH):
                        c = 16 + t * NH + h
                        ins = V.scalar_tensor_tensor(out=hm[:, t, h, :], in0=hm[:, t, h, :], scalar=small[:, c:c + 1],
                                                     in1=o_gate[:, t, h * DH:(h + 1) * DH], op0=ALU.mult, op1=ALU.mult)
                ins.then_inc(hm_ready, 1)
                if l == 0:
                    prep_factors(1)
                out_s5(l, 1, 0)
                out_s5(l, 1, 1)
                if l == 0:
                    prep_blocks(1)
                else:
                    low(0, 0)
                    low(0, 1)
                for t in range(NT):
                    for c in range(2):
                        arrived(dve, ("oh", l, t, c))
                        xs = x_res[:, t, 512 * c:512 * c + 512]
                        wait_drained(dve, ("os", l, t, c))
                        V.tensor_tensor(xs, bank(("oh", l, t, c))[:, :], xs, ALU.add).then_inc(drained["V"], 1)
                        if (t, c) != (NT - 1, 1):
                            k = 2 * t + c
                            if l == 0:
                                ffn_low(k)
                            else:
                                for q in range(2 * k + 2, min(2 * k + 4, FIRST)):
                                    low(0, q)
                    wait_drained(dve, ("oh", l, t, 1))
                    norm_sum(t, spare)
                norm_scale(ROOTS * l + 4, (lambda: prep_c(1)) if l == 0 else None)
                xT(l, 1)
                if l == 0:
                    for j in range(4):
                        wait_drained(dve, ("xT", 0, 1, j))
                        dve.wait_ge(ffn_x_hi, j + 1)
                        k = slice(2 * j, 2 * j + 2)
                        V.tensor_tensor(hnT_lo[:, k, :], hnT[:, k, :], hnT_hi[:, k, :].bitcast(F32),
                                        ALU.subtract).then_inc(ffn_x_lo, 1)
                    for n in range(3, len(f_parts) + SPLIT + 1):
                        if n > SPLIT and f_parts[n - SPLIT - 1][0] == "fu":
                            ffn_hidden(f_parts[n - SPLIT - 1][1])
                        if n < len(f_parts):
                            ffn_low(n)
                    for t in range(NT):
                        for c in range(2):
                            arrived(dve, ("ffn", t, c))
                            xs = x_res[:, t, 512 * c:512 * c + 512]
                            V.tensor_tensor(xs, bank(("ffn", t, c))[:, :], xs, ALU.add).then_inc(drained["V"], 1)
                        wait_drained(dve, ("ffn", t, 1))
                        norm_sum(t, spare)
                    norm_scale(ROOTS)
                    mixer_pads()

            R = lambda i: rt[:, i, :, :]
            R1 = lambda i: rt[:, i, :, 0:1]
            wide = lambda i: rt[:, i, :, 0:1].to_broadcast([P, NT, NE])
            row = lambda ap: ap.unsqueeze(1).to_broadcast([P, NT, NE])
            for e in range(NE):
                ins = V.memset(desc[:, e:e + 1], float(NE - e))
            link(ins)
            dve.wait_ge(s_rt_in, 32)
            arrived(dve, ("router",))
            V.tensor_tensor(R(0), bank(("router",))[:, 0:NT * NE].rearrange("p (t e) -> p t e", t=NT), row(b_rt[:, :]),
                            ALU.add).then_inc(drained["V"], 1)
            wait_drained(dve, ("router",))

            def first_max(src, top, hot):
                link(V.tensor_reduce(R1(top), R(src), AX, ALU.max))
                link(V.tensor_tensor(R(hot), R(src), wide(top), ALU.is_equal))
                link(V.tensor_tensor(R(hot), R(hot), row(desc), ALU.mult))
                link(V.tensor_reduce(R1(23), R(hot), AX, ALU.max))
                link(V.tensor_tensor(R(hot), R(hot), wide(23), ALU.is_equal))

            first_max(0, 1, 2)
            link(V.scalar_tensor_tensor(out=rt[:, 3, :, :], in0=R(2), scalar=-PICK, in1=R(0), op0=ALU.mult,
                                        op1=ALU.add))
            first_max(3, 4, 5)
            V.tensor_tensor(R1(7), R1(4), R1(1), ALU.subtract).then_inc(route_in, 1)
            V.tensor_tensor(R(6), R(2), R(5), ALU.add).then_inc(route_mask, 1)
            dve.wait_ge(route_exp, 1)
            link(V.tensor_scalar(R1(9), R1(8), 1.0, None, ALU.add))
            link(V.reciprocal(R1(9), R1(9)))
            link(V.tensor_tensor(R1(10), R1(9), R1(8), ALU.mult))
            V.tensor_tensor(R(11), R(2), wide(9), ALU.mult)
            link(V.tensor_tensor(R(12), R(5), wide(10), ALU.mult))
            link(V.tensor_tensor(R(11), R(11), R(12), ALU.add))
            arrived(dve, ("pos",))
            pos = bank(("pos",))
            link(V.scalar_tensor_tensor(out=rt[:, 13, :, :].rearrange("p t e -> p (t e)"), in0=pos[:, 0:NT * NE], scalar=1.0,
                                        in1=rt[:, 6, :, :].rearrange("p t e -> p (t e)"), op0=ALU.add, op1=ALU.mult))
            V.tensor_scalar(R(13), R(13), 1.0, None, ALU.subtract)
            O = lambda i: over[:, i, :]
            link(V.tensor_scalar(O(0), pos[:, NT * NE:NT * NE + NE], float(P), None, ALU.is_gt))
            link(V.tensor_tensor_scan(O(1), ones[:, 0:NE], O(0), 0.0, ALU.mult, ALU.add))
            link(V.tensor_scalar(O(7), desc, -1.0, float(NE), ALU.mult, ALU.add))
            V.tensor_copy(posI[:, :, 0:NE], R(13))
            V.memset(posI[:, :, NE:], -1.0)
            V.memset(gateI[:, :, NE:], 0.0)
            V.tensor_copy(gateI[:, :, 0:NE], R(11))
            link(V.tensor_copy(n_list[:, 0:1], O(1)[:, NE - 1:NE]))
            def second_tiles():
                for k in range(3):
                    link(V.tensor_scalar(O(2), O(1), float(k + 1), None, ALU.is_equal))
                    link(V.tensor_tensor(O(2), O(2), O(0), ALU.mult))
                    link(V.tensor_tensor(O(3), O(2), O(7), ALU.mult))
                    link(V.tensor_reduce(O(4)[:, 0:1], O(3), AX, ALU.add))
                    link(V.tensor_copy(n_list[:, k + 1:k + 2], O(4)[:, 0:1]))
                    link(V.tensor_tensor(R(14), R(13), row(O(2)), ALU.mult))
                    link(V.tensor_reduce(R1(15), R(14), AX, ALU.add))
                    link(V.tensor_scalar(posI[:, :, NE + k:NE + k + 1], R1(15), float(P), None, ALU.subtract))
                    link(V.tensor_tensor(R(14), R(11), row(O(2)), ALU.mult))
                    ins = V.tensor_reduce(gateI[:, :, NE + k:NE + k + 1], R(14), AX, ALU.add)
                    if k < 2:
                        link(ins)
                ins.then_inc(items_ready, 1)
                dve.wait_ge(items_ready, 1)

            def choose(nxt):
                for t in range(NT):
                    p = posI[:, t, nxt]
                    g = gateI[:, t, nxt]
                    V.tensor_scalar(pick[:, t, :], times[:, 0:P], p, None, ALU.is_equal)
                    ins = V.tensor_scalar(pickg[:, t, :], times[:, 0:P], p, g, ALU.is_equal, ALU.mult)
                ins.then_inc(v_pick, 1)

            gcol = vec_col(1, "norm_ffn")

            def take_tokens(it):
                for half, b in ((0, 5), (1, 2)):
                    dve.wait_ge(e_gather, it * 2 + (half + 1))
                    k = slice(4 * half, 4 * half + 4)
                    w = vec[:, gcol + 4 * half:gcol + 4 * half + 4].unsqueeze(2).to_broadcast([P, 4, P])
                    V.tensor_tensor(xe[:, k, :], v3(ps[b][:, :], 4), w, ALU.mult).then_inc(xe_steps, 1)
                    dve.wait_ge(xe_steps, it * 4 + (2 * half + 1))
                    V.tensor_copy(xe_hi[:, k, :], xe[:, k, :]).then_inc(xe_steps, 1)
                    dve.wait_ge(xe_steps, it * 4 + (2 * half + 2))
                    V.tensor_tensor(xe_lo[:, k, :], xe[:, k, :], xe_hi[:, k, :].bitcast(F32),
                                    ALU.subtract).then_inc(v_xe, 1)

            def add_out(it):
                for t in range(NT):
                    add_out_tile(it, t)

            def add_out_tile(it, t):
                for c in range(2):
                    n = 2 * t + c
                    dve.wait_ge(e_sc, it * 4 + (n - 3))
                    xs = x_res[:, t, 512 * c:512 * c + 512]
                    V.tensor_tensor(xs, ps[SCATTER[n]][:, :], xs, ALU.add).then_inc(v_add, 1)

            def hidden(it, j):
                part_used(dve, it, "u", j)
                dve.wait_ge(a_silu, it * NJ + (j + 1))
                V.tensor_tensor(e_hid[:, 2 if j == NJ - 1 else j % 2, :], e_silu[:, j % 2, :],
                                ps[2 * (j % 2) + 1][:, :], ALU.mult).then_inc(v_hid, 1)

            def hidden_low(it, j):
                dve.wait_ge(a_hT, it * NJ + (j + 1))
                V.tensor_tensor(hidT_lo[:, :, :], v3(ps[4][:, :], 4), hidT_hi[:, :, :].bitcast(F32),
                                ALU.subtract).then_inc(v_hT, 1)

            def item(it, first=False):
                for q in range(SPLITS):
                    if q == after_part(part_no("d", NJ - 2, 3)) - SPLITS:
                        if not first:
                            hidden_low(it - 1, NJ - 1)
                        take_tokens(it)
                    for j in range(NJ):
                        if q == after_part(part_no("u", j, 3)):
                            hidden(it, j)
                        if j and q == after_part(part_no("u", j, 0)):
                            hidden_low(it, j - 1)
                    if q == after_part(part_no("g", 1, 3)) + 1 and not first:
                        add_out(it)
                    if first and q == part_no("g", 5):
                        second_tiles()
                    if q == after_part(part_no("u", 2, 3)) + 2:
                        dve.wait_ge(e_pt, it + 1)
                        choose(bass.ds(it + 1, 1))
                    if q >= FIRST or not first:
                        low(it, q)

            choose(slice(0, 1))
            item(0, first=True)
            with dve.Fori(1, NE) as e:
                item(e)
            n_over = dve.value_load(n_list[0:1, 0:1], min_val=0, max_val=3)
            with dve.If(n_over > 0):
                with dve.Fori(0, n_over) as k:
                    item(k + NE)
            hidden_low(n_over + (NE - 1), NJ - 1)
            for t in range(NT):
                add_out_tile(n_over + NE, t)
                dve.wait_ge(v_add, (n_over + NE) * 4 + (2 * t - 2))
                norm_sum(t, hn[:, t, :])
            dve.wait_ge(s_gfin, 16)
            for t in range(NT):
                dve.wait_ge(rs_ready, ROOTS * DEPTH + t + 1)
                V.scalar_tensor_tensor(out=hn[:, t, :], in0=x_res[:, t, :], scalar=small[:, t:t + 1], in1=gfin,
                                       op0=ALU.mult, op1=ALU.mult).then_inc(fin_ready, 1)

        @block.tensor
        def _(pe):
            M = nc.tensor.matmul

            def done(ins):
                ins.then_inc(product_ready, 1)

            def prep(l):
                pe.wait_ge(blk_ready, 2 * l + 1)
                for i, n in enumerate(("b_re", "b_im")):
                    open_bank(pe, (n, l))
                    for c in range(CT):
                        ins = nc.tensor.transpose(bank((n, l))[:, c * P:(c + 1) * P],
                                                  b_blk[:, i, PPC * c:PPC * c + PPC, :, :]
                                                  .rearrange("p a b c -> p (a b c)"), ident[:, :])
                    done(ins)
                pe.wait_ge(blk_ready, 2 * l + 2)
                for i, n in enumerate(("c_re", "c_im")):
                    open_bank(pe, (n, l))
                    for c in range(CT):
                        ins = nc.tensor.transpose(bank((n, l))[:, c * P:(c + 1) * P],
                                                  c_dup[:, i, c, :, :].rearrange("p a b -> p (a b)"), ident[:, :])
                    done(ins)

            def norm(l, what):
                pe.wait_ge(hn_ready, (2 * l + what + 1) * NT)
                for j in range(4):
                    n = ("xT", l, what, j)
                    open_bank(pe, n)
                    for k in range(2):
                        for t in range(NT):
                            a = (2 * j + k) * P
                            ins = nc.tensor.transpose(bank(n)[:, k * SEQ + t * P:k * SEQ + (t + 1) * P],
                                                      hn[:, t, a:a + P], ident[:, :])
                    done(ins)

            def have_hnT(l, what):
                for j in range(4):
                    wait_drained(pe, ("xT", l, what, j))

            def channels(name, w, cols, last_of=None):
                open_bank(pe, name)
                for i, a in enumerate(cols):
                    for k in range(KT):
                        ins = M(bank(name)[:, i * SEQ:(i + 1) * SEQ], w[:, k, a:a + P], hnT[:, k, :],
                                start=(k == 0), stop=(k == KT - 1))
                return ins

            def mixer(l):
                have_hnT(l, 0)
                chunk_wait(pe, ("u", l))
                for i in range(2):
                    ins = channels(("u", l, i), v3(chunk(("u", l)), KT), (2 * i * P, 2 * i * P + P))
                    done(ins)
                if l == 0:
                    prep(0)

                def bu(i):
                    n = ("bu", l, i)
                    open_bank(pe, n)
                    c, j = divmod(i, PPC)
                    r = slice(32 * j, 32 * j + 32)
                    for m in range(2):
                        ins = M(bank(n)[:, m * SEQ:(m + 1) * SEQ], bT[r, m, c, :], uT[r, c, :], start=True, stop=True)
                    done(ins)

                wait_drained(pe, ("u", l, 1))
                wait_drained(pe, ("b_im", l))
                for i in range(4):
                    bu(i)
                for i in range(PAIRS):
                    for n in mixer_steps(l).get(i, []):
                        if n[0] == "if":
                            pe.wait_ge(s_wif, 32 * (l + 1))
                            open_bank(pe, n)
                            for k in range(KT):
                                ins = M(bank(n)[0:F_ROW + NH, 0:SEQ], w_if[:, k, :], hnT[:, k, :],
                                        start=(k == 0), stop=(k == KT - 1))
                            done(ins)
                        elif n[0] == "tr":
                            pe.wait_ge(gate_rows, l + 1)
                            open_bank(pe, n)
                            for m, src in enumerate((3, 0)):
                                for t in range(NT):
                                    a = (2 * m + t) * NH
                                    ins = nc.tensor.transpose(bank(n)[:, a:a + NH],
                                                              gates[:, src, t * P:(t + 1) * P], ident[0:NH, 0:NH])
                            done(ins)
                        elif n[0] == "qk":
                            c = ("q" if n[2] < 2 else "k", l)
                            chunk_wait(pe, c)
                            a = (n[2] % 2) * 2 * P
                            done(channels(n, v3(chunk(c), KT), (a, a + P)))
                        else:
                            chunk_wait(pe, (n[0], l))
                            open_bank(pe, n)
                            for k in range(KT):
                                ins = M(bank(n)[:, :], hnT[:, k, n[2] * P:(n[2] + 1) * P],
                                        v3(chunk((n[0], l)), KT)[:, k, :], start=(k == 0), stop=(k == KT - 1))
                            done(ins)
                    if i + 4 < PAIRS:
                        bu(i + 4)
                    n = l * PAIRS + i
                    c, j = divmod(i, PPC)
                    if j == 0:
                        open_bank(pe, ("y", l, c))
                    if i == 0:
                        wait_drained(pe, ("c_im", l))
                    pe.wait_ge(tile_done, n + 1)
                    r = slice(32 * j, 32 * j + 32)
                    for q, (m, a, b) in enumerate(((0, 0, 0), (1, 0, 1), (2, 1, 0), (2, 1, 1))):
                        ins = M(bank(("y", l, c))[r, 0:SEQ], cT[:, m, c, 32 * j:32 * j + 32], back[:, n % 2, a, b, :],
                                start=(q == 0), stop=(q == 3))
                    ins.then_inc(back_used, 1)
                for n in mixer_tail(l):
                    kind = n[0]
                    if kind == "mu":
                        open_bank(pe, n)
                        done(M(bank(n)[:, 0:SEQ], head_pick[:, n[2], :], gate_max[:, :], start=True, stop=True))
                    elif kind == "sc":
                        h = n[2]
                        if h == 0:
                            pe.wait_ge(qk_ready, 4 * (l + 1))
                        open_bank(pe, n)
                        M(bank(n)[:, 0:SEQ], qk[:, NH + h, 0:P], qk[:, h, :], start=True, stop=True)
                        done(M(bank(n)[:, SEQ:SEQ + P], qk[:, NH + h, P:SEQ], qk[:, h, P:SEQ], start=True, stop=True))
                    elif kind == "num":
                        h = n[2]
                        open_bank(pe, n)
                        wait_drained(pe, ("sc", l, h))
                        num = v3(bank(n)[:, :], 2)
                        s = scr[:, h % 2, :]
                        M(num[:, 0, 0:DH + 1], s[:, 0:P], v_aug[:, 0, h, :], start=True, stop=True)
                        M(num[:, 1, 0:DH + 1], s[:, P:SEQ], v_aug[:, 0, h, :], start=True, stop=False)
                        done(M(num[:, 1, 0:DH + 1], s[:, SEQ:], v_aug[:, 1, h, :], start=False, stop=True))
                    elif kind == "z":
                        if n[2] == 0:
                            chunk_wait(pe, ("glu", l))
                            pe.wait_ge(glu_ready, CT * (l + 1))
                        w = v3(chunk(("glu", l))[:, 0:DS5 * CT], CT)
                        open_bank(pe, n)
                        for m in range(2):
                            a = (2 * n[2] + m) * P
                            for k in range(CT):
                                ins = M(bank(n)[:, m * SEQ:(m + 1) * SEQ], w[:, k, a:a + P], gT[:, k, :],
                                        start=(k == 0), stop=(k == CT - 1))
                        done(ins)
                    elif kind == "ss":
                        pe.wait_ge(squares_s5, l + 1)
                        open_bank(pe, n)
                        for t in range(NT):
                            for c in range(CT):
                                ins = M(bank(n)[:, t:t + 1], gT[:, c, t * P:(t + 1) * P], ones[:, 0:1],
                                        start=(c == 0), stop=(c == CT - 1))
                        done(ins)
                    elif kind == "hmT":
                        if n[2] == 0:
                            pe.wait_ge(hm_ready, l + 1)
                        open_bank(pe, n)
                        for k in range(2):
                            for t in range(NT):
                                ins = nc.tensor.transpose(bank(n)[:, k * SEQ + t * P:k * SEQ + (t + 1) * P],
                                                          hm[:, t, 2 * n[2] + k, :], ident[:, :])
                        done(ins)
                    else:
                        k0 = CT if kind == "os" else 0
                        if n[0:1] + n[2:] == ("oh", 0, 0):
                            for i in range(2):
                                wait_drained(pe, ("hmT", l, i))
                        t, c = n[2:]
                        if kind == "os":
                            pe.wait_ge(mixed_s5, l + 1)
                        chunk_wait(pe, ("out", l, c))
                        open_bank(pe, n)
                        for k in range(4):
                            ins = M(bank(n)[:, :], mixT[:, k0 + k, t * P:(t + 1) * P],
                                    v3(chunk(("out", l, c)), KT)[:, k0 + k, :], start=(k == 0), stop=(k == 3))
                        done(ins)

            pe.wait_ge(consts, 1)
            pe.wait_ge(s_par, 16 * (2 * len(VEC_ROWS) + 5))
            done(nc.tensor.transpose(bank(("vec",))[:, 0:DEPTH * VEC_PER], vec_rows[0:DEPTH * VEC_PER, :],
                                     ident[0:DEPTH * VEC_PER, 0:DEPTH * VEC_PER]))
            pe.wait_ge(dt_wide, 1)
            done(nc.tensor.transpose(bank(("s5p",))[:, 0:96], s5_rows[0:96, :], ident[0:96, 0:96]))
            for l in range(DEPTH):
                norm(l, 0)
                mixer(l)
                if l == 0:
                    prep(1)
                norm(l, 1)
                if l == 1:
                    have_hnT(l, 1)
                if l == 0:
                    def down(f):
                        n = f_parts.index(("fd", f))
                        pe.wait_ge(ffn_hid, f + 1)
                        pe.wait_ge(ffn_lo, n + 1)
                        hi, lo = ffn_split(n, w_hi), ffn_split(n, w_lo)
                        for t in range(NT):
                            h_hi = f_hid_hi[:, f % 3, t * P:(t + 1) * P]
                            h_lo = f_hid_lo[:, f % 3, t * P:(t + 1) * P]
                            for c in range(2):
                                if f == 0:
                                    open_bank(pe, ("ffn", t, c))
                                y = bank(("ffn", t, c))[:, :]
                                cols = slice(512 * c, 512 * c + 512)
                                M(y, h_hi, hi[:, cols], start=(f == 0), stop=False)
                                M(y, h_lo, hi[:, cols], start=False, stop=False)
                                ins = M(y, h_hi, lo[:, cols], start=False, stop=(f == FT - 1))
                                if f == FT - 1:
                                    done(ins)
                        if f < FT - 1:
                            ins.then_inc(ffn_used, 1)

                    for f in range(FT):
                        open_bank(pe, ("gu", f))
                        for m, c in enumerate(("fg", "fu")):
                            n = f_parts.index((c, f))
                            pe.wait_ge(ffn_lo, n + 1)
                            hi, lo = ffn_split(n, w_hi), ffn_split(n, w_lo)
                            y = bank(("gu", f))[:, m * SEQ:(m + 1) * SEQ]
                            for k in range(KT):
                                if f == 0 and m == 0 and k % 2 == 0:
                                    pe.wait_ge(ffn_x_lo, k // 2 + 1)
                                M(y, hi[:, k, :], hnT_hi[:, k, :], start=(k == 0), stop=False)
                                M(y, hi[:, k, :], hnT_lo[:, k, :], start=False, stop=False)
                                ins = M(y, lo[:, k, :], hnT_hi[:, k, :], start=False, stop=(k == KT - 1))
                            if m == 0:
                                ins.then_inc(ffn_used, 1)
                        done(ins)
                        if f:
                            down(f - 1)
                    down(FT - 1)

            pe.wait_ge(s_rt_in, 32)
            open_bank(pe, ("logits",))
            for k in range(KT):
                ins = M(bank(("logits",))[0:NE, 0:SEQ], w_rt[:, k, :], hnT[:, k, :], start=(k == 0),
                        stop=(k == KT - 1))
            done(ins)
            open_bank(pe, ("router",))
            wait_drained(pe, ("logits",))
            for t in range(NT):
                ins = nc.tensor.transpose(bank(("router",))[:, t * NE:(t + 1) * NE],
                                          logitsT[0:NE, t * P:(t + 1) * P], ident[0:NE, 0:NE])
            done(ins)
            pe.wait_ge(route_mask, 1)
            open_bank(pe, ("pos",))
            b = bank(("pos",))
            M(b[:, 0:NE], lower[:, :], rt[:, 6, 0, :], start=True, stop=True)
            M(b[:, NE:2 * NE], ones[:, :], rt[:, 6, 0, :], start=True, stop=False)
            M(b[:, NE:2 * NE], lower[:, :], rt[:, 6, 1, :], start=False, stop=True)
            M(b[:, 2 * NE:3 * NE], ones[:, :], rt[:, 6, 0, :], start=True, stop=False)
            done(M(b[:, 2 * NE:3 * NE], ones[:, :], rt[:, 6, 1, :], start=False, stop=True))

            def gather(it):
                pe.wait_ge(v_pick, it + 1)
                for half, b in ((0, 5), (1, 2)):
                    for k in range(4):
                        a = (4 * half + k) * P
                        for t in range(NT):
                            ins = M(ps[b][:, k * P:(k + 1) * P], hn[:, t, a:a + P], pick[:, t, :],
                                    start=(t == 0), stop=(t == NT - 1))
                    ins.then_inc(e_gather, 1)

            def swiglu(it, kind, j, b):
                for z in range(4):
                    q = part_no(kind, j, z)
                    pe.wait_ge(lo_ready, it * SPLITS + (q + 1))
                    hi, lo = v3(w_hi[:, q % SPLIT, :], 2), v3(w_lo[:, q % SPLIT, :], 2)
                    if j == 0 and kind == "g" and z % 2 == 0:
                        pe.wait_ge(v_xe, it * 2 + (z // 2 + 1))
                    for i in range(2):
                        k = 2 * z + i
                        M(ps[b][:, :], xe_hi[:, k, :], hi[:, i, :], start=(k == 0), stop=False)
                        M(ps[b][:, :], xe_lo[:, k, :], hi[:, i, :], start=False, stop=False)
                        ins = M(ps[b][:, :], xe_hi[:, k, :], lo[:, i, :], start=False, stop=(k == KT - 1))
                    ins.then_inc(split_used, 1)

            def transpose_hidden(it, j):
                pe.wait_ge(v_hid, it * NJ + (j + 1))
                for i in range(GW // P):
                    ins = nc.tensor.transpose(ps[4][:, i * P:(i + 1) * P],
                                              e_hid[:, 2 if j == NJ - 1 else j % 2, i * P:(i + 1) * P], ident[:, :])
                ins.then_inc(e_tr, 1)

            def down(it, j):
                pe.wait_ge(v_hT, it * NJ + (j + 1))
                for z in range(4):
                    q = part_no("d", j, z)
                    pe.wait_ge(lo_ready, it * SPLITS + (q + 1))
                    for n in range(2):
                        y = ps[6 + n][:, :]
                        cols = slice(512 * n, 512 * n + 512)
                        M(y, hidT_hi[:, z, :], w_hi[:, q % SPLIT, cols], start=(j == 0 and z == 0), stop=False)
                        M(y, hidT_lo[:, z, :], w_hi[:, q % SPLIT, cols], start=False, stop=False)
                        ins = M(y, hidT_hi[:, z, :], w_lo[:, q % SPLIT, cols], start=False,
                                stop=(j == NJ - 1 and z == 3))
                    ins.then_inc(split_used, 1)

            def scatter(it):
                pe.wait_ge(a_ye, it)
                pe.wait_ge(a_pt, it)
                for t in range(NT):
                    for c in range(2):
                        M(ps[SCATTER[2 * t + c]][:, :], pickT[:, t, :], ye[:, 512 * c:512 * c + 512], start=True,
                          stop=True).then_inc(e_sc, 1)

            def item(it, first=False):
                for j in range(NJ):
                    b = 2 * (j % 2)
                    if j == 2 and not first:
                        pe.wait_ge(v_add, it * 4)
                    swiglu(it, "g", j, b)
                    if j:
                        transpose_hidden(it, j - 1)
                    if j == 1 and not first:
                        scatter(it)
                    swiglu(it, "u", j, b + 1)
                    if j == 1:
                        for t in range(NT):
                            ins = nc.tensor.transpose(ps[5][:, t * P:(t + 1) * P], pickg[:, t, :], ident[:, :])
                        ins.then_inc(e_pt, 1)
                    if j:
                        if j == 1 and not first:
                            pe.wait_ge(v_add, it * 4)
                        down(it, j - 1)
                transpose_hidden(it, NJ - 1)
                pe.wait_ge(a_pt, it + 1)
                gather(it + 1)
                down(it, NJ - 1)

            gather(0)
            item(0, first=True)
            with pe.Fori(1, NE) as e:
                item(e)
            pe.wait_ge(items_ready, 1)
            n_over = pe.value_load(n_list[0:1, 0:1], min_val=0, max_val=3)
            with pe.If(n_over > 0):
                with pe.Fori(0, n_over) as k:
                    item(k + NE)
            n = n_over + NE
            scatter(n)


_INS = ['x', 'norm_mix', 'w_in', 'conv_qk', 'b_igate', 'b_fgate', 'norm_mlstm', 's5_a_re', 's5_a_im', 's5_log_dt',
        's5_b_re', 's5_b_im', 's5_c_re', 's5_c_im', 's5_d', 'w_glu', 'norm_s5', 'w_out', 'norm_ffn', 'ffn_w_gate',
        'ffn_w_up', 'ffn_w_down', 'moe_w_router', 'moe_b_router', 'moe_w_gate', 'moe_w_up', 'moe_w_down',
        'norm_final']
_OUTS = [((1, SEQ, DM), 'float32')]


def kernel(**inputs):
    import numpy as _np
    import concourse.bacc as _bacc
    from concourse import mybir as _mybir
    from concourse.bass_utils import run_bass_kernel_spmd as _run

    nc = _bacc.Bacc("TRN2", target_bir_lowering=False, num_devices=1)
    arrays, args = {}, []
    for name in _INS:
        a = _np.ascontiguousarray(inputs[name])
        arrays[f"in_{name}_dram"] = a
        args.append(nc.dram_tensor(f"in_{name}_dram", a.shape, _mybir.dt.from_np(a.dtype), kind="ExternalInput").ap())
    for i, (shape, dtype) in enumerate(_OUTS):
        dt = _mybir.dt.from_np(_np.dtype(dtype))
        args.append(nc.dram_tensor(f"out_{i}_dram", shape, dt, kind="ExternalOutput").ap())
    trunk_kernel(nc, *args)
    r = _run(nc, [arrays], core_ids=[0])
    got = tuple(r.results[0][f"out_{i}_dram"] for i in range(len(_OUTS)))
    return got[0]
```
